# Optimizing a Trainium2 kernel written in Bass

```python
import math
import jax, jax.numpy as jnp
from jax import lax
import numpy as np

D_MODEL = 2048
BATCH = 1
SEQ = 512
DEPTH = 2

HEAD_DIM = 128
N_MIX_HEADS = 8
GDN_QK_HEADS = 4
MIX_WIDTH = N_MIX_HEADS * HEAD_DIM
GDN_QK_WIDTH = GDN_QK_HEADS * HEAD_DIM
N_MEM = 256
MEM_HEADS = 4
MEM_WIDTH = MEM_HEADS * HEAD_DIM
CONV_WIDTH = 4
GDN_CHUNK = 64
SB_BLOCK = 128
SB_SUB = 32
PEER_HEADS = 4
PEER_NKEYS = 128
PEER_EXPERTS = PEER_NKEYS * PEER_NKEYS
PEER_QDIM = 256
PEER_HALF = PEER_QDIM // 2
PEER_HALF_TOPK = 16
PEER_TOPK = 8
PEER_BLOCK = 128
N_MIXERS = 2
N_GDN_LAYERS = (DEPTH + 1) // 2
N_SB_LAYERS = DEPTH // 2
DN_ALPHA = (2.0 * DEPTH) ** 0.25
DN_BETA = (8.0 * DEPTH) ** -0.25
LN_EPS = 1e-5
RMS_EPS = 1e-6
GDN_CONV_CH = 2 * GDN_QK_WIDTH + MIX_WIDTH
GDN_IN = 2 * GDN_QK_WIDTH + 2 * MIX_WIDTH + 2 * N_MIX_HEADS + MEM_WIDTH
SB_IN = 3 * MIX_WIDTH + MEM_WIDTH

kernel_name = 'hybrid_gdn_stickbreak_peer_deepnorm'

def layer_norm(x, g, b):
    xf = x.astype(jnp.float32)
    mu = jnp.mean(xf, -1, keepdims=True)
    var = jnp.mean(jnp.square(xf - mu), -1, keepdims=True)
    y = (xf - mu) * lax.rsqrt(var + LN_EPS) * g.astype(jnp.float32) + b.astype(jnp.float32)
    return y.astype(x.dtype)

def rms_norm(x, g):
    xf = x.astype(jnp.float32)
    return xf * lax.rsqrt(jnp.mean(xf * xf, -1, keepdims=True) + RMS_EPS) * g.astype(jnp.float32)

def l2norm(x):
    xf = x.astype(jnp.float32)
    return xf * lax.rsqrt(jnp.sum(xf * xf, -1, keepdims=True) + RMS_EPS)

def causal_conv(x, w):
    return lax.conv_general_dilated(x, w[:, None, :], window_strides=(1,), padding=[(CONV_WIDTH - 1, 0)],
                                    dimension_numbers=('NWC', 'WIO', 'NWC'), feature_group_count=x.shape[-1])

def gated_deltanet(q, k, v, z, b, a, conv_w, a_log, dt_bias, onorm_g):
    B_, S_, _ = q.shape
    f32 = jnp.float32
    C = GDN_CHUNK
    qkv = jax.nn.silu(causal_conv(jnp.concatenate([q, k, v], -1), conv_w))
    q, k, v = jnp.split(qkv, [GDN_QK_WIDTH, 2 * GDN_QK_WIDTH], axis=-1)
    rep = N_MIX_HEADS // GDN_QK_HEADS
    q = jnp.repeat(l2norm(q.reshape(B_, S_, GDN_QK_HEADS, HEAD_DIM)), rep, axis=2) * (HEAD_DIM ** -0.5)
    k = jnp.repeat(l2norm(k.reshape(B_, S_, GDN_QK_HEADS, HEAD_DIM)), rep, axis=2)
    v = v.reshape(B_, S_, N_MIX_HEADS, HEAD_DIM).astype(f32)
    beta = jax.nn.sigmoid(b.astype(f32))
    g = -jnp.exp(a_log.astype(f32)) * jax.nn.softplus(a.astype(f32) + dt_bias.astype(f32))
    n = S_ // C

    def chunks(t):
        return jnp.moveaxis(t.reshape(B_, n, C, *t.shape[2:]), 3, 1)

    qc, kc, vc, bc, gc = chunks(q), chunks(k), chunks(v), chunks(beta), chunks(g)
    gcum = jnp.cumsum(gc, axis=-1)
    glast = gcum[..., -1]
    causal = jnp.tril(jnp.ones((C, C), bool))
    strict = jnp.tril(jnp.ones((C, C), bool), -1)
    decay = jnp.exp(jnp.where(causal, gcum[..., :, None] - gcum[..., None, :], -jnp.inf))
    kb = kc * bc[..., None]
    m_low = jnp.where(strict, jnp.einsum('bhncd,bhnsd->bhncs', kb, kc) * decay, 0.0)
    eye = jnp.eye(C, dtype=f32)
    rhs = jnp.concatenate([vc * bc[..., None], kb * jnp.exp(gcum)[..., None]], -1)
    sol = lax.linalg.triangular_solve(eye + m_low, rhs, left_side=True, lower=True, unit_diagonal=True)
    u, w = sol[..., :HEAD_DIM], sol[..., HEAD_DIM:]
    aqk = jnp.einsum('bhncd,bhnsd->bhncs', qc, kc) * decay
    qg = qc * jnp.exp(gcum)[..., None]
    kd = kc * jnp.exp(glast[..., None] - gcum)[..., None]

    def step(state, inp):
        qg_n, kd_n, u_n, w_n, aqk_n, gl_n = inp
        v_new = u_n - jnp.einsum('bhck,bhkv->bhcv', w_n, state)
        o = jnp.einsum('bhck,bhkv->bhcv', qg_n, state) + jnp.einsum('bhcs,bhsv->bhcv', aqk_n, v_new)
        state = state * jnp.exp(gl_n)[..., None, None] + jnp.einsum('bhck,bhcv->bhkv', kd_n, v_new)
        return state, o

    xs = tuple(jnp.moveaxis(t, 2, 0) for t in (qg, kd, u, w, aqk, glast))
    s0 = jnp.zeros((B_, N_MIX_HEADS, HEAD_DIM, HEAD_DIM), f32)
    _, o = lax.scan(step, s0, xs)
    o = jnp.moveaxis(o, 0, 2).transpose(0, 2, 3, 1, 4).reshape(B_, S_, N_MIX_HEADS, HEAD_DIM)
    o = rms_norm(o, onorm_g) * jax.nn.silu(z.reshape(B_, S_, N_MIX_HEADS, HEAD_DIM).astype(f32))
    return o.reshape(B_, S_, MIX_WIDTH).astype(z.dtype)

def stick_breaking(q, k, v):
    B_, S_, _ = q.shape
    f32 = jnp.float32
    hi = lax.Precision.HIGHEST
    q = q.reshape(B_, S_, N_MIX_HEADS, HEAD_DIM).astype(f32) * (HEAD_DIM ** -0.5)
    k = k.reshape(B_, S_, N_MIX_HEADS, HEAD_DIM).astype(f32)
    vf = v.reshape(B_, S_, N_MIX_HEADS, HEAD_DIM).astype(f32)
    nb = S_ // SB_BLOCK
    tri_sub = (jnp.arange(SB_SUB)[:, None] > jnp.arange(SB_SUB)[None, :]).astype(f32)
    outs = []
    for blk in range(nb):
        L = (blk + 1) * SB_BLOCK
        n_sub = L // SB_SUB
        q_blk = q[:, blk * SB_BLOCK:(blk + 1) * SB_BLOCK]
        zs = jnp.einsum('bqhd,bshd->bhqs', q_blk, k[:, :L])
        q_pos = blk * SB_BLOCK + jnp.arange(SB_BLOCK)
        mask = jnp.arange(L)[None, :] < q_pos[:, None]
        zs = jnp.where(mask, zs, -jnp.inf)
        log_not = jax.nn.log_sigmoid(-zs)
        ln_sub = log_not.reshape(B_, N_MIX_HEADS, SB_BLOCK, n_sub, SB_SUB)
        within = jnp.einsum('bhqnj,js->bhqns', ln_sub, tri_sub, precision=hi)
        tri_blk = (jnp.arange(n_sub)[:, None] > jnp.arange(n_sub)[None, :]).astype(f32)
        offs = jnp.einsum('bhqm,mn->bhqn', jnp.sum(ln_sub, -1), tri_blk, precision=hi)
        later = (within + offs[..., None]).reshape(B_, N_MIX_HEADS, SB_BLOCK, L)
        att = jnp.exp(log_not + zs + later)
        outs.append(jnp.einsum('bhqs,bshd->bqhd', att, vf[:, :L]))
    o = jnp.concatenate(outs, axis=1)
    return o.reshape(B_, S_, MIX_WIDTH).astype(v.dtype)

def memory_attention(qm, mem, w_kv):
    B_, S_, _ = qm.shape
    km, vm = jnp.split(mem @ w_kv, 2, axis=-1)
    q = qm.reshape(B_, S_, MEM_HEADS, HEAD_DIM)
    km = km.reshape(B_, N_MEM, MEM_HEADS, HEAD_DIM)
    vm = vm.reshape(B_, N_MEM, MEM_HEADS, HEAD_DIM)
    s = jnp.einsum('bqhd,bmhd->bhqm', q, km).astype(jnp.float32) * (HEAD_DIM ** -0.5)
    p = jax.nn.softmax(s, axis=-1)
    o = jnp.einsum('bhqm,bmhd->bqhd', p.astype(vm.dtype), vm)
    return o.reshape(B_, S_, MEM_WIDTH)

def peer(x, w_q, sub_keys, u_tab, v_tab):
    B_, S_, D = x.shape
    f32 = jnp.float32
    T = B_ * S_
    xt = x.reshape(T, D)
    qry = (xt @ w_q).reshape(T, PEER_HEADS, 2, PEER_HALF).astype(f32)
    s = jnp.einsum('thpc,pnc->thpn', qry, sub_keys.astype(f32))
    sv, si = lax.top_k(s, PEER_HALF_TOPK)
    cand = (sv[:, :, 0, :, None] + sv[:, :, 1, None, :]).reshape(T, PEER_HEADS, PEER_HALF_TOPK * PEER_HALF_TOPK)
    cv, ci = lax.top_k(cand, PEER_TOPK)
    i1 = jnp.take_along_axis(si[:, :, 0], ci // PEER_HALF_TOPK, axis=-1)
    i2 = jnp.take_along_axis(si[:, :, 1], ci % PEER_HALF_TOPK, axis=-1)
    expert = (i1 * PEER_NKEYS + i2).reshape(T, PEER_HEADS * PEER_TOPK)
    gate = jax.nn.softmax(cv, axis=-1).reshape(T, PEER_HEADS * PEER_TOPK)
    nb = T // PEER_BLOCK

    def block(args):
        xb, eb, gb = args
        h = jnp.einsum('td,ted->te', xb, u_tab[eb])
        act = (jax.nn.gelu(h.astype(f32), approximate=False) * gb).astype(x.dtype)
        return jnp.einsum('te,ted->td', act, v_tab[eb])

    out = lax.map(block, (xt.reshape(nb, PEER_BLOCK, D), expert.reshape(nb, PEER_BLOCK, -1),
                          gate.reshape(nb, PEER_BLOCK, -1)))
    return out.reshape(B_, S_, D)

def setup_inputs(seed: int = 0) -> dict:
    key = jax.random.key(seed)
    ks = jax.random.split(key, 20)
    f32 = jnp.float32
    D = D_MODEL

    def nrm(k, shape, scale):
        return jax.random.normal(k, shape, f32) * scale

    x = nrm(ks[0], (BATCH, SEQ, D), 1.0)
    mem = nrm(ks[1], (BATCH, N_MEM, D), 1.0)
    v0 = 2 * GDN_QK_WIDTH
    gdn_scale = jnp.ones((GDN_IN,), f32).at[v0:v0 + MIX_WIDTH].set(DN_BETA)
    gdn_w_in = nrm(ks[2], (N_GDN_LAYERS, D, GDN_IN), D ** -0.5) * gdn_scale
    gdn_conv = nrm(ks[3], (N_GDN_LAYERS, CONV_WIDTH, GDN_CONV_CH), CONV_WIDTH ** -0.5)
    gdn_a_log = jnp.log(jax.random.uniform(ks[4], (N_GDN_LAYERS, N_MIX_HEADS), f32, 1.0, 16.0))
    dt = jnp.exp(jax.random.uniform(ks[5], (N_GDN_LAYERS, N_MIX_HEADS), f32, math.log(1e-3), math.log(1e-1)))
    gdn_dt_bias = dt + jnp.log(-jnp.expm1(-dt))
    gdn_onorm = 1.0 + nrm(ks[6], (N_GDN_LAYERS, HEAD_DIM), 0.02)
    sb_scale = jnp.ones((SB_IN,), f32).at[2 * MIX_WIDTH:3 * MIX_WIDTH].set(DN_BETA)
    sb_w_in = nrm(ks[7], (N_SB_LAYERS, D, SB_IN), D ** -0.5) * sb_scale
    mem_scale = jnp.ones((2 * MEM_WIDTH,), f32).at[MEM_WIDTH:].set(DN_BETA)
    mem_w_kv = nrm(ks[8], (DEPTH, D, 2 * MEM_WIDTH), D ** -0.5) * mem_scale
    w_out = nrm(ks[9], (DEPTH, MIX_WIDTH + MEM_WIDTH, D), (MIX_WIDTH + MEM_WIDTH) ** -0.5 * DN_BETA)
    ln_mix_g = 1.0 + nrm(ks[10], (DEPTH, D), 0.02)
    ln_mix_b = nrm(ks[11], (DEPTH, D), 0.02)
    peer_w_q = nrm(ks[12], (DEPTH, D, PEER_HEADS * PEER_QDIM), D ** -0.5)
    peer_keys = nrm(ks[13], (DEPTH, 2, PEER_NKEYS, PEER_HALF), PEER_HALF ** -0.5)
    peer_u = nrm(ks[14], (DEPTH, PEER_EXPERTS, D), D ** -0.5)
    peer_v = nrm(ks[15], (DEPTH, PEER_EXPERTS, D), DN_BETA * PEER_HEADS ** -0.5)
    ln_ffn_g = 1.0 + nrm(ks[16], (DEPTH, D), 0.02)
    ln_ffn_b = nrm(ks[17], (DEPTH, D), 0.02)
    return {'x': x, 'mem': mem, 'gdn_w_in': gdn_w_in, 'gdn_conv': gdn_conv, 'gdn_a_log': gdn_a_log,
            'gdn_dt_bias': gdn_dt_bias, 'gdn_onorm': gdn_onorm, 'sb_w_in': sb_w_in, 'mem_w_kv': mem_w_kv,
            'w_out': w_out, 'ln_mix_g': ln_mix_g, 'ln_mix_b': ln_mix_b, 'peer_w_q': peer_w_q,
            'peer_keys': peer_keys, 'peer_u': peer_u, 'peer_v': peer_v, 'ln_ffn_g': ln_ffn_g, 'ln_ffn_b': ln_ffn_b}

def reference(x, mem, gdn_w_in, gdn_conv, gdn_a_log, gdn_dt_bias, gdn_onorm, sb_w_in, mem_w_kv, w_out,
              ln_mix_g, ln_mix_b, peer_w_q, peer_keys, peer_u, peer_v, ln_ffn_g, ln_ffn_b):
    q_w, v_w = GDN_QK_WIDTH, MIX_WIDTH
    gdn_splits = [q_w, 2 * q_w, 2 * q_w + v_w, 2 * q_w + 2 * v_w, 2 * q_w + 2 * v_w + N_MIX_HEADS,
                  2 * q_w + 2 * v_w + 2 * N_MIX_HEADS]
    sb_splits = [MIX_WIDTH, 2 * MIX_WIDTH, 3 * MIX_WIDTH]
    for i in range(DEPTH):
        li = i // N_MIXERS
        if i % N_MIXERS == 0:
            p = x @ gdn_w_in[li]
            q, k, v, z, b, a, qm = jnp.split(p, gdn_splits, axis=-1)
            mix = gated_deltanet(q, k, v, z, b, a, gdn_conv[li], gdn_a_log[li], gdn_dt_bias[li], gdn_onorm[li])
        else:
            p = x @ sb_w_in[li]
            q, k, v, qm = jnp.split(p, sb_splits, axis=-1)
            mix = stick_breaking(q, k, v)
        mem_o = memory_attention(qm, mem, mem_w_kv[i])
        y = jnp.concatenate([mix, mem_o], axis=-1) @ w_out[i]
        x = layer_norm(DN_ALPHA * x + y, ln_mix_g[i], ln_mix_b[i])
        f = peer(x, peer_w_q[i], peer_keys[i], peer_u[i], peer_v[i])
        x = layer_norm(DN_ALPHA * x + f, ln_ffn_g[i], ln_ffn_b[i])
    return x


_drawn_inputs = setup_inputs


def setup_inputs(seed=0):
    import zlib

    import numpy as np

    out = dict(_drawn_inputs(seed))
    spreads = {}
    factors = {'gdn_onorm': 5.268, 'mem': 2.746}
    for name, (base, spread) in spreads.items():
        noise = np.random.default_rng([zlib.crc32(name.encode()), seed]).standard_normal(out[name].shape)
        drawn = base * np.exp(spread * noise) if base else spread * noise
        out[name] = __import__('jax').numpy.asarray(drawn.astype(out[name].dtype))
    for name, factor in factors.items():
        out[name] = (out[name] * factor).astype(out[name].dtype)
    return out
```

```python
from contextlib import ExitStack

import concourse.bass as bass
from concourse import mybir

F32 = mybir.dt.float32
U32 = mybir.dt.uint32
ALU = mybir.AluOpType
ACT = mybir.ActivationFunctionType
AX_X = mybir.AxisListType.X

P = 128
CHUNK = 64
SUB = 4
WCOLS = 256
RING = 3
DIAGS = 3
GROUP = 8
HALF_TOPK = 16
TOPK = 8
LN_EPS = 1e-5
RMS_EPS = 1e-6
BANKS = 4
LEVELS = (2, 4, 8, 16, 32)


def build(nc, x, mem, gdn_w_in, gdn_conv, gdn_a_log, gdn_dt_bias, gdn_onorm, sb_w_in, mem_w_kv, w_out,
          ln_mix_g, ln_mix_b, peer_w_q, peer_keys, peer_u, peer_v, ln_ffn_g, ln_ffn_b, out):
    _, S, D = x.shape
    DEPTH = w_out.shape[0]
    NMEM = mem.shape[1]
    KT = D // P
    NT = S // P
    TU = 2
    T = TU * P
    HALVES = NT // TU
    H = gdn_a_log.shape[1]
    HQ = H // 2
    MH = mem_w_kv.shape[2] // (2 * P)
    PH = peer_w_q.shape[2] // (2 * P)
    NK = peer_keys.shape[2]
    NE = peer_u.shape[1]
    SLOTS = PH * TOPK
    KO = w_out.shape[1] // P
    ALPHA = (2.0 * DEPTH) ** 0.25
    SCALE = float(P) ** -0.5
    assert (S, D, DEPTH, NMEM, T, H, MH, PH, NK) == (512, 2048, 2, 256, 256, 8, 4, 4, 128)
    UNITS = [(l, f) for l in range(DEPTH) for f in range(HALVES)]
    NPROJ = 14
    NOUT = D // WCOLS
    NQRY = 2 * PH * P // WCOLS
    NKV = 2 * MH * P // WCOLS
    QM0 = 2 * HQ * P + 2 * H * P + 2 * H

    PLAN, LOADS, USER = {}, {}, {}

    def plan(*name):
        PLAN[name] = len(PLAN)

    def load(*name, user=None):
        LOADS[name] = len(LOADS)
        USER[LOADS[name]] = user or name

    def plan_norm(kind, u):
        for c in range(4):
            plan("norm_g", kind, u, c)
            plan("norm_b", kind, u, c)

    plan("keys", 0)
    for u, (l, f) in enumerate(UNITS):
        if u >= HALVES:
            plan_norm(1, u - HALVES)
        if f == 0:
            load("mem", l, user=("memT", l, 7))
            for j in range(8):
                plan("memT", l, j)
            for w in range(NKV):
                load("kv", l, w)
                plan("kv", l, w)
        for j in range(8):
            plan("xT", u, 0, j)
        for w in range(NPROJ):
            load("proj", u, w)
            plan("proj", u, w)
        if l % 2 == 0:
            for s in ("ba", "gcum", "rows"):
                plan(s, u)
            for i in range(4):
                plan("l2", u, i)
            for j in range(HQ):
                for s in ("ktok", "vtok", "bcb", "bcg", "seg", "kq", "kk", "T0"):
                    plan(s, u, j)
                for i in range(len(LEVELS)):
                    plan("P", u, j, i)
                    plan("TP", u, j, i)
                    plan("PU", u, j, i)
                plan("u", u, j)
                plan("w", u, j)
                plan("o", u, j)
                plan("oss", u, j)
        else:
            for h in range(H):
                for b in range(f + 1):
                    plan("z", u, h, b)
                for b in range(f + 1):
                    plan("later", u, h, b)
                plan("sbo", u, h)
        for m in range(MH):
            plan("ms", u, m)
            plan("mpT", u, m)
            plan("mo", u, m)
        for w in range(NOUT):
            load("out", u, w)
            plan("out", u, w)
        plan_norm(0, u)
        for j in range(8):
            plan("xT", u, 1, j)
        for w in range(NQRY):
            load("qry", u, w)
            plan("qry", u, w)
        for t in range(TU):
            plan("score", u, t, 0)
            plan("score", u, t, 1)
    for u in (len(UNITS) - HALVES, len(UNITS) - 1):
        plan_norm(1, u)

    def full(eng, *name):
        eng.wait_ge(group_done, PLAN[name] + 1)

    def was_read(eng, *name):
        n = PLAN[name]
        eng.wait_ge(bank_read[n % BANKS], n // BANKS + 1)

    with ExitStack() as ctx:
        def sb(name, shape, dt=F32):
            return ctx.enter_context(nc.sbuf_tensor(name, shape, dt))

        def sem(name):
            return ctx.enter_context(nc.semaphore(name))

        acc = ctx.enter_context(nc.psum_tensor("acc", [P, 4, 512], F32))
        banks = ctx.enter_context(nc.psum_tensor("banks", [P, BANKS, 512], F32))

        X = sb("X", [P, NT, D])
        XT = sb("XT", [P, KT * T])
        W = sb("W", [P, 2, KT * WCOLS])
        UR = sb("UR", [P, RING, D])
        VR = sb("VR", [P, RING, D])
        NV = sb("NV", [64, 256])
        MIX = sb("MIX", [P, KO * T])
        KM = sb("KM", [P, MH, NMEM])
        VM = sb("VM", [P, NMEM // P, MH * P])
        R = sb("R", [P, 11264])
        xT = XT[:, :].rearrange("p (k t) -> p k t", k=KT)
        mixT = MIX[:, :].rearrange("p (k t) -> p k t", k=KO)
        qryT = MIX[:, 0:2 * PH * T].rearrange("p (k t) -> p k t", k=2 * PH)
        qT = R[:, 0:2048].rearrange("p (h t) -> p h t", t=T)
        qmT = R[:, 2048:3072].rearrange("p (h t) -> p h t", t=T)
        vT = R[:, 3072:5120].rearrange("p (h t) -> p h t", t=T)
        zT = R[:, 5120:7168].rearrange("p (h t) -> p h t", t=T)
        convin = R[:, 7168:7168 + 1040].rearrange("p (r b t) -> p r b t", r=2, b=2)
        convout = R[:, 8208:8208 + 1024].rearrange("p (r b t) -> p r b t", r=2, b=2)
        sbkT = R[:, 3072:7168].rearrange("p (h t) -> p h t", t=S)
        sbv = R[:, 7168:11264].rearrange("p (t f) -> p t f", t=NT)

        def half_bank(region, i):
            return region[:, 512 * i:512 * i + 512]

        work = [half_bank(XT, i) for i in range(8)] + [half_bank(R[:, 7168:11264], i) for i in range(6)]
        (seg_g, decay, kbT, qgT, Kp, Kd, Vp, MT, U, Tm, Pm, Lm, aqkT, spare) = work
        u_sb, wT, o_sb = decay, kbT, Vp
        vnew = seg_g[:, 0:2 * P].rearrange("p (h v) -> p h v", h=2)
        bgT = spare[0:16, 0:T]
        state = R[:, 10240:11264].rearrange("p (h v) -> p h v", h=H)
        sq = [Lm, Pm]
        rs = [MT, aqkT]
        hist = sb("hist", [P, 16, 3])
        convw = sb("convw", [P, 16, 4])
        wba = sb("wba", [P, KT, 16])
        onorm = sb("onorm", [P, 1])
        dtb = sb("dtb", [P, H])
        nexp = sb("nexp", [P, H])
        gx = sb("gx", [P, TU, 16])
        ge = sb("ge", [P, TU, 16])
        ga = sb("ga", [P, TU, H])
        gl = sb("gl", [P, TU, H])
        g = sb("g", [P, TU, H])
        eg = sb("eg", [P, TU, 32])
        bg = sb("bg", [P, TU, 16])
        bexpg = sb("bexpg", [P, TU, H])
        ident = sb("ident", [P, P])
        ones = sb("ones", [P, P])
        tri_le = sb("tri_le", [P, P])
        tri_gt = sb("tri_gt", [P, P])
        full_ge = sb("full_ge", [P, P])
        lvl = sb("lvl", [P, 6, P])
        sbmask = lvl[:, 0:4, :].rearrange("p a c -> p (a c)").rearrange("p (b t) -> p b t", b=2)
        iota16 = sb("iota16", [P, 16])
        eps = sb("eps", [P, 2])
        stats = sb("stats", [P, TU, 4, 6])
        mv = sb("mv", [P, TU, 2])
        rstd = sb("rstd", [P, TU, 2])
        keysT = sb("keysT", [P, 2 * DEPTH, NK])
        nmax = sb("nmax", [P, 2, TU])
        msum = sb("msum", [P, 2, TU])
        sb_z = XT[:, 0:1024].rearrange("p (s t) -> p s t", t=T)
        sb_e = XT[:, 1024:2048].rearrange("p (s t) -> p s t", t=T)
        sb_sp = XT[:, 2048:3072].rearrange("p (s t) -> p s t", t=T)
        sb_att = XT[:, 3072:4096].rearrange("p (s t) -> p s t", t=T)
        mem_p = XT[:, 0:512].rearrange("p (t m) -> p t m", t=TU)
        mem_pT = XT[:, 512:1024].rearrange("p (m t) -> p m t", m=2)
        s_sb = R[:, 0:1024].rearrange("p (g n) -> p g n", g=8)
        s_wk = R[:, 1024:2048].rearrange("p (g n) -> p g n", g=8)
        cand = XT[:, 0:1024].rearrange("p (h i j) -> p h i j", h=PH, i=16)
        hot = [XT[:, 1024 + 512 * i:1536 + 512 * i].rearrange("p (h k i) -> p h k i", h=PH, k=TOPK) for i in range(2)]
        tv = XT[:, 2048:2176].rearrange("p (g k) -> p g k", g=2 * PH)
        ti = XT[:, 2176:2304].bitcast(U32).rearrange("p (g k) -> p g k", g=2 * PH)
        tif = XT[:, 2304:2432].rearrange("p (g k) -> p g k", g=2 * PH)
        cv = XT[:, 2432:2464].rearrange("p (h k) -> p h k", h=PH)
        ci = XT[:, 2464:2496].bitcast(U32).rearrange("p (h k) -> p h k", h=PH)
        cp = XT[:, 2496:2560].bitcast(U32).rearrange("p (s k) -> p s k", s=2)
        cpf = XT[:, 2560:2624].rearrange("p (s k) -> p s k", s=2)
        i12 = XT[:, 2624:2688].rearrange("p (s k) -> p s k", s=2)
        cd = XT[:, 2688:2720].rearrange("p (h k) -> p h k", h=PH)
        csum = XT[:, 2720:2728].rearrange("p (s h) -> p s h", s=2)
        gate = sb("gate", [P, 2, TU, SLOTS])
        idx = sb("idx", [P, 2, TU, SLOTS], U32)
        hdot = sb("hdot", [P, 2, GROUP])
        gel = sb("gel", [P, 2, GROUP])
        coef = sb("coef", [P, 2, GROUP])
        diag = sb("diag", [P, DIAGS, P])

        group_done = sem("group_done")
        bank_read = [sem(f"bank_read{b}") for b in range(BANKS)]
        w_landed = [sem(f"w_landed{b}") for b in range(2)]
        x_landed = sem("x_landed")
        small_landed = sem("small_landed")
        consts_made = sem("consts_made")
        pool_step = sem("pool_step")
        sbmask_made = sem("sbmask_made")
        dve_step = sem("dve_step")
        act_step = sem("act_step")
        conv_made = sem("conv_made")
        qkv_made = sem("qkv_made")
        gate_in = sem("gate_in")
        gate_exp = sem("gate_exp")
        g_made = sem("g_made")
        rows_made = sem("rows_made")
        squared = sem("squared")
        inverse_norm = sem("inverse_norm")
        qk_normed = sem("qk_normed")
        seg_made = sem("seg_made")
        kv_scaled = sem("kv_scaled")
        level_made = sem("level_made")
        inverse_made = sem("inverse_made")
        aqk_made = sem("aqk_made")
        state_made = sem("state_made")
        ws_done = sem("ws_done")
        ds_done = sem("ds_done")
        vnew_made = sem("vnew_made")
        o_gated = sem("o_gated")
        softplus_in = sem("softplus_in")
        softplus_ln = sem("softplus_ln")
        softplus_made = sem("softplus_made")
        att_exp = sem("att_exp")
        att_made = sem("att_made")
        mmax_made = sem("mmax_made")
        mexp_made = sem("mexp_made")
        mprob_made = sem("mprob_made")
        stats_made = sem("stats_made")
        rstd_made = sem("rstd_made")
        x_normed = sem("x_normed")
        cdiff_made = sem("cdiff_made")
        cexp_made = sem("cexp_made")
        routed = sem("routed")
        u_landed = [sem(f"u_landed{r}") for r in range(RING)]
        v_landed = [sem(f"v_landed{r}") for r in range(RING)]
        dot_made = sem("dot_made")
        gelu_made = sem("gelu_made")
        coef_made = sem("coef_made")
        diag_made = sem("diag_made")
        v_used = sem("v_used")
        acc_read = sem("acc_read")
        stored = sem("stored")

        xr = x.rearrange("a (t p) d -> p (a t) d", p=P)
        outr = out.rearrange("a (t p) d -> p (a t) d", p=P)
        u_rows = peer_u.rearrange("l e d -> (l e) d")
        v_rows = peer_v.rearrange("l e d -> (l e) d")

        def norm_index(kind, u):
            if kind == 0:
                return u if u < HALVES else 2 * u - HALVES + 1
            return 2 * u + HALVES if u < HALVES else 2 * HALVES * (DEPTH - 1) + u

        def bank(*name):
            return banks[:, PLAN[name] % BANKS, :]

        def sub(ap, n=SUB):
            return ap.rearrange("p (s c) -> p s c", s=n)

        block = ctx.enter_context(nc.Block())

        @block.sync
        def _(sp):
            with nc.allow_non_contiguous_dma(reason="small parameters, once"):
                for i, v in enumerate((ln_mix_g, ln_mix_b, ln_ffn_g, ln_ffn_b)):
                    sp.dma_start(NV[16 * i:16 * i + 16, :], v.rearrange("l (a c) -> (l a) c", c=256)).then_inc(small_landed, 16)
                sp.dma_start(UR[:, 0, 0:2 * DEPTH * P].rearrange("p (a c) -> p a c", c=P),
                             peer_keys.rearrange("l h n c -> n (l h) c")).then_inc(small_landed, 16)
                for i in range(4):
                    sp.dma_start(convw[:, :, i], gdn_conv[0, i, :].rearrange("(b p) -> p b", p=P)).then_inc(small_landed, 16)
                sp.dma_start(wba[:, :, :], gdn_w_in[0, :, QM0 - 16:QM0].rearrange("(k p) c -> p k c", p=P)).then_inc(small_landed, 16)
                sp.dma_start(onorm[:, :], gdn_onorm.rearrange("a p -> p a")).then_inc(small_landed, 16)
                sp.dma_start(dtb[:, :], gdn_dt_bias.to_broadcast([P, H])).then_inc(small_landed, 16)
                sp.dma_start(nexp[:, :], gdn_a_log.to_broadcast([P, H])).then_inc(small_landed, 16)

            def weights(*name):
                m = LOADS[name]
                if m >= 2:
                    full(sp, *USER[m - 2])
                dst = W[:, m % 2, :]
                what, a = name[0], name[1]
                if what == "mem":
                    src = mem.rearrange("a (t p) d -> p (a t) d", p=P)
                    dst = dst.rearrange("p (t d) -> p t d", t=NMEM // P)
                else:
                    if what == "kv":
                        src = mem_w_kv[a, :, WCOLS * name[2]:WCOLS * (name[2] + 1)]
                    elif what == "proj":
                        c = WCOLS * name[2]
                        if UNITS[a][0] == 0:
                            c += 16 if name[2] >= 12 else 0
                            src = gdn_w_in[0, :, c:c + WCOLS]
                        else:
                            src = sb_w_in[0, :, c:c + WCOLS]
                    elif what == "out":
                        src = w_out[UNITS[a][0], :, WCOLS * name[2]:WCOLS * (name[2] + 1)]
                        dst = W[:, m % 2, 0:KO * WCOLS]
                    else:
                        src = peer_w_q[UNITS[a][0], :, WCOLS * name[2]:WCOLS * (name[2] + 1)]
                    src = src.rearrange("(k p) c -> p k c", p=P)
                    dst = dst.rearrange("p (k c) -> p k c", c=WCOLS)
                sp.dma_start(dst, src).then_inc(w_landed[m % 2], 16)

            first = True
            for name in LOADS:
                weights(*name)
                if first:
                    sp.dma_start(X[:, :, :], xr).then_inc(x_landed, 16)
                    first = False
            for i, u in enumerate((len(UNITS) - 2, len(UNITS) - 1)):
                sp.wait_ge(x_normed, norm_index(1, u) + 1)
                sp.dma_start(outr[:, TU * i:TU * i + TU, :], X[:, TU * i:TU * i + TU, :]).then_inc(stored, 16)
            sp.wait_ge(stored, 32)

        @block.gpsimd
        def _(pool):
            steps = [0]

            def link(ins):
                steps[0] += 1
                ins.then_inc(pool_step, 1)
                pool.wait_ge(pool_step, steps[0])

            for m in (ident, tri_le, tri_gt, full_ge, lvl):
                value = 0.0 if m is lvl or m is ident else 1.0
                link(pool.memset(m[:], value))
            link(pool.memset(ones[:, :], 1.0))
            link(pool.memset(eps[:, 0:1], LN_EPS))
            link(pool.memset(eps[:, 1:2], RMS_EPS))

            def keep(ap, pattern, base, mult, op=ALU.is_ge, fill=0.0):
                link(pool.affine_select(out=ap, in_=ap, compare_op=op, fill=fill, base=base, pattern=pattern,
                                        channel_multiplier=mult))

            keep(ident[:, :], [[-1, P]], 0, 1, ALU.not_equal, 1.0)
            keep(tri_le[:, :], [[1, P]], 0, -1)
            keep(tri_le[:, CHUNK:P], [[0, CHUNK]], -CHUNK, 1)
            keep(tri_gt[:, :], [[-1, P]], 0, 1, ALU.is_gt)
            keep(tri_gt[:, 0:CHUNK], [[0, CHUNK]], CHUNK - 1, -1)
            keep(full_ge[:, :], [[-1, P]], 0, 1)
            for i, w in enumerate((1,) + LEVELS):
                v = lvl[:, i, :].rearrange("p (b h w) -> p b h w", h=2, w=w)[:, :, 1, :]
                link(pool.memset(v, 1.0))
                keep(v, [[-2 * w, P // (2 * w)], [0, w]], 0, 1)
                keep(v, [[2 * w, P // (2 * w)], [0, w]], w - 1, -1)
            link(pool.iota(iota16[:, :], [[1, 16]], base=0, channel_multiplier=0, allow_small_or_imprecise_dtypes=True))
            pool.memset(state[:, :, :], 0.0).then_inc(consts_made, 1)

            def gather(ring, rows, landed, used, u, k):
                n = u * TU * SLOTS + k
                if n >= RING:
                    pool.wait_ge(used, n - RING + 1)
                t, s = k // SLOTS, k % SLOTS
                pool.indirect_dma_start(ring[:, n % RING, :], None, rows,
                                        bass.IndirectOffsetOnAxis(idx[:, u % 2, t, s:s + 1], 0)
                                        ).then_inc(landed[n % RING], 16)

            for u in range(len(UNITS)):
                for kk in range(TU * SLOTS // GROUP + 1):
                    for i in range(GROUP):
                        k = kk * GROUP + i
                        if k < TU * SLOTS:
                            if k % SLOTS == 0:
                                pool.wait_ge(routed, TU * u + k // SLOTS + 1)
                                if k == 0 and u == HALVES - 1:
                                    link(pool.memset(sbmask[:, :, :], 1.0))
                                    pool.affine_select(out=sbmask[:, :, :], in_=sbmask[:, :, :], compare_op=ALU.is_gt, fill=0.0,
                                                       base=0, pattern=[[-P, 2], [1, T]], channel_multiplier=-1
                                                       ).then_inc(sbmask_made, 1)
                            if u == 0 and k == 0:
                                was_read(pool, "keys", 0)
                            gather(UR, u_rows, u_landed, dot_made, u, k)
                        if kk >= 1:
                            gather(VR, v_rows, v_landed, v_used, u, k - GROUP)

        @block.tensor
        def _(pe):
            order = [0]

            def group(*name):
                n = PLAN[name]
                assert n == order[0], (name, n, order[0])
                order[0] += 1
                if n >= BANKS:
                    pe.wait_ge(bank_read[n % BANKS], n // BANKS)
                return banks[:, n % BANKS, :]

            def done(ins):
                ins.then_inc(group_done, 1)

            def weights(*name):
                m = LOADS[name]
                pe.wait_ge(w_landed[m % 2], 16 * (m // 2 + 1))
                return W[:, m % 2, :].rearrange("p (k c) -> p k c", c=WCOLS)

            def by_feature(ps, w, src, kt):
                for b in range(2):
                    for k in range(kt):
                        last = pe.matmul(sub(ps, 2)[:, b, :], w[:, k, b * P:b * P + P], src[:, k, :],
                                         start=(k == 0), stop=(k == kt - 1))
                done(last)

            def by_token(ps, w, src, kt):
                for t in range(TU):
                    for k in range(kt):
                        last = pe.matmul(sub(ps, 2)[:, t, :], src[:, k, t * P:t * P + P], w[:, k, :],
                                         start=(k == 0), stop=(k == kt - 1))
                done(last)

            def norm(kind, u):
                l = UNITS[u][0]
                for c in range(4):
                    for v, name in enumerate(("norm_g", "norm_b")):
                        ps = group(name, kind, u, c)
                        for i in range(2):
                            r = 8 * (4 * kind + 2 * v + l) + 2 * c + i
                            last = pe.matmul(ps[:, 256 * i:256 * i + 256], ident[0:64, r:r + 1].to_broadcast([64, P]),
                                             NV[:, :], start=True, stop=True)
                        done(last)

            def x_transposes(u, which):
                if which == 1:
                    pe.wait_ge(x_normed, norm_index(0, u) + 1)
                elif u >= HALVES:
                    pe.wait_ge(x_normed, norm_index(1, u - HALVES) + 1)
                else:
                    pe.wait_ge(x_landed, 16)
                for j in range(8):
                    ps = sub(group("xT", u, which, j))
                    for i in range(SUB):
                        last = pe.transpose(ps[:, i, :], X[:, TU * UNITS[u][1] + j // 4, ((j % 4) * SUB + i) * P:((j % 4) * SUB + i + 1) * P],
                                            ident[:, :])
                    done(last)
                was_read(pe, "xT", u, which, 5)
                was_read(pe, "xT", u, which, 4)
                was_read(pe, "xT", u, which, 7)
                was_read(pe, "xT", u, which, 6)

            def project(u):
                l = UNITS[u][0]
                for w in range(NPROJ):
                    ps = group("proj", u, w)
                    tokens = l % 2 == 1 and 8 <= w < 12
                    (by_token if tokens else by_feature)(ps, weights("proj", u, w), xT, KT)

            def memory_kv(l):
                m = LOADS[("mem", l)]
                pe.wait_ge(w_landed[m % 2], 16 * (m // 2 + 1))
                rows = W[:, m % 2, :].rearrange("p (t d) -> p t d", t=2)
                for j in range(8):
                    ps = sub(group("memT", l, j))
                    for i in range(SUB):
                        last = pe.transpose(ps[:, i, :], rows[:, j // 4, ((j % 4) * SUB + i) * P:((j % 4) * SUB + i + 1) * P],
                                            ident[:, :])
                    done(last)
                for j in range(4, 8):
                    was_read(pe, "memT", l, j)
                for w in range(NKV):
                    ps = group("kv", l, w)
                    (by_feature if w < NKV // 2 else by_token)(ps, weights("kv", l, w), xT, KT)

            def deltanet(u):
                f = UNITS[u][1]
                ps = group("ba", u)
                for t in range(TU):
                    for k in range(KT):
                        last = pe.matmul(ps[:, 16 * t:16 * t + 16], xT[:, k, t * P:t * P + P], wba[:, k, :],
                                         start=(k == 0), stop=(k == KT - 1))
                done(last)
                pe.wait_ge(g_made, u + 1)
                ps = group("gcum", u)
                for t in range(TU):
                    chunks = [tri_le[:, c:c + 1].to_broadcast([P, P]) for c in (CHUNK - 1, P - 1)]
                    for i, a in enumerate([tri_le[:, :], tri_gt[:, :]] + chunks):
                        last = pe.matmul(ps[:, 32 * t + 8 * i:32 * t + 8 * i + 8], a, g[:, t, :], start=True, stop=True)
                done(last)
                pe.wait_ge(rows_made, u + 1)
                ps = group("rows", u)
                for t in range(TU):
                    last = pe.transpose(ps[0:16, t * P:t * P + P], bg[:, t, :], ident[:, :])
                done(last)
                for i in range(4):
                    pe.wait_ge(squared, 4 * f + i + 1)
                    done(pe.matmul(group("l2", u, i), ones[:, :], sq[i % 2], start=True, stop=True))
                for j in range(HQ):
                    delta_heads(u, j)

            def delta_heads(u, j):
                f = UNITS[u][1]
                gj = HQ * f + j
                if j == 0:
                    pe.wait_ge(qk_normed, 4 * f + 4)
                    was_read(pe, "rows", u)
                ps = sub(group("ktok", u, j))
                for t in range(TU):
                    last = pe.transpose(ps[:, t, :], qT[:, HQ + j, t * P:t * P + P], ident[:, :])
                done(last)
                ps = sub(group("vtok", u, j))
                for i in range(SUB):
                    last = pe.transpose(ps[:, i, :], vT[:, 2 * j + i // 2, (i % 2) * P:(i % 2) * P + P], ident[:, :])
                done(last)
                for s, base in (("bcb", 0), ("bcg", H)):
                    ps = sub(group(s, u, j), 2)
                    for h in range(2):
                        r = base + 2 * j + h
                        last = pe.matmul(ps[:, h, :], ident[0:16, r:r + 1].to_broadcast([16, P]), bgT,
                                         start=True, stop=True)
                    done(last)
                pe.wait_ge(seg_made, gj + 1)
                ps = sub(group("seg", u, j))
                for i in range(SUB):
                    last = pe.matmul(ps[:, i, :], sub(seg_g)[:, i, :], tri_le[:, :], start=True, stop=True)
                done(last)
                ps = sub(group("kq", u, j))
                for t in range(TU):
                    last = pe.matmul(ps[:, t, :], qT[:, HQ + j, t * P:t * P + P], qT[:, j, t * P:t * P + P],
                                     start=True, stop=True)
                done(last)
                was_read(pe, "bcb", u, j)
                ps = sub(group("kk", u, j))
                for i in range(SUB):
                    t = i % 2
                    last = pe.matmul(ps[:, i, :], qT[:, HQ + j, t * P:t * P + P], sub(kbT)[:, i, :], start=True, stop=True)
                done(last)
                pe.wait_ge(inverse_made, (2 * len(LEVELS)) * gj + 1)
                ps = sub(group("T0", u, j))
                for i in range(SUB):
                    last = pe.transpose(ps[:, i, :], sub(U)[:, i, :], ident[:, :])
                done(last)
                was_read(pe, "T0", u, j)
                for n in range(len(LEVELS)):
                    pe.wait_ge(level_made, len(LEVELS) * gj + n + 1)
                    if n:
                        pe.wait_ge(inverse_made, 2 * len(LEVELS) * gj + 2 * n + 1)
                    ps = sub(group("P", u, j, n))
                    for i in range(SUB):
                        last = pe.matmul(ps[:, i, :], sub(Lm)[:, i, :], sub(Tm)[:, i, :], start=True, stop=True)
                    done(last)
                    was_read(pe, "P", u, j, n)
                    ps = sub(group("TP", u, j, n))
                    for i in range(SUB):
                        last = pe.matmul(ps[:, i, :], sub(U)[:, i, :], sub(Pm)[:, i, :], start=True, stop=True)
                    done(last)
                    ps = sub(group("PU", u, j, n))
                    for i in range(SUB):
                        last = pe.matmul(ps[:, i, :], sub(Pm)[:, i, :], sub(U)[:, i, :], start=True, stop=True)
                    done(last)
                was_read(pe, "PU", u, j, len(LEVELS) - 1)
                pe.wait_ge(kv_scaled, 2 * (gj + 1))
                ps = sub(group("u", u, j))
                for i in range(SUB):
                    last = pe.matmul(ps[:, i, :], sub(U)[:, i, :], sub(Vp)[:, i, :], start=True, stop=True)
                done(last)
                ps = sub(group("w", u, j))
                for i in range(SUB):
                    last = pe.matmul(ps[:, i, :], sub(Kp)[:, i, :], sub(U)[:, i, :], start=True, stop=True)
                done(last)
                was_read(pe, "u", u, j)
                was_read(pe, "w", u, j)
                was_read(pe, "bcg", u, j)
                pe.wait_ge(aqk_made, gj + 1)
                ps_o = sub(group("o", u, j), 2)
                scr = scratch_banks(u, j)
                for c in range(2 * TU):
                    t, lo = c // 2, CHUNK * (c % 2)
                    n = 4 * gj + c
                    if c:
                        pe.wait_ge(state_made, n)
                    for h in range(2):
                        last = pe.matmul(scr[0][lo:lo + CHUNK, P * h:P * h + P], sub(wT)[:, 2 * h + t, lo:lo + CHUNK],
                                         state[:, 2 * j + h, :], start=True, stop=True)
                    last.then_inc(ws_done, 1)
                    pe.wait_ge(vnew_made, n + 1)
                    for h in range(2):
                        cols = slice(t * P + lo, t * P + lo + CHUNK)
                        pe.matmul(ps_o[:, h, cols], state[:, 2 * j + h, :], qgT.rearrange("p (h t) -> p h t", h=2)[:, h, cols],
                                  start=True, stop=False)
                        pe.matmul(ps_o[:, h, cols], vnew[lo:lo + CHUNK, h, :], sub(aqkT)[lo:lo + CHUNK, 2 * h + t, lo:lo + CHUNK],
                                  start=False, stop=True)
                    for h in range(2):
                        last = pe.matmul(scr[1][:, P * h:P * h + P], sub(Kd)[lo:lo + CHUNK, 2 * h + t, :],
                                         vnew[lo:lo + CHUNK, h, :], start=True, stop=True)
                    if c == 2 * TU - 1:
                        done(last)
                    else:
                        last.then_inc(ds_done, 1)
                pe.wait_ge(state_made, 4 * gj + 4)
                pe.wait_ge(o_gated, 2 * gj + 1)
                done(pe.matmul(group("oss", u, j), ones[:, :], Pm, start=True, stop=True))

            def scratch_banks(u, j):
                n = PLAN[("o", u, j)]
                for i in (1, 2):
                    pe.wait_ge(bank_read[(n + i) % BANKS], (n + i) // BANKS)
                return [banks[:, (n + i) % BANKS, :] for i in (1, 2)]

            def stick_breaking(u):
                f = UNITS[u][1]
                nb = f + 1
                for h in range(H):
                    for b in range(nb):
                        ps = sub(group("z", u, h, b), 2)
                        if h == 0 and b == 0:
                            for w in range(10, 14):
                                was_read(pe, "proj", u, w)
                        for i in range(2):
                            s = (2 * b + i) * P
                            last = pe.matmul(ps[:, i, :], sbkT[:, h, s:s + P], qT[:, h, :], start=True, stop=True)
                        done(last)
                    pe.wait_ge(softplus_made, H * f + h + 1)
                    for b in range(nb):
                        ps = sub(group("later", u, h, b), 2)
                        for i in range(2):
                            for s in range(2 * b + i, 2 * nb):
                                a = full_ge if s == 2 * b + i else ones
                                last = pe.matmul(ps[:, i, :], a[:, :], sb_sp[:, s, :], start=(s == 2 * b + i), stop=(s == 2 * nb - 1))
                        done(last)
                    pe.wait_ge(att_made, H * f + h + 1)
                    ps = group("sbo", u, h)
                    for s in range(2 * nb):
                        last = pe.matmul(ps[:, 0:T], sbv[:, s, h * P:h * P + P], sb_att[:, s, :], start=(s == 0), stop=(s == 2 * nb - 1))
                    done(last)

            def memory_attention(u):
                for m in range(MH):
                    ps = sub(group("ms", u, m), 2)
                    for t in range(TU):
                        last = pe.matmul(ps[:, t, :], qmT[:, m, t * P:t * P + P], KM[:, m, :], start=True, stop=True)
                    done(last)
                    pe.wait_ge(mprob_made, MH * u + m + 1)
                    ps = sub(group("mpT", u, m))
                    for mm in range(2):
                        for t in range(TU):
                            last = pe.transpose(ps[:, 2 * mm + t, :], mem_p[:, t, mm * P:mm * P + P], ident[:, :])
                    done(last)
                    was_read(pe, "mpT", u, m)
                    ps = group("mo", u, m)
                    for mm in range(2):
                        last = pe.matmul(ps[:, 0:T], VM[:, mm, m * P:m * P + P], mem_pT[:, mm, :], start=(mm == 0), stop=(mm == 1))
                    done(last)

            def out_projection(u):
                for w in range(NOUT):
                    ps = group("out", u, w)
                    if w == 0:
                        was_read(pe, "mo", u, MH - 1)
                        f = UNITS[u][1]
                        if UNITS[u][0] % 2 == 0:
                            pe.wait_ge(o_gated, 2 * HQ * (f + 1))
                        else:
                            was_read(pe, "sbo", u, H - 1)
                    by_token(ps, weights("out", u, w), mixT, KO)

            def queries(u):
                for w in range(NQRY):
                    by_feature(group("qry", u, w), weights("qry", u, w), xT, KT)
                for t in range(TU):
                    for i in range(2):
                        ps = sub(group("score", u, t, i))
                        if t == 0 and i == 0:
                            for w in range(NQRY):
                                was_read(pe, "qry", u, w)
                        for k in range(SUB):
                            b = SUB * i + k
                            last = pe.matmul(ps[:, k, :], qryT[:, b, t * P:t * P + P], keysT[:, 2 * UNITS[u][0] + b % 2, :],
                                             start=True, stop=True)
                        done(last)

            def expert_slot(u, k):
                n = u * TU * SLOTS + k
                pe.wait_ge(diag_made, n + 1)
                pe.wait_ge(v_landed[n % RING], 16 * (n // RING + 1))
                if k % SLOTS == 0 and n:
                    pe.wait_ge(acc_read, n // SLOTS)
                for c in range(4):
                    last = pe.matmul(acc[:, c, :], diag[:, n % DIAGS, :], VR[:, n % RING, 512 * c:512 * c + 512],
                                     start=(k % SLOTS == 0), stop=(k % SLOTS == SLOTS - 1))
                last.then_inc(v_used, 1)

            pe.wait_ge(consts_made, 1)
            pe.wait_ge(small_landed, 16 * 13)
            ps = sub(group("keys", 0))
            for i in range(2 * DEPTH):
                last = pe.transpose(ps[:, i, :], UR[:, 0, i * P:i * P + P], ident[:, :])
            done(last)

            def mix(u):
                l, f = UNITS[u]
                if u >= HALVES:
                    norm(1, u - HALVES)
                if f == 0:
                    memory_kv(l)
                x_transposes(u, 0)
                project(u)
                (deltanet if l % 2 == 0 else stick_breaking)(u)
                memory_attention(u)
                out_projection(u)
                norm(0, u)
                x_transposes(u, 1)
                queries(u)

            for u in range(len(UNITS)):
                mix(u)
                for k in range(TU * SLOTS):
                    expert_slot(u, k)
            norm(1, len(UNITS) - 2)
            norm(1, len(UNITS) - 1)

        @block.scalar
        def _(act):
            counts = {}

            def link(ins, s=None):
                s = act_step if s is None else s
                counts[s.name] = counts.get(s.name, 0) + 1
                ins.then_inc(s, 1)
                act.wait_ge(s, counts[s.name])

            def read(ins, *name):
                ins.then_inc(bank_read[PLAN[name] % BANKS], 1)

            def copy_out(dst, *name, cols=512, func=ACT.Copy, scale=1.0, shape=None):
                full(act, *name)
                src = bank(*name)[:, 0:cols]
                if shape:
                    src = sub(src, shape)
                read(act.activation(dst, src, func, scale=scale), *name)

            def x_copies(u, which):
                if which == 0 and u:
                    act.wait_ge(routed, TU * u)
                for j in range(8):
                    k, t = SUB * (j % 4), j // 4
                    copy_out(xT[:, k:k + SUB, t * P:t * P + P], "xT", u, which, j, shape=SUB)

            def memory_kv(l, u):
                if u:
                    act.wait_ge(routed, TU * u)
                for j in range(8):
                    k, t = SUB * (j % 4), j // 4
                    copy_out(xT[:, k:k + SUB, t * P:t * P + P], "memT", l, j, shape=SUB)
                for w in range(NKV):
                    if w < NKV // 2:
                        copy_out(KM[:, 2 * w:2 * w + 2, :], "kv", l, w, shape=2)
                    else:
                        c = WCOLS * (w - NKV // 2)
                        copy_out(VM[:, :, c:c + WCOLS], "kv", l, w, shape=2)

            def project(u):
                l, f = UNITS[u]
                if l % 2 == 1:
                    for w in range(NPROJ):
                        if w < 4:
                            copy_out(qT[:, 2 * w:2 * w + 2, :], "proj", u, w, scale=SCALE, shape=2)
                        elif w < 8:
                            copy_out(sbkT[:, 2 * w - 8:2 * w - 6, f * T:f * T + T], "proj", u, w, shape=2)
                        elif w < 12:
                            c = WCOLS * (w - 8)
                            copy_out(sbv[:, TU * f:TU * f + TU, c:c + WCOLS], "proj", u, w, shape=2)
                        else:
                            copy_out(qmT[:, 2 * w - 24:2 * w - 22, :], "proj", u, w, shape=2)
                    return

                def silu(w):
                    act.wait_ge(conv_made, 8 * f + w + 1)
                    dst = qT[:, 2 * w:2 * w + 2, :] if w < 4 else vT[:, 2 * w - 8:2 * w - 6, :]
                    act.activation(dst, convout[:, w % 2, :, :], ACT.Silu).then_inc(qkv_made, 1)

                for w in range(NPROJ):
                    if w < 8:
                        if w >= 2:
                            act.wait_ge(conv_made, 8 * f + w - 1)
                        copy_out(convin[:, w % 2, :, 3:3 + T], "proj", u, w, shape=2)
                        if w:
                            silu(w - 1)
                    elif w < 12:
                        if w == 8:
                            silu(7)
                        copy_out(zT[:, 2 * w - 16:2 * w - 14, :], "proj", u, w, func=ACT.Silu, shape=2)
                    else:
                        copy_out(qmT[:, 2 * w - 24:2 * w - 22, :], "proj", u, w, shape=2)

            def power(dst, src, scale):
                link(act.activation(dst, src, ACT.Ln, scale=scale, bias=eps[:, 1:2]))
                return act.activation(dst, dst, ACT.Exp, scale=-0.5)

            def deltanet(u):
                f = UNITS[u][1]
                act.wait_ge(gate_in, u + 1)
                link(act.activation(ge[:, :, :], gx[:, :, :], ACT.Exp))
                act.activation(gl[:, :, :], ge[:, :, 0:H], ACT.Ln, bias=1.0).then_inc(gate_exp, 1)
                full(act, "gcum", u)
                read(act.activation(eg[:, :, :], sub(bank("gcum", u)[:, 0:64], 2), ACT.Exp), "gcum", u)
                full(act, "rows", u)
                read(act.activation(bgT, bank("rows", u)[0:16, 0:T], ACT.Copy), "rows", u)
                for i in range(4):
                    if i == 0:
                        act.wait_ge(qkv_made, 8 * f + 8)
                    else:
                        full(act, "l2", u, i - 1)
                    act.activation(sq[i % 2], R[:, 512 * i:512 * i + 512], ACT.Square).then_inc(squared, 1)
                    if i >= 1:
                        inverse(u, i - 1)
                inverse(u, 3)
                for j in range(HQ):
                    delta_heads(u, j)

            def inverse(u, i):
                f = UNITS[u][1]
                full(act, "l2", u, i)
                if i >= 2:
                    act.wait_ge(qk_normed, 4 * f + i - 1)
                ins = act.activation(rs[i % 2], bank("l2", u, i), ACT.Ln, bias=eps[:, 1:2])
                read(ins, "l2", u, i)
                was_read(act, "l2", u, i)
                act.activation(rs[i % 2], rs[i % 2], ACT.Exp, scale=-0.5).then_inc(inverse_norm, 1)

            def delta_heads(u, j):
                f = UNITS[u][1]
                gj = HQ * f + j
                if gj:
                    act.wait_ge(o_gated, 2 * gj)
                for i in range(SUB):
                    h, t = 2 * j + i // 2, i % 2
                    ins = act.activation(sub(seg_g)[:, i, :], tri_gt[:, :], ACT.Copy, scale=g[:, t, h:h + 1])
                ins.then_inc(seg_made, 1)
                full(act, "vtok", u, j)
                for i in range(SUB):
                    h, t = 2 * j + i // 2, i % 2
                    ins = act.activation(sub(Vp)[:, i, :], sub(bank("vtok", u, j))[:, i, :], ACT.Copy, scale=bg[:, t, h:h + 1])
                read(ins, "vtok", u, j)
                full(act, "seg", u, j)
                read(act.activation(decay, bank("seg", u, j), ACT.Exp), "seg", u, j)
                copy_out(Tm, "T0", u, j)
                for n in range(len(LEVELS)):
                    copy_out(Pm, "P", u, j, n)
                copy_out(u_sb, "u", u, j)
                copy_out(wT, "w", u, j)
                full(act, "o", u, j)
                act.activation(Pm, bank("o", u, j), ACT.Square).then_inc(o_gated, 1)
                read(act.activation(o_sb, bank("o", u, j), ACT.Copy), "o", u, j)
                full(act, "oss", u, j)
                read(act.activation(Lm, bank("oss", u, j), ACT.Ln, scale=1.0 / P, bias=eps[:, 1:2]), "oss", u, j)
                was_read(act, "oss", u, j)
                act.activation(Lm, Lm, ACT.Exp, scale=-0.5).then_inc(inverse_norm, 1)

            def stick_breaking(u):
                f = UNITS[u][1]
                nb = f + 1
                for h in range(H):
                    if h:
                        act.wait_ge(att_made, H * f + h)
                    for b in range(nb):
                        copy_out(sb_z[:, 2 * b:2 * b + 2, :], "z", u, h, b, shape=2)
                    act.wait_ge(softplus_in, H * f + h + 1)
                    e = sb_e[:, 0:2 * nb, :]
                    link(act.activation(e, e, ACT.Exp))
                    act.activation(e, e, ACT.Ln, bias=1.0).then_inc(softplus_ln, 1)
                    for b in range(nb):
                        was_read(act, "later", u, h, b)
                    a = sb_att[:, 0:2 * nb, :]
                    act.activation(a, a, ACT.Exp).then_inc(att_exp, 1)
                    copy_out(mixT[:, h, :], "sbo", u, h, cols=T)

            def memory_attention(u):
                for m in range(MH):
                    full(act, "ms", u, m)
                    act.wait_ge(mmax_made, MH * u + m + 1)
                    ps = sub(bank("ms", u, m), 2)
                    if m:
                        full(act, "mpT", u, m - 1)
                    for t in range(TU):
                        ins = act.activation(mem_p[:, t, :], ps[:, t, :], ACT.Exp, scale=SCALE, bias=nmax[:, m % 2, t:t + 1],
                                             accum_out=msum[:, m % 2, t:t + 1])
                        if t == 0:
                            link(ins)
                    read(ins, "ms", u, m)
                    if m:
                        full(act, "mo", u, m - 1)
                    copy_out(mem_pT[:, :, :], "mpT", u, m, shape=2)
                    copy_out(mixT[:, H + m, :], "mo", u, m, cols=T)

            def norm(kind, u):
                act.wait_ge(stats_made, norm_index(kind, u) + 1)
                link(act.activation(rstd[:, :, 0], mv[:, :, 1], ACT.Ln, bias=eps[:, 0:1]))
                act.activation(rstd[:, :, 1], rstd[:, :, 0], ACT.Exp, scale=-0.5).then_inc(rstd_made, 1)

            def queries(u):
                for w in range(NQRY):
                    copy_out(qryT[:, 2 * w:2 * w + 2, :], "qry", u, w, shape=2)
                for t in range(TU):
                    if t:
                        act.wait_ge(routed, TU * u + t)
                    for i in range(2):
                        copy_out(s_sb[:, SUB * i:SUB * i + SUB, :], "score", u, t, i, shape=SUB)
                    act.wait_ge(cdiff_made, TU * u + t + 1)
                    act.activation(cd[:, :, :], cd[:, :, :], ACT.Exp).then_inc(cexp_made, 1)

            def expert_gelu(u, kk):
                n = u * TU * SLOTS // GROUP + kk
                act.wait_ge(dot_made, GROUP * (n + 1))
                if n >= 2:
                    act.wait_ge(coef_made, n - 1)
                act.activation(gel[:, n % 2, :], hdot[:, n % 2, :], ACT.Gelu).then_inc(gelu_made, 1)

            def expert_diag(u, k):
                n = u * TU * SLOTS + k
                if k % GROUP == 0:
                    act.wait_ge(coef_made, n // GROUP + 1)
                if n >= DIAGS:
                    act.wait_ge(v_used, n - DIAGS + 1)
                act.activation(diag[:, n % DIAGS, :], ident[:, :], ACT.Copy,
                               scale=coef[:, (n // GROUP) % 2, k % GROUP:k % GROUP + 1]).then_inc(diag_made, 1)

            act.wait_ge(consts_made, 1)
            act.wait_ge(small_landed, 16 * 13)
            copy_out(keysT[:, :, :], "keys", 0, shape=4)
            link(act.activation(nexp[:, :], nexp[:, :], ACT.Exp))

            def mix(u):
                l, f = UNITS[u]
                if u >= HALVES:
                    norm(1, u - HALVES)
                if f == 0:
                    memory_kv(l, u)
                x_copies(u, 0)
                project(u)
                (deltanet if l % 2 == 0 else stick_breaking)(u)
                memory_attention(u)
                norm(0, u)
                x_copies(u, 1)
                queries(u)

            for u in range(len(UNITS)):
                mix(u)
                for kk in range(TU * SLOTS // GROUP + 1):
                    if kk:
                        for i in range(GROUP):
                            expert_diag(u, (kk - 1) * GROUP + i)
                    if kk < TU * SLOTS // GROUP:
                        expert_gelu(u, kk)
            norm(1, len(UNITS) - 2)
            norm(1, len(UNITS) - 1)

        @block.vector
        def _(dve):
            counts = {}

            def link(ins, s=None):
                s = dve_step if s is None else s
                counts[s.name] = counts.get(s.name, 0) + 1
                ins.then_inc(s, 1)
                dve.wait_ge(s, counts[s.name])

            def read(ins, *name):
                ins.then_inc(bank_read[PLAN[name] % BANKS], 1)
                was_read(dve, *name)

            def project(u):
                l, f = UNITS[u]
                if l % 2 == 1:
                    return
                for w in range(8):
                    r = w % 2
                    if w >= 2:
                        dve.wait_ge(qkv_made, 8 * f + w - 1)
                    if f == 0:
                        link(dve.memset(convin[:, r, :, 0:3], 0.0))
                    else:
                        link(dve.tensor_copy(convin[:, r, :, 0:3], hist[:, 2 * w:2 * w + 2, :]))
                    was_read(dve, "proj", u, w)
                    link(dve.tensor_copy(hist[:, 2 * w:2 * w + 2, :], convin[:, r, :, T:T + 3]))
                    for i in range(4):
                        for b in range(2):
                            c, o = convw[:, 2 * w + b, i:i + 1], convout[:, r, b, :]
                            src = convin[:, r, b, i:i + T]
                            if i == 0:
                                ins = dve.tensor_scalar(o, src, c, None, ALU.mult)
                            else:
                                ins = dve.scalar_tensor_tensor(out=o, in0=src, scalar=c, in1=o, op0=ALU.mult, op1=ALU.add)
                            if i == 3 and b == 1:
                                link(ins, conv_made)
                            elif b == 1:
                                link(ins)

            def deltanet(u):
                f = UNITS[u][1]
                full(dve, "ba", u)
                ps = sub(bank("ba", u)[:, 0:32], 2)
                link(dve.tensor_tensor(ga[:, :, :], ps[:, :, H:2 * H], dtb[:, None, :].to_broadcast([P, TU, H]), ALU.add))
                read(dve.tensor_scalar(gx[:, :, H:2 * H], ps[:, :, 0:H], -1.0, 80.0, ALU.mult, ALU.min), "ba", u)
                link(dve.scalar_tensor_tensor(out=gx[:, :, 0:H], in0=ga[:, :, :], scalar=-1.0, in1=ga[:, :, :],
                                              op0=ALU.mult, op1=ALU.min), gate_in)
                dve.wait_ge(gate_exp, u + 1)
                link(dve.scalar_tensor_tensor(out=gl[:, :, :], in0=ga[:, :, :], scalar=0.0, in1=gl[:, :, :],
                                              op0=ALU.max, op1=ALU.add))
                link(dve.tensor_scalar(bg[:, :, 0:H], ge[:, :, H:2 * H], 1.0, None, ALU.add))
                link(dve.reciprocal(bg[:, :, 0:H], bg[:, :, 0:H]))
                link(dve.scalar_tensor_tensor(out=g[:, :, :], in0=gl[:, :, :], scalar=-1.0,
                                              in1=nexp[:, None, :].to_broadcast([P, TU, H]), op0=ALU.mult, op1=ALU.mult), g_made)
                was_read(dve, "gcum", u)
                link(dve.tensor_tensor(bexpg[:, :, :], bg[:, :, 0:H], eg[:, :, 0:H], ALU.mult))
                link(dve.tensor_copy(bg[:, :, H:2 * H], eg[:, :, 0:H]), rows_made)
                for i in range(4):
                    dve.wait_ge(inverse_norm, (4 + HQ) * f + i + 1)
                    a = R[:, 512 * i:512 * i + 512]
                    link(dve.scalar_tensor_tensor(out=a, in0=a, scalar=SCALE if i < 2 else 1.0, in1=rs[i % 2],
                                                  op0=ALU.mult, op1=ALU.mult), qk_normed)
                for j in range(HQ):
                    delta_heads(u, j)

            def delta_heads(u, j):
                f = UNITS[u][1]
                gj = HQ * f + j
                full(dve, "ktok", u, j)
                ps = sub(bank("ktok", u, j))
                for i in range(SUB):
                    h, t = 2 * j + i // 2, i % 2
                    dve.tensor_scalar(sub(Kp)[:, i, :], ps[:, t, :], bexpg[:, t, h:h + 1], None, ALU.mult).then_inc(kv_scaled, 1) \
                        if i == 3 else dve.tensor_scalar(sub(Kp)[:, i, :], ps[:, t, :], bexpg[:, t, h:h + 1], None, ALU.mult)
                for i in range(SUB):
                    h, t = 2 * j + i // 2, i % 2
                    ins = dve.tensor_scalar(sub(Kd)[:, i, :], ps[:, t, :], eg[:, t, H + h:H + h + 1], None, ALU.mult)
                read(ins, "ktok", u, j)
                full(dve, "bcb", u, j)
                k2 = qT[:, HQ + j:HQ + j + 1, :].to_broadcast([P, 2, T])
                q2 = qT[:, j:j + 1, :].to_broadcast([P, 2, T])
                read(dve.tensor_tensor(sub(kbT, 2), k2, sub(bank("bcb", u, j), 2), ALU.mult), "bcb", u, j)
                full(dve, "bcg", u, j)
                read(dve.tensor_tensor(sub(qgT, 2), q2, sub(bank("bcg", u, j), 2), ALU.mult), "bcg", u, j)
                was_read(dve, "seg", u, j)
                four = [P, SUB, P]
                link(dve.tensor_tensor(sub(decay), sub(decay), tri_le[:, None, :].to_broadcast(four), ALU.mult))
                full(dve, "kq", u, j)
                for h in range(2):
                    ins = dve.tensor_tensor(sub(aqkT)[:, 2 * h:2 * h + 2, :], sub(bank("kq", u, j))[:, 0:2, :],
                                            sub(decay)[:, 2 * h:2 * h + 2, :], ALU.mult)
                read(ins, "kq", u, j)
                full(dve, "kk", u, j)
                read(dve.tensor_tensor(MT, bank("kk", u, j), decay, ALU.mult), "kk", u, j)
                link(dve.tensor_tensor(sub(Lm), sub(MT), lvl[:, 0:1, :].to_broadcast(four), ALU.mult), aqk_made)
                link(dve.scalar_tensor_tensor(out=sub(U), in0=sub(Lm), scalar=-1.0, in1=ident[:, None, :].to_broadcast(four),
                                              op0=ALU.mult, op1=ALU.add), inverse_made)
                for n in range(len(LEVELS)):
                    if n:
                        full(dve, "P", u, j, n - 1)
                    link(dve.tensor_tensor(sub(Lm), sub(MT), lvl[:, n + 1:n + 2, :].to_broadcast(four), ALU.mult), level_made)
                    full(dve, "PU", u, j, n)
                    last = n == len(LEVELS) - 1
                    read(dve.tensor_tensor(Tm, Tm, bank("TP", u, j, n), ALU.subtract), "TP", u, j, n)
                    read(dve.tensor_tensor(U, U, bank("PU", u, j, n), ALU.subtract), "PU", u, j, n)
                    if not last:
                        link(dve.tensor_copy(mv[:, 0, 0:1], eps[:, 0:1]), inverse_made)
                        link(dve.tensor_copy(mv[:, 0, 0:1], eps[:, 0:1]), inverse_made)
                    else:
                        link(dve.tensor_copy(mv[:, 0, 0:1], eps[:, 0:1]), inverse_made)
                dve.tensor_copy(mv[:, 0, 0:1], eps[:, 0:1]).then_inc(kv_scaled, 1)
                was_read(dve, "u", u, j)
                scr = [banks[:, (PLAN[("o", u, j)] + i) % BANKS, :] for i in (1, 2)]
                for c in range(2 * TU):
                    t, lo = c // 2, CHUNK * (c % 2)
                    n = 4 * gj + c
                    dve.wait_ge(ws_done, n + 1)
                    us = u_sb.rearrange("p (h t v) -> p h t v", h=2, t=TU)[lo:lo + CHUNK, :, t, :]
                    link(dve.tensor_tensor(vnew[lo:lo + CHUNK, :, :], us, sub(scr[0][:, 0:2 * P], 2)[lo:lo + CHUNK], ALU.subtract), vnew_made)
                    if c == 2 * TU - 1:
                        full(dve, "o", u, j)
                    else:
                        dve.wait_ge(ds_done, 3 * gj + c + 1)
                    for h in range(2):
                        s = state[:, 2 * j + h, :]
                        x0 = 16 + H * (c % 2) + 2 * j + h
                        ins = dve.scalar_tensor_tensor(out=s, in0=s, scalar=eg[:, t, x0:x0 + 1], in1=scr[1][:, P * h:P * h + P],
                                                       op0=ALU.mult, op1=ALU.add)
                    link(ins, state_made)
                dve.wait_ge(inverse_norm, (4 + HQ) * f + 4 + j + 1)
                was_read(dve, "o", u, j)
                link(dve.scalar_tensor_tensor(out=o_sb, in0=o_sb, scalar=onorm[:, 0:1], in1=Lm, op0=ALU.mult, op1=ALU.mult))
                link(dve.tensor_tensor(MIX[:, 2 * j * T:(2 * j + 2) * T], o_sb, R[:, 5120 + 2 * j * T:5120 + (2 * j + 2) * T], ALU.mult))
                dve.tensor_copy(mv[:, 0, 0:1], eps[:, 0:1]).then_inc(o_gated, 1)

            def stick_breaking(u):
                f = UNITS[u][1]
                nb = f + 1
                dve.wait_ge(sbmask_made, 1)
                for h in range(H):
                    for b in range(nb):
                        was_read(dve, "z", u, h, b)
                    link(dve.scalar_tensor_tensor(out=XT[:, 1024:1024 + 512 * nb], in0=XT[:, 0:512 * nb], scalar=-1.0,
                                                  in1=XT[:, 0:512 * nb], op0=ALU.mult, op1=ALU.min), softplus_in)
                    dve.wait_ge(softplus_ln, H * f + h + 1)
                    link(dve.scalar_tensor_tensor(out=XT[:, 2048:2048 + 512 * nb], in0=XT[:, 0:512 * nb], scalar=0.0,
                                                  in1=XT[:, 1024:1024 + 512 * nb], op0=ALU.max, op1=ALU.add))
                    m = sb_sp[:, 2 * nb - 2:2 * nb, :]
                    link(dve.tensor_tensor(m, m, sbmask[:, :, :], ALU.mult), softplus_made)
                    for b in range(nb):
                        full(dve, "later", u, h, b)
                        read(dve.tensor_tensor(sb_att[:, 2 * b:2 * b + 2, :], sb_z[:, 2 * b:2 * b + 2, :],
                                               sub(bank("later", u, h, b), 2), ALU.subtract), "later", u, h, b)
                    dve.wait_ge(att_exp, H * f + h + 1)
                    m = sb_att[:, 2 * nb - 2:2 * nb, :]
                    link(dve.tensor_tensor(m, m, sbmask[:, :, :], ALU.mult), att_made)

            def memory_attention(u):
                for m in range(MH):
                    full(dve, "ms", u, m)
                    link(dve.tensor_reduce(nmax[:, m % 2, :], sub(bank("ms", u, m), 2), AX_X, ALU.max))
                    link(dve.tensor_scalar(nmax[:, m % 2, :], nmax[:, m % 2, :], -SCALE, None, ALU.mult), mmax_made)
                    was_read(dve, "ms", u, m)
                    link(dve.reciprocal(msum[:, m % 2, :], msum[:, m % 2, :]))
                    for t in range(TU):
                        ins = dve.tensor_scalar(mem_p[:, t, :], mem_p[:, t, :], msum[:, m % 2, t:t + 1], None, ALU.mult)
                    link(ins, mprob_made)

            def out_projection(u):
                t0 = TU * UNITS[u][1]
                for w in range(NOUT):
                    full(dve, "out", u, w)
                    a = X[:, t0:t0 + TU, WCOLS * w:WCOLS * (w + 1)]
                    read(dve.scalar_tensor_tensor(out=a, in0=a, scalar=ALPHA, in1=sub(bank("out", u, w), 2),
                                                  op0=ALU.mult, op1=ALU.add), "out", u, w)

            def norm(kind, u):
                t0 = TU * UNITS[u][1]
                for t in range(TU):
                    for c in range(4):
                        ins = dve.bn_stats(stats[:, t, c, :], X[:, t0 + t, 512 * c:512 * c + 512])
                link(ins)
                for t in range(TU):
                    ins = dve.bn_aggr(mv[:, t, :], stats[:, t, :, :])
                link(ins, stats_made)
                dve.wait_ge(rstd_made, norm_index(kind, u) + 1)
                for t in range(TU):
                    a = X[:, t0 + t, :]
                    ins = dve.tensor_scalar(a, a, mv[:, t, 0:1], rstd[:, t, 1:2], ALU.subtract, ALU.mult)
                link(ins)
                for c in range(4):
                    a = X[:, t0:t0 + TU, 512 * c:512 * c + 512]
                    for name, op in (("norm_g", ALU.mult), ("norm_b", ALU.add)):
                        full(dve, name, kind, u, c)
                        v = banks[:, PLAN[(name, kind, u, c)] % BANKS:PLAN[(name, kind, u, c)] % BANKS + 1, :]
                        read(dve.tensor_tensor(a, a, v.to_broadcast([P, TU, 512]), op), name, kind, u, c)
                link(dve.tensor_copy(mv[:, 0, 0:1], eps[:, 0:1]), x_normed)

            def queries(u):
                l = UNITS[u][0]
                for t in range(TU):
                    was_read(dve, "score", u, t, 0)
                    was_read(dve, "score", u, t, 1)
                    G8 = range(2 * PH)
                    for b in G8:
                        ins = dve.max(tv[:, b, 0:8], s_sb[:, b, :])
                    link(ins)
                    for b in G8:
                        dve.max_index(ti[:, b, 0:8], tv[:, b, 0:8], s_sb[:, b, :])
                        ins = dve.match_replace(s_wk[:, b, :], tv[:, b, 0:8], s_sb[:, b, :], -3.0e38)
                    link(ins)
                    for b in G8:
                        ins = dve.max(tv[:, b, 8:16], s_wk[:, b, :])
                    link(ins)
                    for b in G8:
                        ins = dve.max_index(ti[:, b, 8:16], tv[:, b, 8:16], s_wk[:, b, :])
                    link(ins)
                    link(dve.tensor_copy(tif[:, :, :], ti[:, :, :]))
                    tvh = tv[:, :, :].rearrange("p (h s) k -> p h s k", s=2)
                    tih = tif[:, :, :].rearrange("p (h s) k -> p h s k", s=2)
                    c4 = [P, PH, HALF_TOPK, HALF_TOPK]
                    link(dve.tensor_tensor(cand, tvh[:, :, 0, :, None].to_broadcast(c4), tvh[:, :, 1, None, :].to_broadcast(c4), ALU.add))
                    flat = XT[:, 0:1024].rearrange("p (h c) -> p h c", h=PH)
                    for h in range(PH):
                        ins = dve.max(cv[:, h, :], flat[:, h, :])
                    link(ins)
                    for h in range(PH):
                        ins = dve.max_index(ci[:, h, :], cv[:, h, :], flat[:, h, :])
                    link(ins)
                    link(dve.tensor_tensor(cd[:, :, :], cv[:, :, :], cv[:, :, 0:1].to_broadcast([P, PH, TOPK]), ALU.subtract), cdiff_made)
                    cif = ci[:, :, :].rearrange("p h k -> p (h k)")
                    dve.tensor_scalar(cp[:, 0, :], cif, 4, None, ALU.logical_shift_right)
                    link(dve.tensor_scalar(cp[:, 1, :], cif, 15, None, ALU.bitwise_and))
                    link(dve.tensor_copy(cpf[:, :, :], cp[:, :, :]))
                    h3 = [P, SLOTS, HALF_TOPK]
                    for s in range(2):
                        o = hot[s].rearrange("p h k i -> p (h k) i")
                        ins = dve.tensor_tensor(o, cpf[:, s, :, None].to_broadcast(h3), iota16[:, None, :].to_broadcast(h3), ALU.is_equal)
                    link(ins)
                    for s in range(2):
                        ins = dve.tensor_tensor(hot[s], hot[s], tih[:, :, s, None, :].to_broadcast([P, PH, TOPK, HALF_TOPK]), ALU.mult)
                    link(ins)
                    for s in range(2):
                        ins = dve.tensor_reduce(i12[:, s, :], hot[s].rearrange("p h k i -> p (h k) i"), AX_X, ALU.add)
                    link(ins)
                    link(dve.scalar_tensor_tensor(out=i12[:, 0, :], in0=i12[:, 0, :], scalar=float(NK), in1=i12[:, 1, :],
                                                  op0=ALU.mult, op1=ALU.add))
                    link(dve.tensor_scalar(idx[:, u % 2, t, :], i12[:, 0, :], float(l * NE), None, ALU.add))
                    dve.wait_ge(cexp_made, TU * u + t + 1)
                    link(dve.tensor_reduce(csum[:, 0, :], cd[:, :, :], AX_X, ALU.add))
                    link(dve.reciprocal(csum[:, 1, :], csum[:, 0, :]))
                    link(dve.tensor_tensor(gate[:, u % 2, t, :].rearrange("p (h k) -> p h k", h=PH), cd[:, :, :],
                                           csum[:, 1, :, None].to_broadcast([P, PH, TOPK]), ALU.mult), routed)

            def expert_dot(u, k):
                n = u * TU * SLOTS + k
                dve.wait_ge(u_landed[n % RING], 16 * (n // RING + 1))
                if k % GROUP == 0 and n // GROUP >= 2:
                    dve.wait_ge(gelu_made, n // GROUP - 1)
                a = UR[:, n % RING, :]
                gi = (n // GROUP) % 2
                dve.tensor_tensor_reduce(a, a, X[:, TU * UNITS[u][1] + k // SLOTS, :], 1.0, 0.0, ALU.mult, ALU.add,
                                         hdot[:, gi, k % GROUP:k % GROUP + 1]).then_inc(dot_made, 1)

            def expert_coef(u, kk):
                n = u * TU * SLOTS // GROUP + kk
                dve.wait_ge(gelu_made, n + 1)
                if n >= 2:
                    dve.wait_ge(diag_made, GROUP * (n - 1))
                t, s = kk * GROUP // SLOTS, kk * GROUP % SLOTS
                dve.tensor_tensor(coef[:, n % 2, :], gel[:, n % 2, :], gate[:, u % 2, t, s:s + GROUP], ALU.mult).then_inc(coef_made, 1)

            def expert_sum(u, t):
                n = TU * u + t
                dve.wait_ge(v_used, SLOTS * (n + 1))
                dve.wait_ge(dot_made, SLOTS * (n + 1))
                a = X[:, TU * UNITS[u][1] + t, :]
                dve.scalar_tensor_tensor(out=a, in0=a, scalar=ALPHA, in1=acc[:, :, :].rearrange("p c n -> p (c n)"),
                                         op0=ALU.mult, op1=ALU.add).then_inc(acc_read, 1)
                dve.wait_ge(acc_read, n + 1)

            dve.wait_ge(consts_made, 1)
            dve.wait_ge(small_landed, 16 * 13)
            dve.wait_ge(x_landed, 16)

            def mix(u):
                l, f = UNITS[u]
                if u >= HALVES:
                    norm(1, u - HALVES)
                project(u)
                (deltanet if l % 2 == 0 else stick_breaking)(u)
                memory_attention(u)
                out_projection(u)
                norm(0, u)
                queries(u)

            for u in range(len(UNITS)):
                mix(u)
                for kk in range(TU * SLOTS // GROUP + 1):
                    if kk < TU * SLOTS // GROUP:
                        for i in range(GROUP):
                            expert_dot(u, kk * GROUP + i)
                            if i == 1 and kk:
                                expert_coef(u, kk - 1)
                    else:
                        expert_coef(u, kk - 1)
                    if kk and kk * GROUP % SLOTS == 0:
                        expert_sum(u, kk * GROUP // SLOTS - 1)
            norm(1, len(UNITS) - 2)
            norm(1, len(UNITS) - 1)


_INS = ['x', 'mem', 'gdn_w_in', 'gdn_conv', 'gdn_a_log', 'gdn_dt_bias', 'gdn_onorm', 'sb_w_in', 'mem_w_kv', 'w_out',
        'ln_mix_g', 'ln_mix_b', 'peer_w_q', 'peer_keys', 'peer_u', 'peer_v', 'ln_ffn_g', 'ln_ffn_b']


def kernel(**inputs):
    import numpy as _np
    import concourse.bacc as _bacc
    from concourse import mybir as _mybir
    from concourse.bass_utils import run_bass_kernel_spmd as _run

    nc = _bacc.Bacc("TRN2", target_bir_lowering=False, num_devices=1)
    arrays, args = {}, []
    for name in _INS:
        a = _np.ascontiguousarray(inputs[name])
        arrays[f"in_{name}"] = a
        args.append(nc.dram_tensor(f"in_{name}", a.shape, _mybir.dt.from_np(a.dtype), kind="ExternalInput").ap())
    shape = inputs['x'].shape
    args.append(nc.dram_tensor("out_0", shape, _mybir.dt.float32, kind="ExternalOutput").ap())
    build(nc, *args)
    r = _run(nc, [arrays], core_ids=[0])
    return r.results[0]["out_0"]
```

```python
from contextlib import ExitStack

import concourse.bass as bass
from concourse import mybir

F32 = mybir.dt.float32
U32 = mybir.dt.uint32
ALU = mybir.AluOpType
ACT = mybir.ActivationFunctionType
AX_X = mybir.AxisListType.X

P = 128
CHUNK = 64
SUB = 4
WCOLS = 256
RING = 3
DIAGS = 3
GROUP = 8
HALF_TOPK = 16
TOPK = 8
LN_EPS = 1e-5
RMS_EPS = 1e-6
BANKS = 4
LEVELS = (2, 4, 8, 16, 32)


def build(nc, x, mem, gdn_w_in, gdn_conv, gdn_a_log, gdn_dt_bias, gdn_onorm, sb_w_in, mem_w_kv, w_out,
          ln_mix_g, ln_mix_b, peer_w_q, peer_keys, peer_u, peer_v, ln_ffn_g, ln_ffn_b, out):
    _, S, D = x.shape
    DEPTH = w_out.shape[0]
    NMEM = mem.shape[1]
    KT = D // P
    NT = S // P
    TU = 2
    T = TU * P
    HALVES = NT // TU
    H = gdn_a_log.shape[1]
    HQ = H // 2
    MH = mem_w_kv.shape[2] // (2 * P)
    PH = peer_w_q.shape[2] // (2 * P)
    NK = peer_keys.shape[2]
    NE = peer_u.shape[1]
    SLOTS = PH * TOPK
    KO = w_out.shape[1] // P
    ALPHA = (2.0 * DEPTH) ** 0.25
    SCALE = float(P) ** -0.5
    assert (S, D, DEPTH, NMEM, T, H, MH, PH, NK) == (512, 2048, 2, 256, 256, 8, 4, 4, 128)
    UNITS = [(l, f) for l in range(DEPTH) for f in range(HALVES)]
    NPROJ = 14
    NOUT = D // WCOLS
    NQRY = 2 * PH * P // WCOLS
    NKV = 2 * MH * P // WCOLS
    QM0 = 2 * HQ * P + 2 * H * P + 2 * H

    PLAN, LOADS, USER, COSTS, FIRST = {}, {}, {}, [], []

    def plan(*name, cost=1.0):
        PLAN[name] = len(PLAN)
        COSTS.append(cost)

    def load(*name, user=None):
        LOADS[name] = len(LOADS)
        USER[LOADS[name]] = user or name

    def plan_norm(kind, u, then=None):
        for c in range(4 + 1):
            if c < 4:
                plan("norm_g", kind, u, c)
                plan("norm_b", kind, u, c)
            if then and c >= 1:
                plan("xT", *then, 2 * c - 2)
                plan("xT", *then, 2 * c - 1)

    plan("keys", 0)
    for u, (l, f) in enumerate(UNITS):
        FIRST.append(len(PLAN))
        if f == 0:
            load("mem", l, user=("memT", l, 7))
            for j in range(8):
                plan("memT", l, j)
            for w in range(NKV):
                load("kv", l, w)
                plan("kv", l, w, cost=14.0)
        if u >= HALVES:
            plan_norm(1, u - HALVES, then=(u, 0))
        else:
            for j in range(8):
                plan("xT", u, 0, j)
        if l % 2 == 0:
            plan("ba", u)
        for w in range(NPROJ):
            load("proj", u, w)
            plan("proj", u, w, cost=14.0)
            if l % 2 == 0:
                if 4 <= w < 8:
                    plan("l2", u, w - 4, cost=1.0)
                if w == 8:
                    plan("gcum", u)
                if w == 10:
                    plan("rows", u)
        if l % 2 == 0:
            for j in range(HQ):
                for s in ("ktok", "vtok", "bcb", "bcg", "seg", "kq", "kk", "T0"):
                    plan(s, u, j, cost=1.3)
                for i in range(len(LEVELS)):
                    for s in ("P", "TPU"):
                        for h in range(2):
                            plan(s, u, j, i, h, cost=0.8)
                plan("w", u, j)
                plan("u", u, j)
                plan("o", u, j, cost=10.0)
                plan("oss", u, j, cost=2.0)
        else:
            for h in (0, 1):
                for b in range(f + 1):
                    plan("z", u, h, b, cost=1.0)
            for b in range(f + 1):
                plan("later", u, 0, b, cost=2.0)
            for h in range(H):
                if h + 1 < H:
                    for b in range(f + 1):
                        plan("later", u, h + 1, b, cost=2.0)
                plan("sbo", u, h, cost=1.5 + f)
                if h + 2 < H:
                    for b in range(f + 1):
                        plan("z", u, h + 2, b, cost=1.0)
        plan("ms", u, 0)
        plan("ms", u, 1)
        plan("mpT", u, 0)
        for m in range(MH):
            if m + 2 < MH:
                plan("ms", u, m + 2)
            if m + 1 < MH:
                plan("mpT", u, m + 1)
            plan("mo", u, m)
        for w in range(NOUT):
            load("out", u, w)
            plan("out", u, w, cost=10.5)
        plan_norm(0, u, then=(u, 1))
        for w in range(NQRY):
            load("qry", u, w)
            plan("qry", u, w, cost=14.0)
        for t in range(TU):
            plan("score", u, t, 0, cost=10.0)
            plan("score", u, t, 1)
    FIRST.append(len(PLAN))
    for u in (len(UNITS) - HALVES, len(UNITS) - 1):
        plan_norm(1, u)

    ON_DVE = [8, 8, 8, 0]
    SLOT_COUNT = TU * SLOTS
    DIAG_SLOTS = [n for n in range(len(UNITS) * SLOT_COUNT) if n % GROUP >= ON_DVE[n // SLOT_COUNT]]
    STEPS = SLOT_COUNT + GROUP
    STEPS_AT = {}
    for u in range(1, len(UNITS)):
        whole, so_far = sum(COSTS[FIRST[u]:FIRST[u + 1]]), 0.0
        for n in range(FIRST[u], FIRST[u + 1]):
            STEPS_AT[n] = (u - 1, min(STEPS, int(STEPS * so_far / (0.94 * whole))))
            so_far += COSTS[n]

    class Experts:

        def __init__(self, step):
            self.step, self.at = step, {}

        def until(self, u, k):
            for i in range(self.at.get(u, 0), k):
                self.step(u, i)
            self.at[u] = max(k, self.at.get(u, 0))

        def before(self, *name):
            if PLAN[name] in STEPS_AT:
                self.until(*STEPS_AT[PLAN[name]])

        def rest(self, u):
            self.until(u, STEPS)

    def full(eng, *name, experts=None):
        if experts:
            experts.before(*name)
        eng.wait_ge(group_done, PLAN[name] + 1)

    def was_read(eng, *name, experts=None):
        if experts:
            experts.before(*name)
        n = PLAN[name]
        eng.wait_ge(bank_read[n % BANKS], n // BANKS + 1)

    with ExitStack() as ctx:
        def sb(name, shape, dt=F32):
            return ctx.enter_context(nc.sbuf_tensor(name, shape, dt))

        def sem(name):
            return ctx.enter_context(nc.semaphore(name))

        acc = ctx.enter_context(nc.psum_tensor("acc", [P, 4, 512], F32))
        banks = ctx.enter_context(nc.psum_tensor("banks", [P, BANKS, 512], F32))

        X = sb("X", [P, NT, D])
        XT = sb("XT", [P, KT * T])
        W = sb("W", [P, 2, KT * WCOLS])
        UR = sb("UR", [P, RING, D])
        VR = sb("VR", [P, RING, D])
        NV = sb("NV", [64, 256])
        MIX = sb("MIX", [P, KO * T])
        KM = sb("KM", [P, MH, NMEM])
        VM = sb("VM", [P, NMEM // P, MH * P])
        R = sb("R", [P, 11264])
        xT = XT[:, :].rearrange("p (k t) -> p k t", k=KT)
        mixT = MIX[:, :].rearrange("p (k t) -> p k t", k=KO)
        qryT = MIX[:, 0:2 * PH * T].rearrange("p (k t) -> p k t", k=2 * PH)
        qT = R[:, 0:2048].rearrange("p (h t) -> p h t", t=T)
        qmT = R[:, 2048:3072].rearrange("p (h t) -> p h t", t=T)
        vT = R[:, 3072:5120].rearrange("p (h t) -> p h t", t=T)
        zT = R[:, 5120:7168].rearrange("p (h t) -> p h t", t=T)
        convin = R[:, 7168:7168 + 1040].rearrange("p (r b t) -> p r b t", r=2, b=2)
        convout = R[:, 8208:8208 + 1024].rearrange("p (r b t) -> p r b t", r=2, b=2)
        sbkT = R[:, 3072:7168].rearrange("p (h t) -> p h t", t=S)
        sbv = R[:, 7168:11264].rearrange("p (t f) -> p t f", t=NT)

        def half_bank(region, i):
            return region[:, 512 * i:512 * i + 512]

        work = [half_bank(XT, i) for i in range(8)] + [half_bank(R[:, 7168:11264], i) for i in range(6)]
        (seg_g, decay, kbT, qgT, Kp, Kd, Vp, MT, _, _, Pm, Lm, aqkT, spare) = work
        TT = R[:, 7168:8192].rearrange("p (h w t c) -> p h w t c", h=2, w=2, t=TU)
        levels = (Lm, kbT)
        u_sb, wT, o_sb = decay, kbT, Vp
        vnew = seg_g[:, 0:2 * P].rearrange("p (h v) -> p h v", h=2)
        bgT = spare[0:16, 0:T]
        state = R[:, 10240:11264].rearrange("p (h v) -> p h v", h=H)
        sq = [half_bank(MIX, i) for i in range(4)]
        rs = [half_bank(MIX, 4 + i) for i in range(2)]
        hist = sb("hist", [P, 16, 3])
        convw = sb("convw", [P, 16, 4])
        wba = sb("wba", [P, KT, 16])
        onorm = sb("onorm", [P, 1])
        dtb = sb("dtb", [P, H])
        nexp = sb("nexp", [P, H])
        gx = sb("gx", [P, TU, 16])
        ge = sb("ge", [P, TU, 16])
        ga = sb("ga", [P, TU, H])
        gl = sb("gl", [P, TU, H])
        g = sb("g", [P, TU, H])
        eg = sb("eg", [P, TU, 32])
        bg = sb("bg", [P, TU, 16])
        bexpg = sb("bexpg", [P, TU, H])
        ident = sb("ident", [P, P])
        ones = sb("ones", [P, P])
        tri_le = sb("tri_le", [P, P])
        tri_gt = sb("tri_gt", [P, P])
        full_ge = sb("full_ge", [P, P])
        lvl = sb("lvl", [P, 6, P])
        sbmask = lvl[:, 0:4, :].rearrange("p a c -> p (a c)").rearrange("p (b t) -> p b t", b=2)
        iota16 = sb("iota16", [P, 16])
        eps = sb("eps", [P, 2])
        stats = sb("stats", [P, TU, NOUT, 6])
        mv = sb("mv", [P, TU, 2])
        rstd = sb("rstd", [P, TU, 2])
        keysT = sb("keysT", [P, 2 * DEPTH, NK])
        nmax = sb("nmax", [P, 2, TU])
        msum = sb("msum", [P, 2, TU])
        sb_z = [XT[:, 1024 * i:1024 * i + 1024].rearrange("p (s t) -> p s t", t=T) for i in (0, 1)]
        sb_sp = [XT[:, 1024 * i:1024 * i + 1024].rearrange("p (s t) -> p s t", t=T) for i in (2, 3)]
        mem_p = [half_bank(XT, i).rearrange("p (t m) -> p t m", t=TU) for i in (0, 1)]
        mem_pT = [half_bank(XT, i).rearrange("p (m t) -> p m t", m=2) for i in (2, 3)]
        s_sb = R[:, 0:1024].rearrange("p (g n) -> p g n", g=8)
        s_wk = R[:, 1024:2048].rearrange("p (g n) -> p g n", g=8)
        cand = XT[:, 0:1024].rearrange("p (h i j) -> p h i j", h=PH, i=16)
        hot = [XT[:, 1024 + 512 * i:1536 + 512 * i].rearrange("p (h k i) -> p h k i", h=PH, k=TOPK) for i in range(2)]
        tv = XT[:, 2048:2176].rearrange("p (g k) -> p g k", g=2 * PH)
        ti = XT[:, 2176:2304].bitcast(U32).rearrange("p (g k) -> p g k", g=2 * PH)
        tif = XT[:, 2304:2432].rearrange("p (g k) -> p g k", g=2 * PH)
        cv = XT[:, 2432:2464].rearrange("p (h k) -> p h k", h=PH)
        ci = XT[:, 2464:2496].bitcast(U32).rearrange("p (h k) -> p h k", h=PH)
        cp = XT[:, 2496:2560].bitcast(U32).rearrange("p (s k) -> p s k", s=2)
        cpf = XT[:, 2560:2624].rearrange("p (s k) -> p s k", s=2)
        i12 = XT[:, 2624:2688].rearrange("p (s k) -> p s k", s=2)
        cd = XT[:, 2688:2720].rearrange("p (h k) -> p h k", h=PH)
        csum = XT[:, 2720:2728].rearrange("p (s h) -> p s h", s=2)
        gate = sb("gate", [P, 2, TU, SLOTS])
        idx = sb("idx", [P, 2, TU, SLOTS], U32)
        hdot = sb("hdot", [P, 2, GROUP])
        gel = sb("gel", [P, 2, GROUP])
        coef = sb("coef", [P, 2, GROUP])
        diag = sb("diag", [P, DIAGS, P])

        group_done = sem("group_done")
        bank_read = [sem(f"bank_read{b}") for b in range(BANKS)]
        w_landed = [sem(f"w_landed{b}") for b in range(2)]
        x_landed = sem("x_landed")
        small_landed = sem("small_landed")
        consts_made = sem("consts_made")
        pool_step = sem("pool_step")
        sbmask_made = sem("sbmask_made")
        dve_step = sem("dve_step")
        act_step = sem("act_step")
        conv_made = sem("conv_made")
        qkv_made = sem("qkv_made")
        gate_in = sem("gate_in")
        gate_exp = sem("gate_exp")
        g_made = sem("g_made")
        rows_made = sem("rows_made")
        squared = sem("squared")
        inverse_norm = sem("inverse_norm")
        qk_normed = sem("qk_normed")
        seg_made = sem("seg_made")
        kv_scaled = sem("kv_scaled")
        level_made = sem("level_made")
        inverse_made = sem("inverse_made")
        o_squared = sem("o_squared")
        state_made = sem("state_made")
        ws_done = sem("ws_done")
        ds_done = sem("ds_done")
        vnew_made = sem("vnew_made")
        o_gated = sem("o_gated")
        softplus_in = sem("softplus_in")
        softplus_ln = sem("softplus_ln")
        softplus_made = sem("softplus_made")
        att_in = sem("att_in")
        att_exp = sem("att_exp")
        att_made = sem("att_made")
        mmax_made = sem("mmax_made")
        mexp_made = sem("mexp_made")
        mprob_made = sem("mprob_made")
        stats_made = sem("stats_made")
        rstd_made = sem("rstd_made")
        cdiff_made = sem("cdiff_made")
        cexp_made = sem("cexp_made")
        routed = sem("routed")
        u_landed = [sem(f"u_landed{r}") for r in range(RING)]
        v_landed = [sem(f"v_landed{r}") for r in range(RING)]
        dot_made = sem("dot_made")
        gelu_made = sem("gelu_made")
        coef_made = sem("coef_made")
        diag_made = sem("diag_made")
        v_freed = [sem(f"v_freed{r}") for r in range(RING)]
        v_scaled = sem("v_scaled")
        acc_read = sem("acc_read")
        stored = sem("stored")

        xr = x.rearrange("a (t p) d -> p (a t) d", p=P)
        outr = out.rearrange("a (t p) d -> p (a t) d", p=P)
        u_rows = peer_u.rearrange("l e d -> (l e) d")
        v_rows = peer_v.rearrange("l e d -> (l e) d")

        def norm_index(kind, u):
            if kind == 0:
                return u if u < HALVES else 2 * u - HALVES + 1
            return 2 * u + HALVES if u < HALVES else 2 * HALVES * (DEPTH - 1) + u

        def bank(*name):
            return banks[:, PLAN[name] % BANKS, :]

        def sub(ap, n=SUB):
            return ap.rearrange("p (s c) -> p s c", s=n)

        block = ctx.enter_context(nc.Block())

        @block.sync
        def _(sp):
            with nc.allow_non_contiguous_dma(reason="small parameters, once"):
                for i, v in enumerate((ln_mix_g, ln_mix_b, ln_ffn_g, ln_ffn_b)):
                    sp.dma_start(NV[16 * i:16 * i + 16, :], v.rearrange("l (a c) -> (l a) c", c=256)).then_inc(small_landed, 16)
                sp.dma_start(UR[:, 0, 0:2 * DEPTH * P].rearrange("p (a c) -> p a c", c=P),
                             peer_keys.rearrange("l h n c -> n (l h) c")).then_inc(small_landed, 16)
                for i in range(4):
                    sp.dma_start(convw[:, :, i], gdn_conv[0, i, :].rearrange("(b p) -> p b", p=P)).then_inc(small_landed, 16)
                sp.dma_start(wba[:, :, :], gdn_w_in[0, :, QM0 - 16:QM0].rearrange("(k p) c -> p k c", p=P)).then_inc(small_landed, 16)
                sp.dma_start(onorm[:, :], gdn_onorm.rearrange("a p -> p a")).then_inc(small_landed, 16)
                sp.dma_start(dtb[:, :], gdn_dt_bias.to_broadcast([P, H])).then_inc(small_landed, 16)
                sp.dma_start(nexp[:, :], gdn_a_log.to_broadcast([P, H])).then_inc(small_landed, 16)

            def weights(*name):
                m = LOADS[name]
                if m >= 2:
                    full(sp, *USER[m - 2])
                dst = W[:, m % 2, :]
                what, a = name[0], name[1]
                if what == "mem":
                    src = mem.rearrange("a (t p) d -> p (a t) d", p=P)
                    dst = dst.rearrange("p (t d) -> p t d", t=NMEM // P)
                else:
                    if what == "kv":
                        src = mem_w_kv[a, :, WCOLS * name[2]:WCOLS * (name[2] + 1)]
                    elif what == "proj":
                        c = WCOLS * name[2]
                        if UNITS[a][0] == 0:
                            c += 16 if name[2] >= 12 else 0
                            src = gdn_w_in[0, :, c:c + WCOLS]
                        else:
                            src = sb_w_in[0, :, c:c + WCOLS]
                    elif what == "out":
                        src = w_out[UNITS[a][0], :, WCOLS * name[2]:WCOLS * (name[2] + 1)]
                        dst = W[:, m % 2, 0:KO * WCOLS]
                    else:
                        src = peer_w_q[UNITS[a][0], :, WCOLS * name[2]:WCOLS * (name[2] + 1)]
                    src = src.rearrange("(k p) c -> p k c", p=P)
                    dst = dst.rearrange("p (k c) -> p k c", c=WCOLS)
                sp.dma_start(dst, src).then_inc(w_landed[m % 2], 16)

            first = True
            for name in LOADS:
                weights(*name)
                if first:
                    sp.dma_start(X[:, :, :], xr).then_inc(x_landed, 16)
                    first = False
            for i, u in enumerate((len(UNITS) - 2, len(UNITS) - 1)):
                was_read(sp, "norm_b", 1, u, 3)
                sp.dma_start(outr[:, TU * i:TU * i + TU, :], X[:, TU * i:TU * i + TU, :]).then_inc(stored, 16)
            sp.wait_ge(stored, 32)

        @block.gpsimd
        def _(pool):
            steps = [0]

            def link(ins):
                steps[0] += 1
                ins.then_inc(pool_step, 1)
                pool.wait_ge(pool_step, steps[0])

            for m in (ident, tri_le, tri_gt, full_ge, lvl):
                value = 0.0 if m is lvl or m is ident else 1.0
                link(pool.memset(m[:], value))
            link(pool.memset(ones[:, :], 1.0))
            link(pool.memset(eps[:, 0:1], LN_EPS))
            link(pool.memset(eps[:, 1:2], RMS_EPS))

            def keep(ap, pattern, base, mult, op=ALU.is_ge, fill=0.0):
                link(pool.affine_select(out=ap, in_=ap, compare_op=op, fill=fill, base=base, pattern=pattern,
                                        channel_multiplier=mult))

            keep(ident[:, :], [[-1, P]], 0, 1, ALU.not_equal, 1.0)
            keep(tri_le[:, :], [[1, P]], 0, -1)
            keep(tri_le[:, CHUNK:P], [[0, CHUNK]], -CHUNK, 1)
            keep(tri_gt[:, :], [[-1, P]], 0, 1, ALU.is_gt)
            keep(tri_gt[:, 0:CHUNK], [[0, CHUNK]], CHUNK - 1, -1)
            keep(full_ge[:, :], [[-1, P]], 0, 1)
            for i, w in enumerate((1,) + LEVELS):
                v = lvl[:, i, :].rearrange("p (b h w) -> p b h w", h=2, w=w)[:, :, 1, :]
                link(pool.memset(v, 1.0))
                keep(v, [[-2 * w, P // (2 * w)], [0, w]], 0, 1)
                keep(v, [[2 * w, P // (2 * w)], [0, w]], w - 1, -1)
            link(pool.iota(iota16[:, :], [[1, 16]], base=0, channel_multiplier=0, allow_small_or_imprecise_dtypes=True))
            pool.memset(state[:, :, :], 0.0).then_inc(consts_made, 1)

            def gather(ring, rows, landed, u, k):
                n = u * SLOT_COUNT + k
                if n >= RING:
                    if ring is UR:
                        pool.wait_ge(dot_made, n - RING + 1)
                    else:
                        pool.wait_ge(v_freed[n % RING], n // RING)
                t, s = k // SLOTS, k % SLOTS
                pool.indirect_dma_start(ring[:, n % RING, :], None, rows,
                                        bass.IndirectOffsetOnAxis(idx[:, u % 2, t, s:s + 1], 0)
                                        ).then_inc(landed[n % RING], 16)

            for u in range(len(UNITS)):
                for k in range(STEPS):
                        if k < SLOT_COUNT:
                            if k % SLOTS == 0:
                                pool.wait_ge(routed, TU * u + k // SLOTS + 1)
                                if k == 0 and u == HALVES - 1:
                                    link(pool.memset(sbmask[:, :, :], 1.0))
                                    pool.affine_select(out=sbmask[:, :, :], in_=sbmask[:, :, :], compare_op=ALU.is_gt, fill=0.0,
                                                       base=0, pattern=[[-P, 2], [1, T]], channel_multiplier=-1
                                                       ).then_inc(sbmask_made, 1)
                            if u == 0 and k == 0:
                                was_read(pool, "keys", 0)
                            gather(UR, u_rows, u_landed, u, k)
                        if k >= GROUP:
                            gather(VR, v_rows, v_landed, u, k - GROUP)

        @block.tensor
        def _(pe):
            order = [0]

            def group(*name):
                n = PLAN[name]
                assert n == order[0], (name, n, order[0])
                order[0] += 1
                experts.before(*name)
                if n >= BANKS:
                    pe.wait_ge(bank_read[n % BANKS], n // BANKS)
                return banks[:, n % BANKS, :]

            def done(ins):
                ins.then_inc(group_done, 1)

            def weights(*name):
                m = LOADS[name]
                pe.wait_ge(w_landed[m % 2], 16 * (m // 2 + 1))
                return W[:, m % 2, :].rearrange("p (k c) -> p k c", c=WCOLS)

            def by_feature(ps, w, src, kt):
                for b in range(2):
                    for k in range(kt):
                        last = pe.matmul(sub(ps, 2)[:, b, :], w[:, k, b * P:b * P + P], src[:, k, :],
                                         start=(k == 0), stop=(k == kt - 1))
                done(last)

            def by_token(ps, w, src, kt):
                for t in range(TU):
                    for k in range(kt):
                        last = pe.matmul(sub(ps, 2)[:, t, :], src[:, k, t * P:t * P + P], w[:, k, :],
                                         start=(k == 0), stop=(k == kt - 1))
                done(last)

            def norm(kind, u, then=None):
                l = UNITS[u][0]
                for c in range(4 + 1):
                    if c < 4:
                        for v, name in enumerate(("norm_g", "norm_b")):
                            ps = group(name, kind, u, c)
                            for i in range(2):
                                r = 8 * (4 * kind + 2 * v + l) + 2 * c + i
                                last = pe.matmul(ps[:, 256 * i:256 * i + 256], ident[0:64, r:r + 1].to_broadcast([64, P]),
                                                 NV[:, :], start=True, stop=True)
                            done(last)
                    if then and c >= 1:
                        was_read(pe, "norm_b", kind, u, c - 1)
                        x_transposes(*then, 2 * c - 2)
                        x_transposes(*then, 2 * c - 1)
                if then:
                    x_turned(*then)

            def x_transposes(u, which, j):
                ps = sub(group("xT", u, which, j))
                for i in range(SUB):
                    k = SUB * (j // 2) + i
                    last = pe.transpose(ps[:, i, :], X[:, TU * UNITS[u][1] + j % 2, k * P:k * P + P], ident[:, :])
                done(last)

            def x_turned(u, which):
                for j in range(4, 8):
                    was_read(pe, "xT", u, which, j)

            def project(u):
                l = UNITS[u][0]
                if l % 2 == 0:
                    ps = group("ba", u)
                    for t in range(TU):
                        for k in range(KT):
                            last = pe.matmul(ps[:, 16 * t:16 * t + 16], xT[:, k, t * P:t * P + P], wba[:, k, :],
                                             start=(k == 0), stop=(k == KT - 1))
                    done(last)
                for w in range(NPROJ):
                    ps = group("proj", u, w)
                    tokens = l % 2 == 1 and 8 <= w < 12
                    (by_token if tokens else by_feature)(ps, weights("proj", u, w), xT, KT)
                    if l % 2 == 0:
                        beside_projection(u, w)

            def memory_kv(l):
                m = LOADS[("mem", l)]
                pe.wait_ge(w_landed[m % 2], 16 * (m // 2 + 1))
                rows = W[:, m % 2, :].rearrange("p (t d) -> p t d", t=2)
                for j in range(8):
                    ps = sub(group("memT", l, j))
                    for i in range(SUB):
                        last = pe.transpose(ps[:, i, :], rows[:, j // 4, ((j % 4) * SUB + i) * P:((j % 4) * SUB + i + 1) * P],
                                            ident[:, :])
                    done(last)
                for j in range(4, 8):
                    was_read(pe, "memT", l, j)
                for w in range(NKV):
                    ps = group("kv", l, w)
                    (by_feature if w < NKV // 2 else by_token)(ps, weights("kv", l, w), xT, KT)

            def beside_projection(u, w):
                f = UNITS[u][1]
                if 4 <= w < 8:
                    pe.wait_ge(squared, 4 * f + w - 3)
                    done(pe.matmul(group("l2", u, w - 4), ones[:, :], sq[w - 4], start=True, stop=True))
                if w == 8:
                    pe.wait_ge(g_made, u + 1)
                    ps = group("gcum", u)
                    for t in range(TU):
                        chunks = [tri_le[:, c:c + 1].to_broadcast([P, P]) for c in (CHUNK - 1, P - 1)]
                        for i, a in enumerate([tri_le[:, :], tri_gt[:, :]] + chunks):
                            last = pe.matmul(ps[:, 32 * t + 8 * i:32 * t + 8 * i + 8], a, g[:, t, :], start=True, stop=True)
                    done(last)
                if w == 10:
                    pe.wait_ge(rows_made, u + 1)
                    ps = group("rows", u)
                    for t in range(TU):
                        last = pe.transpose(ps[0:16, t * P:t * P + P], bg[:, t, :], ident[:, :])
                    done(last)

            def deltanet(u):
                for j in range(HQ):
                    delta_heads(u, j)

            def delta_heads(u, j):
                f = UNITS[u][1]
                gj = HQ * f + j
                if j == 0:
                    pe.wait_ge(qk_normed, 4 * f + 4)
                    pe.wait_ge(qkv_made, 8 * f + 8)
                    was_read(pe, "rows", u)
                ps = sub(group("ktok", u, j))
                for t in range(TU):
                    last = pe.transpose(ps[:, t, :], qT[:, HQ + j, t * P:t * P + P], ident[:, :])
                done(last)
                ps = sub(group("vtok", u, j))
                for i in range(SUB):
                    last = pe.transpose(ps[:, i, :], vT[:, 2 * j + i // 2, (i % 2) * P:(i % 2) * P + P], ident[:, :])
                done(last)
                for s, base in (("bcb", 0), ("bcg", H)):
                    ps = sub(group(s, u, j), 2)
                    for h in range(2):
                        r = base + 2 * j + h
                        last = pe.matmul(ps[:, h, :], ident[0:16, r:r + 1].to_broadcast([16, P]), bgT, start=True, stop=True)
                    done(last)
                pe.wait_ge(seg_made, gj + 1)
                ps = sub(group("seg", u, j))
                for i in range(SUB):
                    last = pe.matmul(ps[:, i, :], sub(seg_g)[:, i, :], tri_le[:, :], start=True, stop=True)
                done(last)
                ps = sub(group("kq", u, j))
                for t in range(TU):
                    last = pe.matmul(ps[:, t, :], qT[:, HQ + j, t * P:t * P + P], qT[:, j, t * P:t * P + P],
                                     start=True, stop=True)
                done(last)
                was_read(pe, "bcb", u, j)
                ps = sub(group("kk", u, j))
                for i in range(SUB):
                    t = i % 2
                    last = pe.matmul(ps[:, i, :], qT[:, HQ + j, t * P:t * P + P], sub(kbT)[:, i, :], start=True, stop=True)
                done(last)
                pe.wait_ge(inverse_made, gj + 1)
                ps = sub(group("T0", u, j))
                for i in range(SUB):
                    last = pe.transpose(ps[:, i, :], TT[:, i // 2, 1, i % 2, :], ident[:, :])
                done(last)
                was_read(pe, "T0", u, j)
                for n in range(len(LEVELS)):
                    pe.wait_ge(level_made, len(LEVELS) * gj + n + 1)
                    L = levels[(n + 1) % 2]
                    for h in range(2):
                        if n:
                            was_read(pe, "TPU", u, j, n - 1, h)
                        ps = sub(group("P", u, j, n, h))
                        for t in range(TU):
                            last = pe.matmul(ps[:, t, :], sub(L)[:, 2 * h + t, :], TT[:, h, 0, t, :], start=True, stop=True)
                        done(last)
                    for h in range(2):
                        was_read(pe, "P", u, j, n, h)
                        ps = sub(group("TPU", u, j, n, h))
                        for t in range(TU):
                            pe.matmul(ps[:, t, :], TT[:, h, 1, t, :], sub(Pm)[:, 2 * h + t, :], start=True, stop=True)
                        for t in range(TU):
                            last = pe.matmul(ps[:, TU + t, :], sub(Pm)[:, 2 * h + t, :], TT[:, h, 1, t, :], start=True, stop=True)
                        done(last)
                for h in range(2):
                    was_read(pe, "TPU", u, j, len(LEVELS) - 1, h)
                pe.wait_ge(kv_scaled, gj + 1)
                was_read(pe, "vtok", u, j)
                ps = sub(group("w", u, j))
                for i in range(SUB):
                    last = pe.matmul(ps[:, i, :], sub(Kp)[:, i, :], TT[:, i // 2, 1, i % 2, :], start=True, stop=True)
                done(last)
                ps = sub(group("u", u, j))
                for i in range(SUB):
                    last = pe.matmul(ps[:, i, :], TT[:, i // 2, 1, i % 2, :], sub(Vp)[:, i, :], start=True, stop=True)
                done(last)
                was_read(pe, "ktok", u, j)
                was_read(pe, "bcg", u, j)
                was_read(pe, "kq", u, j)
                was_read(pe, "w", u, j)
                ps_o = sub(group("o", u, j), 2)
                scr = scratch_banks(u, j)
                qg = sub(qgT, 2)
                for c in range(2 * TU):
                    t, lo = c // 2, CHUNK * (c % 2)
                    n = 4 * gj + c
                    cols = slice(t * P + lo, t * P + lo + CHUNK)
                    if c:
                        pe.wait_ge(state_made, n)
                    for h in range(2):
                        last = pe.matmul(scr[0][lo:lo + CHUNK, P * h:P * h + P], sub(wT)[:, 2 * h + t, lo:lo + CHUNK],
                                         state[:, 2 * j + h, :], start=True, stop=True)
                    last.then_inc(ws_done, 1)
                    for h in range(2):
                        pe.matmul(ps_o[:, h, cols], state[:, 2 * j + h, :], qg[:, h, cols],
                                  start=(c == 0 and h == 0), stop=False, skip_group_check=True)
                    pe.wait_ge(vnew_made, n + 1)
                    for h in range(2):
                        last = pe.matmul(scr[1][:, P * h:P * h + P], sub(Kd)[lo:lo + CHUNK, 2 * h + t, :],
                                         vnew[lo:lo + CHUNK, h, :], start=True, stop=True)
                    last.then_inc(ds_done, 1)
                    for h in range(2):
                        last = pe.matmul(ps_o[:, h, cols], vnew[lo:lo + CHUNK, h, :], sub(aqkT)[lo:lo + CHUNK, 2 * h + t, lo:lo + CHUNK],
                                         start=False, stop=(c == 2 * TU - 1 and h == 1), skip_group_check=True)
                done(last)
                pe.wait_ge(state_made, 4 * gj + 4)
                pe.wait_ge(o_squared, gj + 1)
                done(pe.matmul(group("oss", u, j), ones[:, :], Pm, start=True, stop=True))

            def scratch_banks(u, j):
                n = PLAN[("o", u, j)]
                was_read(pe, "u", u, j)
                for i in (1, 2):
                    pe.wait_ge(bank_read[(n + i) % BANKS], (n + i) // BANKS)
                return [banks[:, (n + i) % BANKS, :] for i in (1, 2)]

            def stick_breaking(u):
                f = UNITS[u][1]
                nb = f + 1

                def scores(h):
                    for b in range(nb):
                        ps = sub(group("z", u, h, b), 2)
                        if h == 0 and b == 0:
                            for w in range(10, 14):
                                was_read(pe, "proj", u, w)
                        for i in range(2):
                            s = (2 * b + i) * P
                            last = pe.matmul(ps[:, i, :], sbkT[:, h, s:s + P], qT[:, h, :], start=True, stop=True)
                        done(last)

                def later(h):
                    pe.wait_ge(softplus_made, H * f + h + 1)
                    for b in range(nb):
                        ps = sub(group("later", u, h, b), 2)
                        for i in range(2):
                            for s in range(2 * b + i, 2 * nb):
                                a = full_ge if s == 2 * b + i else ones
                                last = pe.matmul(ps[:, i, :], a[:, :], sb_sp[h % 2][:, s, :],
                                                 start=(s == 2 * b + i), stop=(s == 2 * nb - 1))
                        done(last)

                scores(0)
                scores(1)
                later(0)
                for h in range(H):
                    if h + 1 < H:
                        later(h + 1)
                    pe.wait_ge(att_made, H * f + h + 1)
                    ps = group("sbo", u, h)
                    for s in range(2 * nb):
                        last = pe.matmul(ps[:, 0:T], sbv[:, s, h * P:h * P + P], sb_z[h % 2][:, s, :],
                                         start=(s == 0), stop=(s == 2 * nb - 1))
                    done(last)
                    if h + 2 < H:
                        scores(h + 2)

            def memory_attention(u):
                def scores(m):
                    ps = sub(group("ms", u, m), 2)
                    for t in range(TU):
                        last = pe.matmul(ps[:, t, :], qmT[:, m, t * P:t * P + P], KM[:, m, :], start=True, stop=True)
                    done(last)

                def turn(m):
                    pe.wait_ge(mprob_made, MH * u + m + 1)
                    ps = sub(group("mpT", u, m))
                    for mm in range(2):
                        for t in range(TU):
                            last = pe.transpose(ps[:, 2 * mm + t, :], mem_p[m % 2][:, t, mm * P:mm * P + P], ident[:, :])
                    done(last)

                scores(0)
                scores(1)
                turn(0)
                for m in range(MH):
                    if m + 2 < MH:
                        scores(m + 2)
                    if m + 1 < MH:
                        turn(m + 1)
                    was_read(pe, "mpT", u, m)
                    ps = group("mo", u, m)
                    for mm in range(2):
                        last = pe.matmul(ps[:, 0:T], VM[:, mm, m * P:m * P + P], mem_pT[m % 2][:, mm, :], start=(mm == 0), stop=(mm == 1))
                    done(last)

            def out_projection(u):
                for w in range(NOUT):
                    ps = group("out", u, w)
                    if w == 0:
                        was_read(pe, "mo", u, MH - 1)
                        f = UNITS[u][1]
                        if UNITS[u][0] % 2 == 0:
                            pe.wait_ge(o_gated, HQ * (f + 1))
                        else:
                            was_read(pe, "sbo", u, H - 1)
                    by_token(ps, weights("out", u, w), mixT, KO)

            def queries(u):
                for w in range(NQRY):
                    by_feature(group("qry", u, w), weights("qry", u, w), xT, KT)
                for t in range(TU):
                    for i in range(2):
                        ps = sub(group("score", u, t, i))
                        if t == 0 and i == 0:
                            for w in range(NQRY):
                                was_read(pe, "qry", u, w)
                        for k in range(SUB):
                            b = SUB * i + k
                            last = pe.matmul(ps[:, k, :], qryT[:, b, t * P:t * P + P], keysT[:, 2 * UNITS[u][0] + b % 2, :],
                                             start=True, stop=True)
                        done(last)

            def expert_slot(u, k):
                n, i, D_ = u * SLOT_COUNT + k, k % GROUP, ON_DVE[u]
                if i < D_ - 1:
                    return
                if i == D_ - 1:
                    pe.wait_ge(v_freed[(n - 1) % RING], (n - 1) // RING + 1)
                    a = ident[:, :]
                else:
                    d = DIAG_SLOTS.index(n)
                    pe.wait_ge(diag_made, d + 1)
                    pe.wait_ge(v_landed[n % RING], 16 * (n // RING + 1))
                    a = diag[:, d % DIAGS, :]
                first = k % SLOTS == max(D_ - 1, 0)
                if first and n >= SLOTS:
                    pe.wait_ge(acc_read, n // SLOTS)
                for c in range(4):
                    last = pe.matmul(acc[:, c, :], a, VR[:, n % RING, 512 * c:512 * c + 512],
                                     start=first, stop=(k % SLOTS == SLOTS - 1))
                last.then_inc(v_freed[n % RING], 1)

            def expert_step(u, k):
                if k >= GROUP:
                    expert_slot(u, k - GROUP)

            experts = Experts(expert_step)
            pe.wait_ge(consts_made, 1)
            pe.wait_ge(small_landed, 16 * 13)
            ps = sub(group("keys", 0))
            for i in range(2 * DEPTH):
                last = pe.transpose(ps[:, i, :], UR[:, 0, i * P:i * P + P], ident[:, :])
            done(last)

            def mix(u):
                l, f = UNITS[u]
                if f == 0:
                    memory_kv(l)
                if u >= HALVES:
                    norm(1, u - HALVES, then=(u, 0))
                else:
                    pe.wait_ge(x_landed, 16)
                    for j in range(8):
                        x_transposes(u, 0, j)
                    x_turned(u, 0)
                project(u)
                (deltanet if l % 2 == 0 else stick_breaking)(u)
                memory_attention(u)
                out_projection(u)
                norm(0, u, then=(u, 1))
                queries(u)

            for u in range(len(UNITS)):
                mix(u)
                if u:
                    experts.rest(u - 1)
            norm(1, len(UNITS) - 2)
            experts.rest(len(UNITS) - 1)
            norm(1, len(UNITS) - 1)

        @block.scalar
        def _(act):
            counts = {}

            def experts_full(eng, *name):
                full(eng, *name, experts=experts)

            def experts_read(eng, *name):
                was_read(eng, *name, experts=experts)

            def link(ins, s=None):
                s = act_step if s is None else s
                counts[s.name] = counts.get(s.name, 0) + 1
                ins.then_inc(s, 1)
                act.wait_ge(s, counts[s.name])

            def read(ins, *name):
                ins.then_inc(bank_read[PLAN[name] % BANKS], 1)

            def copy_out(dst, *name, cols=512, func=ACT.Copy, scale=1.0, shape=None, rows=P):
                experts_full(act, *name)
                src = bank(*name)[0:rows, 0:cols]
                if shape:
                    src = sub(src, shape)
                read(act.activation(dst, src, func, scale=scale), *name)

            def x_copies(u, which):
                if which == 0 and u:
                    act.wait_ge(routed, TU * u)
                for j in range(8):
                    k, t = SUB * (j // 2), j % 2
                    copy_out(xT[:, k:k + SUB, t * P:t * P + P], "xT", u, which, j, shape=SUB)

            def memory_kv(l, u):
                if u:
                    act.wait_ge(routed, TU * u)
                for j in range(8):
                    k, t = SUB * (j % 4), j // 4
                    copy_out(xT[:, k:k + SUB, t * P:t * P + P], "memT", l, j, shape=SUB)
                for w in range(NKV):
                    if w < NKV // 2:
                        copy_out(KM[:, 2 * w:2 * w + 2, :], "kv", l, w, shape=2)
                    else:
                        c = WCOLS * (w - NKV // 2)
                        copy_out(VM[:, :, c:c + WCOLS], "kv", l, w, shape=2)

            def project(u):
                l, f = UNITS[u]
                if l % 2 == 1:
                    for w in range(NPROJ):
                        if w < 4:
                            copy_out(qT[:, 2 * w:2 * w + 2, :], "proj", u, w, scale=SCALE, shape=2)
                        elif w < 8:
                            copy_out(sbkT[:, 2 * w - 8:2 * w - 6, f * T:f * T + T], "proj", u, w, shape=2)
                        elif w < 12:
                            c = WCOLS * (w - 8)
                            copy_out(sbv[:, TU * f:TU * f + TU, c:c + WCOLS], "proj", u, w, shape=2)
                        else:
                            copy_out(qmT[:, 2 * w - 24:2 * w - 22, :], "proj", u, w, shape=2)
                    return

                def silu(w):
                    act.wait_ge(conv_made, 8 * f + w + 1)
                    dst = qT[:, 2 * w:2 * w + 2, :] if w < 4 else vT[:, 2 * w - 8:2 * w - 6, :]
                    act.activation(dst, convout[:, w % 2, :, :], ACT.Silu).then_inc(qkv_made, 1)

                for w in range(NPROJ):
                    if 5 <= w < 9:
                        inverse(u, w - 5)
                    if w == 9:
                        experts_full(act, "gcum", u)
                        read(act.activation(eg[:, :, :], sub(bank("gcum", u)[:, 0:64], 2), ACT.Exp), "gcum", u)
                    if w == 11:
                        copy_out(bgT, "rows", u, cols=T, rows=16)
                    if w < 8:
                        if w >= 2:
                            act.wait_ge(conv_made, 8 * f + w - 1)
                        copy_out(convin[:, w % 2, :, 3:3 + T], "proj", u, w, shape=2)
                        if w == 1:
                            gates(u)
                    elif w < 12:
                        copy_out(zT[:, 2 * w - 16:2 * w - 14, :], "proj", u, w, func=ACT.Silu, shape=2)
                    else:
                        copy_out(qmT[:, 2 * w - 24:2 * w - 22, :], "proj", u, w, shape=2)
                    if 1 <= w < 9:
                        silu(w - 1)
                        if w < 5:
                            act.wait_ge(qkv_made, 8 * f + w)
                            act.activation(sq[w - 1], R[:, 512 * w - 512:512 * w], ACT.Square).then_inc(squared, 1)

            def gates(u):
                experts.before("ba", u)
                act.wait_ge(gate_in, u + 1)
                link(act.activation(ge[:, :, :], gx[:, :, :], ACT.Exp))
                act.activation(gl[:, :, :], ge[:, :, 0:H], ACT.Ln, bias=1.0).then_inc(gate_exp, 1)

            def deltanet(u):
                for j in range(HQ):
                    delta_heads(u, j)

            def inverse(u, i):
                f = UNITS[u][1]
                experts_full(act, "l2", u, i)
                if i >= 2:
                    act.wait_ge(qk_normed, 4 * f + i - 1)
                ins = act.activation(rs[i % 2], bank("l2", u, i), ACT.Ln, bias=eps[:, 1:2])
                read(ins, "l2", u, i)
                experts_read(act, "l2", u, i)
                act.activation(rs[i % 2], rs[i % 2], ACT.Exp, scale=-0.5).then_inc(inverse_norm, 1)

            def delta_heads(u, j):
                f = UNITS[u][1]
                gj = HQ * f + j
                if j:
                    act.wait_ge(o_gated, gj)
                for i in range(SUB):
                    h, t = 2 * j + i // 2, i % 2
                    ins = act.activation(sub(seg_g)[:, i, :], tri_gt[:, :], ACT.Copy, scale=g[:, t, h:h + 1])
                ins.then_inc(seg_made, 1)
                experts_full(act, "vtok", u, j)
                for i in range(SUB):
                    h, t = 2 * j + i // 2, i % 2
                    ins = act.activation(sub(Vp)[:, i, :], sub(bank("vtok", u, j))[:, i, :], ACT.Copy, scale=bg[:, t, h:h + 1])
                read(ins, "vtok", u, j)
                experts_full(act, "seg", u, j)
                read(act.activation(decay, bank("seg", u, j), ACT.Exp), "seg", u, j)
                experts_full(act, "T0", u, j)
                read(act.activation(TT[:, :, 0, :, :], bank("T0", u, j).rearrange("p (h t c) -> p h t c", h=2, t=TU), ACT.Copy),
                     "T0", u, j)
                for n in range(len(LEVELS)):
                    for h in range(2):
                        copy_out(Pm[:, 2 * P * h:2 * P * h + 2 * P], "P", u, j, n, h, cols=2 * P)
                copy_out(wT, "w", u, j)
                copy_out(u_sb, "u", u, j)
                experts_full(act, "o", u, j)
                act.activation(Pm, bank("o", u, j), ACT.Square).then_inc(o_squared, 1)
                read(act.activation(o_sb, bank("o", u, j), ACT.Copy), "o", u, j)
                experts_full(act, "oss", u, j)
                read(act.activation(Lm, bank("oss", u, j), ACT.Ln, scale=1.0 / P, bias=eps[:, 1:2]), "oss", u, j)
                experts_read(act, "oss", u, j)
                act.activation(Lm, Lm, ACT.Exp, scale=-0.5).then_inc(inverse_norm, 1)

            def stick_breaking(u):
                f = UNITS[u][1]
                nb = f + 1

                def scores(h):
                    for b in range(nb):
                        copy_out(sb_z[h % 2][:, 2 * b:2 * b + 2, :], "z", u, h, b, shape=2)
                    act.wait_ge(softplus_in, H * f + h + 1)
                    e = sb_sp[h % 2][:, 0:2 * nb, :]
                    link(act.activation(e, e, ACT.Exp))
                    act.activation(e, e, ACT.Ln, bias=1.0).then_inc(softplus_ln, 1)

                scores(0)
                scores(1)
                for h in range(H):
                    experts.before("later", u, h, nb - 1)
                    act.wait_ge(att_in, H * f + h + 1)
                    a = sb_z[h % 2][:, 0:2 * nb, :]
                    act.activation(a, a, ACT.Exp).then_inc(att_exp, 1)
                    copy_out(mixT[:, h, :], "sbo", u, h, cols=T)
                    if h + 2 < H:
                        scores(h + 2)

            def memory_attention(u):
                def exponentials(m):
                    experts_full(act, "ms", u, m)
                    act.wait_ge(mmax_made, MH * u + m + 1)
                    ps = sub(bank("ms", u, m), 2)
                    for t in range(TU):
                        ins = act.activation(mem_p[m % 2][:, t, :], ps[:, t, :], ACT.Exp, scale=SCALE, bias=nmax[:, m % 2, t:t + 1],
                                             accum_out=msum[:, m % 2, t:t + 1])
                        if t == 0:
                            link(ins)
                    read(ins, "ms", u, m)

                def turned(m):
                    copy_out(mem_pT[m % 2][:, :, :], "mpT", u, m, shape=2)

                exponentials(0)
                exponentials(1)
                turned(0)
                for m in range(MH):
                    if m + 2 < MH:
                        exponentials(m + 2)
                    if m + 1 < MH:
                        turned(m + 1)
                    copy_out(mixT[:, H + m, :], "mo", u, m, cols=T)

            def norm(kind, u):
                if kind == 0:
                    experts.before("out", u, NOUT - 1)
                act.wait_ge(stats_made, norm_index(kind, u) + 1)
                link(act.activation(rstd[:, :, 0], mv[:, :, 1], ACT.Ln, bias=eps[:, 0:1]))
                act.activation(rstd[:, :, 1], rstd[:, :, 0], ACT.Exp, scale=-0.5).then_inc(rstd_made, 1)

            def queries(u):
                for w in range(NQRY):
                    copy_out(qryT[:, 2 * w:2 * w + 2, :], "qry", u, w, shape=2)
                for t in range(TU):
                    if t:
                        act.wait_ge(routed, TU * u + t)
                    for i in range(2):
                        copy_out(s_sb[:, SUB * i:SUB * i + SUB, :], "score", u, t, i, shape=SUB)
                    act.wait_ge(cdiff_made, TU * u + t + 1)
                    act.activation(cd[:, :, :], cd[:, :, :], ACT.Exp).then_inc(cexp_made, 1)

            def expert_gelu(u, kk):
                n = u * TU * SLOTS // GROUP + kk
                act.wait_ge(dot_made, GROUP * (n + 1))
                if n >= 2:
                    act.wait_ge(coef_made, n - 1)
                act.activation(gel[:, n % 2, :], hdot[:, n % 2, :], ACT.Gelu).then_inc(gelu_made, 1)

            def expert_diag(u, k):
                n = u * SLOT_COUNT + k
                if k % GROUP < ON_DVE[u]:
                    return
                d = DIAG_SLOTS.index(n)
                if k % GROUP == ON_DVE[u]:
                    act.wait_ge(coef_made, n // GROUP + 1)
                if d >= DIAGS:
                    m = DIAG_SLOTS[d - DIAGS]
                    act.wait_ge(v_freed[m % RING], m // RING + 1)
                act.activation(diag[:, d % DIAGS, :], ident[:, :], ACT.Copy,
                               scale=coef[:, (n // GROUP) % 2, k % GROUP:k % GROUP + 1]).then_inc(diag_made, 1)

            def expert_step(u, k):
                if k >= GROUP:
                    expert_diag(u, k - GROUP)
                if k % GROUP == GROUP - 1 and k < SLOT_COUNT:
                    expert_gelu(u, k // GROUP)

            experts = Experts(expert_step)
            act.wait_ge(consts_made, 1)
            act.wait_ge(small_landed, 16 * 13)
            copy_out(keysT[:, :, :], "keys", 0, shape=4)
            link(act.activation(nexp[:, :], nexp[:, :], ACT.Exp))

            def mix(u):
                l, f = UNITS[u]
                if f == 0:
                    memory_kv(l, u)
                if u >= HALVES:
                    norm(1, u - HALVES)
                x_copies(u, 0)
                project(u)
                (deltanet if l % 2 == 0 else stick_breaking)(u)
                memory_attention(u)
                norm(0, u)
                x_copies(u, 1)
                queries(u)

            for u in range(len(UNITS)):
                mix(u)
                if u:
                    experts.rest(u - 1)
            norm(1, len(UNITS) - 2)
            experts.rest(len(UNITS) - 1)
            norm(1, len(UNITS) - 1)

        @block.vector
        def _(dve):
            counts = {}

            def experts_full(eng, *name):
                full(eng, *name, experts=experts)

            def experts_read(eng, *name):
                was_read(eng, *name, experts=experts)

            def link(ins, s=None):
                s = dve_step if s is None else s
                counts[s.name] = counts.get(s.name, 0) + 1
                ins.then_inc(s, 1)
                dve.wait_ge(s, counts[s.name])

            def read(ins, *name):
                ins.then_inc(bank_read[PLAN[name] % BANKS], 1)
                experts_read(dve, *name)

            def project(u):
                l, f = UNITS[u]
                if l % 2 == 1:
                    return
                gates(u)
                for w in range(8):
                    if w == 2:
                        decays(u)
                    if 5 <= w:
                        normalise(u, w - 5)
                    r = w % 2
                    if w >= 2:
                        dve.wait_ge(qkv_made, 8 * f + w - 1)
                    if f == 0:
                        link(dve.memset(convin[:, r, :, 0:3], 0.0))
                    else:
                        link(dve.tensor_copy(convin[:, r, :, 0:3], hist[:, 2 * w:2 * w + 2, :]))
                    experts_read(dve, "proj", u, w)
                    link(dve.tensor_copy(hist[:, 2 * w:2 * w + 2, :], convin[:, r, :, T:T + 3]))
                    for i in range(4):
                        for b in range(2):
                            c, o = convw[:, 2 * w + b, i:i + 1], convout[:, r, b, :]
                            src = convin[:, r, b, i:i + T]
                            if i == 0:
                                ins = dve.tensor_scalar(o, src, c, None, ALU.mult)
                            else:
                                ins = dve.scalar_tensor_tensor(out=o, in0=src, scalar=c, in1=o, op0=ALU.mult, op1=ALU.add)
                            if i == 3 and b == 1:
                                link(ins, conv_made)
                            elif b == 1:
                                link(ins)
                normalise(u, 3)
                experts_read(dve, "gcum", u)
                link(dve.tensor_tensor(bexpg[:, :, :], bg[:, :, 0:H], eg[:, :, 0:H], ALU.mult))
                link(dve.tensor_copy(bg[:, :, H:2 * H], eg[:, :, 0:H]), rows_made)

            def gates(u):
                experts_full(dve, "ba", u)
                ps = sub(bank("ba", u)[:, 0:32], 2)
                link(dve.tensor_tensor(ga[:, :, :], ps[:, :, H:2 * H], dtb[:, None, :].to_broadcast([P, TU, H]), ALU.add))
                read(dve.tensor_scalar(gx[:, :, H:2 * H], ps[:, :, 0:H], -1.0, 80.0, ALU.mult, ALU.min), "ba", u)
                link(dve.scalar_tensor_tensor(out=gx[:, :, 0:H], in0=ga[:, :, :], scalar=-1.0, in1=ga[:, :, :],
                                              op0=ALU.mult, op1=ALU.min), gate_in)

            def decays(u):
                dve.wait_ge(gate_exp, u + 1)
                link(dve.scalar_tensor_tensor(out=gl[:, :, :], in0=ga[:, :, :], scalar=0.0, in1=gl[:, :, :],
                                              op0=ALU.max, op1=ALU.add))
                link(dve.tensor_scalar(bg[:, :, 0:H], ge[:, :, H:2 * H], 1.0, None, ALU.add))
                link(dve.reciprocal(bg[:, :, 0:H], bg[:, :, 0:H]))
                link(dve.scalar_tensor_tensor(out=g[:, :, :], in0=gl[:, :, :], scalar=-1.0,
                                              in1=nexp[:, None, :].to_broadcast([P, TU, H]), op0=ALU.mult, op1=ALU.mult), g_made)

            def normalise(u, i):
                f = UNITS[u][1]
                experts.before("l2", u, i)
                dve.wait_ge(inverse_norm, (4 + HQ) * f + i + 1)
                a = R[:, 512 * i:512 * i + 512]
                link(dve.scalar_tensor_tensor(out=a, in0=a, scalar=SCALE if i < 2 else 1.0, in1=rs[i % 2],
                                              op0=ALU.mult, op1=ALU.mult), qk_normed)

            def deltanet(u):
                for j in range(HQ):
                    delta_heads(u, j)

            def delta_heads(u, j):
                f = UNITS[u][1]
                gj = HQ * f + j
                experts_full(dve, "ktok", u, j)
                ps = sub(bank("ktok", u, j))
                for i in range(SUB):
                    h, t = 2 * j + i // 2, i % 2
                    ins = dve.tensor_scalar(sub(Kp)[:, i, :], ps[:, t, :], bexpg[:, t, h:h + 1], None, ALU.mult)
                ins.then_inc(kv_scaled, 1)
                for i in range(SUB):
                    h, t = 2 * j + i // 2, i % 2
                    ins = dve.tensor_scalar(sub(Kd)[:, i, :], ps[:, t, :], eg[:, t, H + h:H + h + 1], None, ALU.mult)
                read(ins, "ktok", u, j)
                experts_full(dve, "bcb", u, j)
                k2 = qT[:, HQ + j:HQ + j + 1, :].to_broadcast([P, 2, T])
                q2 = qT[:, j:j + 1, :].to_broadcast([P, 2, T])
                read(dve.tensor_tensor(sub(kbT, 2), k2, sub(bank("bcb", u, j), 2), ALU.mult), "bcb", u, j)
                experts_full(dve, "bcg", u, j)
                read(dve.tensor_tensor(sub(qgT, 2), q2, sub(bank("bcg", u, j), 2), ALU.mult), "bcg", u, j)
                experts_read(dve, "seg", u, j)
                four = [P, SUB, P]
                link(dve.tensor_tensor(sub(decay), sub(decay), tri_le[:, None, :].to_broadcast(four), ALU.mult))
                experts_full(dve, "kq", u, j)
                for h in range(2):
                    ins = dve.tensor_tensor(sub(aqkT)[:, 2 * h:2 * h + 2, :], sub(bank("kq", u, j))[:, 0:2, :],
                                            sub(decay)[:, 2 * h:2 * h + 2, :], ALU.mult)
                read(ins, "kq", u, j)
                experts_full(dve, "kk", u, j)
                read(dve.tensor_tensor(MT, bank("kk", u, j), decay, ALU.mult), "kk", u, j)
                link(dve.tensor_tensor(sub(Lm), sub(MT), lvl[:, 0:1, :].to_broadcast(four), ALU.mult))
                quarters = [P, 2, TU, P]
                link(dve.tensor_tensor(TT[:, :, 1, :, :], ident[:, None, None, :].to_broadcast(quarters),
                                       Lm.rearrange("p (h t c) -> p h t c", h=2, t=TU), ALU.subtract), inverse_made)

                def level(n):
                    if n < len(LEVELS):
                        link(dve.tensor_tensor(sub(levels[(n + 1) % 2]), sub(MT), lvl[:, n + 1:n + 2, :].to_broadcast(four), ALU.mult), level_made)

                level(0)
                level(1)
                for n in range(len(LEVELS)):
                    for h in range(2):
                        experts_full(dve, "TPU", u, j, n, h)
                        a = R[:, 7168 + 512 * h:7680 + 512 * h]
                        read(dve.tensor_tensor(a, a, bank("TPU", u, j, n, h), ALU.subtract), "TPU", u, j, n, h)
                    level(n + 2)
                experts_read(dve, "u", u, j)
                scr = [banks[:, (PLAN[("o", u, j)] + i) % BANKS, :] for i in (1, 2)]
                experts.before("o", u, j)
                for c in range(2 * TU):
                    t, lo = c // 2, CHUNK * (c % 2)
                    n = 4 * gj + c
                    dve.wait_ge(ws_done, n + 1)
                    us = u_sb.rearrange("p (h t v) -> p h t v", h=2, t=TU)[lo:lo + CHUNK, :, t, :]
                    link(dve.tensor_tensor(vnew[lo:lo + CHUNK, :, :], us, sub(scr[0][:, 0:2 * P], 2)[lo:lo + CHUNK], ALU.subtract), vnew_made)
                    dve.wait_ge(ds_done, n + 1)
                    for h in range(2):
                        s = state[:, 2 * j + h, :]
                        x0 = 16 + H * (c % 2) + 2 * j + h
                        ins = dve.scalar_tensor_tensor(out=s, in0=s, scalar=eg[:, t, x0:x0 + 1], in1=scr[1][:, P * h:P * h + P],
                                                       op0=ALU.mult, op1=ALU.add)
                    link(ins, state_made)
                experts.before("oss", u, j)
                dve.wait_ge(inverse_norm, (4 + HQ) * f + 4 + j + 1)
                experts_read(dve, "o", u, j)
                link(dve.scalar_tensor_tensor(out=o_sb, in0=o_sb, scalar=onorm[:, 0:1], in1=Lm, op0=ALU.mult, op1=ALU.mult))
                link(dve.tensor_tensor(MIX[:, 2 * j * T:(2 * j + 2) * T], o_sb, R[:, 5120 + 2 * j * T:5120 + (2 * j + 2) * T], ALU.mult), o_gated)

            def stick_breaking(u):
                f = UNITS[u][1]
                nb = f + 1
                dve.wait_ge(sbmask_made, 1)
                n = 512 * nb

                def softplus(h):
                    z, e = XT[:, 1024 * (h % 2):1024 * (h % 2) + n], XT[:, 2048 + 1024 * (h % 2):2048 + 1024 * (h % 2) + n]
                    for b in range(nb):
                        experts_read(dve, "z", u, h, b)
                    link(dve.scalar_tensor_tensor(out=e, in0=z, scalar=-1.0, in1=z, op0=ALU.mult, op1=ALU.min), softplus_in)
                    dve.wait_ge(softplus_ln, H * f + h + 1)
                    link(dve.scalar_tensor_tensor(out=e, in0=z, scalar=0.0, in1=e, op0=ALU.max, op1=ALU.add))
                    m = sb_sp[h % 2][:, 2 * nb - 2:2 * nb, :]
                    link(dve.tensor_tensor(m, m, sbmask[:, :, :], ALU.mult), softplus_made)

                def subtract_later(h):
                    for b in range(nb):
                        experts_full(dve, "later", u, h, b)
                        a = sb_z[h % 2][:, 2 * b:2 * b + 2, :]
                        read(dve.tensor_tensor(a, a, sub(bank("later", u, h, b), 2), ALU.subtract), "later", u, h, b)

                softplus(0)
                softplus(1)
                subtract_later(0)
                for h in range(H):
                    m = sb_z[h % 2][:, 2 * nb - 2:2 * nb, :]
                    link(dve.tensor_tensor(m, m, sbmask[:, :, :], ALU.mult), att_in)
                    if h + 1 < H:
                        subtract_later(h + 1)
                    dve.wait_ge(att_exp, H * f + h + 1)
                    link(dve.tensor_tensor(m, m, sbmask[:, :, :], ALU.mult), att_made)
                    if h + 2 < H:
                        softplus(h + 2)

            def memory_attention(u):
                def maxima(m):
                    experts_full(dve, "ms", u, m)
                    link(dve.tensor_reduce(nmax[:, m % 2, :], sub(bank("ms", u, m), 2), AX_X, ALU.max))
                    link(dve.tensor_scalar(nmax[:, m % 2, :], nmax[:, m % 2, :], -SCALE, None, ALU.mult), mmax_made)

                def probabilities(m):
                    experts_read(dve, "ms", u, m)
                    link(dve.reciprocal(msum[:, m % 2, :], msum[:, m % 2, :]))
                    for t in range(TU):
                        ins = dve.tensor_scalar(mem_p[m % 2][:, t, :], mem_p[m % 2][:, t, :], msum[:, m % 2, t:t + 1], None, ALU.mult)
                    link(ins, mprob_made)

                maxima(0)
                for m in range(MH):
                    if m + 1 < MH:
                        maxima(m + 1)
                    probabilities(m)

            def out_projection(u):
                t0 = TU * UNITS[u][1]
                for w in range(NOUT):
                    experts_full(dve, "out", u, w)
                    a = X[:, t0:t0 + TU, WCOLS * w:WCOLS * (w + 1)]
                    read(dve.scalar_tensor_tensor(out=a, in0=a, scalar=ALPHA, in1=sub(bank("out", u, w), 2),
                                                  op0=ALU.mult, op1=ALU.add), "out", u, w)
                    for t in range(TU):
                        ins = dve.bn_stats(stats[:, t, w, :], X[:, t0 + t, WCOLS * w:WCOLS * (w + 1)])
                link(ins)

            def norm(kind, u):
                t0 = TU * UNITS[u][1]
                if kind == 1:
                    for t in range(TU):
                        for c in range(4):
                            ins = dve.bn_stats(stats[:, t, c, :], X[:, t0 + t, 512 * c:512 * c + 512])
                    link(ins)
                for t in range(TU):
                    ins = dve.bn_aggr(mv[:, t, :], stats[:, t, 0:4 if kind else NOUT, :])
                link(ins, stats_made)
                dve.wait_ge(rstd_made, norm_index(kind, u) + 1)
                for t in range(TU):
                    a = X[:, t0 + t, :]
                    ins = dve.tensor_scalar(a, a, mv[:, t, 0:1], rstd[:, t, 1:2], ALU.subtract, ALU.mult)
                link(ins)
                for c in range(4):
                    a = X[:, t0:t0 + TU, 512 * c:512 * c + 512]
                    for name, op in (("norm_g", ALU.mult), ("norm_b", ALU.add)):
                        experts_full(dve, name, kind, u, c)
                        b = PLAN[(name, kind, u, c)] % BANKS
                        read(dve.tensor_tensor(a, a, banks[:, b:b + 1, :].to_broadcast([P, TU, 512]), op), name, kind, u, c)

            def queries(u):
                l = UNITS[u][0]
                for t in range(TU):
                    experts_read(dve, "score", u, t, 0)
                    experts_read(dve, "score", u, t, 1)
                    G8 = range(2 * PH)
                    for b in G8:
                        ins = dve.max(tv[:, b, 0:8], s_sb[:, b, :])
                    link(ins)
                    for b in G8:
                        dve.max_index(ti[:, b, 0:8], tv[:, b, 0:8], s_sb[:, b, :])
                        ins = dve.match_replace(s_wk[:, b, :], tv[:, b, 0:8], s_sb[:, b, :], -3.0e38)
                    link(ins)
                    for b in G8:
                        ins = dve.max(tv[:, b, 8:16], s_wk[:, b, :])
                    link(ins)
                    for b in G8:
                        ins = dve.max_index(ti[:, b, 8:16], tv[:, b, 8:16], s_wk[:, b, :])
                    link(ins)
                    link(dve.tensor_copy(tif[:, :, :], ti[:, :, :]))
                    tvh = tv[:, :, :].rearrange("p (h s) k -> p h s k", s=2)
                    tih = tif[:, :, :].rearrange("p (h s) k -> p h s k", s=2)
                    c4 = [P, PH, HALF_TOPK, HALF_TOPK]
                    link(dve.tensor_tensor(cand, tvh[:, :, 0, :, None].to_broadcast(c4), tvh[:, :, 1, None, :].to_broadcast(c4), ALU.add))
                    flat = XT[:, 0:1024].rearrange("p (h c) -> p h c", h=PH)
                    for h in range(PH):
                        ins = dve.max(cv[:, h, :], flat[:, h, :])
                    link(ins)
                    for h in range(PH):
                        ins = dve.max_index(ci[:, h, :], cv[:, h, :], flat[:, h, :])
                    link(ins)
                    link(dve.tensor_tensor(cd[:, :, :], cv[:, :, :], cv[:, :, 0:1].to_broadcast([P, PH, TOPK]), ALU.subtract), cdiff_made)
                    cif = ci[:, :, :].rearrange("p h k -> p (h k)")
                    dve.tensor_scalar(cp[:, 0, :], cif, 4, None, ALU.logical_shift_right)
                    link(dve.tensor_scalar(cp[:, 1, :], cif, 15, None, ALU.bitwise_and))
                    link(dve.tensor_copy(cpf[:, :, :], cp[:, :, :]))
                    h3 = [P, SLOTS, HALF_TOPK]
                    for s in range(2):
                        o = hot[s].rearrange("p h k i -> p (h k) i")
                        ins = dve.tensor_tensor(o, cpf[:, s, :, None].to_broadcast(h3), iota16[:, None, :].to_broadcast(h3), ALU.is_equal)
                    link(ins)
                    for s in range(2):
                        ins = dve.tensor_tensor(hot[s], hot[s], tih[:, :, s, None, :].to_broadcast([P, PH, TOPK, HALF_TOPK]), ALU.mult)
                    link(ins)
                    for s in range(2):
                        ins = dve.tensor_reduce(i12[:, s, :], hot[s].rearrange("p h k i -> p (h k) i"), AX_X, ALU.add)
                    link(ins)
                    link(dve.scalar_tensor_tensor(out=i12[:, 0, :], in0=i12[:, 0, :], scalar=float(NK), in1=i12[:, 1, :],
                                                  op0=ALU.mult, op1=ALU.add))
                    link(dve.tensor_scalar(idx[:, u % 2, t, :], i12[:, 0, :], float(l * NE), None, ALU.add))
                    dve.wait_ge(cexp_made, TU * u + t + 1)
                    link(dve.tensor_reduce(csum[:, 0, :], cd[:, :, :], AX_X, ALU.add))
                    link(dve.reciprocal(csum[:, 1, :], csum[:, 0, :]))
                    link(dve.tensor_tensor(gate[:, u % 2, t, :].rearrange("p (h k) -> p h k", h=PH), cd[:, :, :],
                                           csum[:, 1, :, None].to_broadcast([P, PH, TOPK]), ALU.mult), routed)

            def expert_dot(u, k):
                n = u * TU * SLOTS + k
                dve.wait_ge(u_landed[n % RING], 16 * (n // RING + 1))
                if k % GROUP == 0 and n // GROUP >= 2:
                    dve.wait_ge(gelu_made, n // GROUP - 1)
                a = UR[:, n % RING, :]
                gi = (n // GROUP) % 2
                dve.tensor_tensor_reduce(a, a, X[:, TU * UNITS[u][1] + k // SLOTS, :], 1.0, 0.0, ALU.mult, ALU.add,
                                         hdot[:, gi, k % GROUP:k % GROUP + 1]).then_inc(dot_made, 1)

            def expert_coef(u, kk):
                n = u * TU * SLOTS // GROUP + kk
                dve.wait_ge(gelu_made, n + 1)
                diags = sum(m < GROUP * (n - 1) for m in DIAG_SLOTS)
                if diags:
                    dve.wait_ge(diag_made, diags)
                t, s = kk * GROUP // SLOTS, kk * GROUP % SLOTS
                link(dve.tensor_tensor(coef[:, n % 2, :], gel[:, n % 2, :], gate[:, u % 2, t, s:s + GROUP], ALU.mult), coef_made)

            def expert_value(u, k):
                n, i = u * SLOT_COUNT + k, k % GROUP
                if i >= ON_DVE[u]:
                    return
                dve.wait_ge(v_landed[n % RING], 16 * (n // RING + 1))
                a, c = VR[:, n % RING, :], coef[:, (n // GROUP) % 2, i:i + 1]
                if i == 0:
                    link(dve.tensor_scalar(a, a, c, None, ALU.mult), v_scaled)
                else:
                    m = n - 1
                    dve.scalar_tensor_tensor(out=a, in0=a, scalar=c, in1=VR[:, m % RING, :], op0=ALU.mult, op1=ALU.add
                                             ).then_inc(v_freed[m % RING], 1)
                    dve.wait_ge(v_freed[m % RING], m // RING + 1)

            def expert_sum(u, t):
                n = TU * u + t
                m = SLOTS * (n + 1) - 1
                dve.wait_ge(v_freed[m % RING], m // RING + 1)
                dve.wait_ge(dot_made, SLOTS * (n + 1))
                a = X[:, TU * UNITS[u][1] + t, :]
                dve.scalar_tensor_tensor(out=a, in0=a, scalar=ALPHA, in1=acc[:, :, :].rearrange("p c n -> p (c n)"),
                                         op0=ALU.mult, op1=ALU.add).then_inc(acc_read, 1)
                dve.wait_ge(acc_read, n + 1)

            dve.wait_ge(consts_made, 1)
            dve.wait_ge(small_landed, 16 * 13)
            dve.wait_ge(x_landed, 16)

            def mix(u):
                l, f = UNITS[u]
                if u >= HALVES:
                    norm(1, u - HALVES)
                project(u)
                (deltanet if l % 2 == 0 else stick_breaking)(u)
                memory_attention(u)
                out_projection(u)
                norm(0, u)
                queries(u)

            def expert_step(u, k):
                if k % GROUP == 0 and k:
                    expert_coef(u, k // GROUP - 1)
                if k < SLOT_COUNT:
                    expert_dot(u, k)
                if k >= GROUP:
                    expert_value(u, k - GROUP)
                if k >= GROUP and (k - GROUP) % SLOTS == SLOTS - 1:
                    expert_sum(u, (k - GROUP) // SLOTS)

            experts = Experts(expert_step)
            for u in range(len(UNITS)):
                mix(u)
                if u:
                    experts.rest(u - 1)
            norm(1, len(UNITS) - 2)
            experts.rest(len(UNITS) - 1)
            norm(1, len(UNITS) - 1)


_INS = ['x', 'mem', 'gdn_w_in', 'gdn_conv', 'gdn_a_log', 'gdn_dt_bias', 'gdn_onorm', 'sb_w_in', 'mem_w_kv', 'w_out',
        'ln_mix_g', 'ln_mix_b', 'peer_w_q', 'peer_keys', 'peer_u', 'peer_v', 'ln_ffn_g', 'ln_ffn_b']


def kernel(**inputs):
    import numpy as _np
    import concourse.bacc as _bacc
    from concourse import mybir as _mybir
    from concourse.bass_utils import run_bass_kernel_spmd as _run

    nc = _bacc.Bacc("TRN2", target_bir_lowering=False, num_devices=1)
    arrays, args = {}, []
    for name in _INS:
        a = _np.ascontiguousarray(inputs[name])
        arrays[f"in_{name}"] = a
        args.append(nc.dram_tensor(f"in_{name}", a.shape, _mybir.dt.from_np(a.dtype), kind="ExternalInput").ap())
    shape = inputs['x'].shape
    args.append(nc.dram_tensor("out_0", shape, _mybir.dt.float32, kind="ExternalOutput").ap())
    build(nc, *args)
    r = _run(nc, [arrays], core_ids=[0])
    return r.results[0]["out_0"]
```

```python
from contextlib import ExitStack

import concourse.bass as bass
from concourse import mybir

F32 = mybir.dt.float32
U32 = mybir.dt.uint32
ALU = mybir.AluOpType
ACT = mybir.ActivationFunctionType
AX_X = mybir.AxisListType.X

P = 128
CHUNK = 64
SUB = 4
WCOLS = 256
RING = 3
DIAGS = 3
GROUP = 8
HALF_TOPK = 16
TOPK = 8
LN_EPS = 1e-5
RMS_EPS = 1e-6
FLT_MAX = 3.4e38
BANKS = 4
AHEAD = 3
LEVELS = (2, 4, 8, 16, 32)


def build(nc, x, mem, gdn_w_in, gdn_conv, gdn_a_log, gdn_dt_bias, gdn_onorm, sb_w_in, mem_w_kv, w_out,
          ln_mix_g, ln_mix_b, peer_w_q, peer_keys, peer_u, peer_v, ln_ffn_g, ln_ffn_b, out):
    _, S, D = x.shape
    DEPTH = w_out.shape[0]
    NMEM = mem.shape[1]
    KT = D // P
    NT = S // P
    TU = 2
    T = TU * P
    HALVES = NT // TU
    H = gdn_a_log.shape[1]
    HQ = H // 2
    MH = mem_w_kv.shape[2] // (2 * P)
    PH = peer_w_q.shape[2] // (2 * P)
    NK = peer_keys.shape[2]
    NE = peer_u.shape[1]
    SLOTS = PH * TOPK
    KO = w_out.shape[1] // P
    ALPHA = (2.0 * DEPTH) ** 0.25
    SCALE = float(P) ** -0.5
    assert (S, D, DEPTH, NMEM, T, H, MH, PH, NK) == (512, 2048, 2, 256, 256, 8, 4, 4, 128)
    UNITS = [(l, f) for l in range(DEPTH) for f in range(HALVES)]
    NPROJ = 14
    NOUT = D // WCOLS
    NQRY = 2 * PH * P // WCOLS
    NKV = 2 * MH * P // WCOLS
    QM0 = 2 * HQ * P + 2 * H * P + 2 * H

    NORM_AFTER_ROUTING = [u > 0 and u + 1 < len(UNITS) and UNITS[u + 1][1] == 0 for u in range(len(UNITS))]
    NORM_BESIDE_QUERIES = [u > 0 and u + 1 < len(UNITS) and not NORM_AFTER_ROUTING[u] for u in range(len(UNITS))]
    CHUNKS_AFTER_QUERY = ((), (0,), (1,), (2, 3))
    PLAN, LOADS, USER, COSTS, FIRST, LAST = {}, {}, {}, [], [], []

    SHARE = {
        "ktok": 0.7, "vtok": 0.7, "bcb": 0.7, "bcg": 0.7, "seg": 0.7, "kq": 0.7, "kk": 0.7, "T0": 0.7, "w": 0.7, "u": 0.7,
        "P": 2.8, "TPU": 2.8, "ws": 0.85, "o": 0.85, "ds": 0.85, "oss": 0.85,
        "z": 1.68, "later": 1.68, "sbo": 1.68, "ms": 1.67, "mpT": 1.67, "mo": 1.67,
        "norm_g": 1.44, "norm_b": 1.44, "xT": 0.71, "qry": 1.7,
    }

    def plan(*name, cost=1.0):
        PLAN[name] = len(PLAN)
        COSTS.append(cost * SHARE.get(name[0], 1.0))

    def load(*name, user=None):
        LOADS[name] = len(LOADS)
        USER[LOADS[name]] = user or name

    def plan_norm(kind, u, then=None, tile=()):
        for c in range(4 + 1):
            if c < 4:
                plan("norm_g", kind, u, c, *tile)
                plan("norm_b", kind, u, c, *tile)
            if then and c >= 1:
                plan("xT", *then, 2 * c - 2)
                plan("xT", *then, 2 * c - 1)

    def plan_memory(l):
        load("mem", l, user=("memT", l, 7))
        for j in range(8):
            plan("memT", l, j)
        for w in range(NKV):
            load("kv", l, w)
            plan("kv", l, w, cost=14.0)

    def plan_scan(u, j, i):
        if j < 0:
            return
        if i < 4 * TU:
            for name in (("ws",) if i % 2 == 0 else ("o", "ds")):
                plan(name, u, j, i // 2, cost=0.7)
        elif i == 4 * TU:
            plan("oss", u, j, cost=1.7)

    def plan_memory_attention(u, beside):
        plan("ms", u, 0)
        plan("ms", u, 1)
        beside(0)
        plan("mpT", u, 0)
        beside(1)
        for m in range(MH):
            if m + 2 < MH:
                plan("ms", u, m + 2)
            if m + 1 < MH:
                plan("mpT", u, m + 1)
            beside(2 * m + 2)
            plan("mo", u, m)
            if m + 1 < MH:
                beside(2 * m + 3)

    def plan_turn(u):
        for j in range(8):
            plan("xT", u, 0, j)

    plan_memory(0)
    plan("keys", 0)
    plan_turn(0)
    for u, (l, f) in enumerate(UNITS):
        FIRST.append(len(PLAN))
        if l % 2 == 0:
            plan("ba", u)
        for w in range(NPROJ):
            load("proj", u, w)
            plan("proj", u, w, cost=14.0)
            if l % 2 == 0:
                if 4 <= w < 8:
                    plan("l2", u, w - 4, cost=1.0)
                if w == 8:
                    plan("gcum", u)
                if w == 10:
                    plan("rows", u)
        if l % 2 == 0:
            for j in range(HQ):
                plan("ktok", u, j)
                plan("vtok", u, j)
                plan_scan(u, j - 1, 0)
                plan("bcb", u, j, cost=1.3)
                plan("bcg", u, j, cost=1.3)
                plan_scan(u, j - 1, 1)
                plan("seg", u, j, cost=1.3)
                plan_scan(u, j - 1, 2)
                plan("kq", u, j, cost=0.8)
                plan("kk", u, j, cost=1.3)
                plan_scan(u, j - 1, 3)
                plan("T0", u, j)
                plan_scan(u, j - 1, 4)
                for i in range(len(LEVELS)):
                    for h in range(2):
                        plan("P", u, j, i, h, cost=0.8)
                    plan_scan(u, j - 1, 5 + i)
                    for h in range(2):
                        plan("TPU", u, j, i, h, cost=0.8)
                plan("w", u, j)
                plan("u", u, j)
            plan_memory_attention(u, lambda i: plan_scan(u, HQ - 1, i))
        else:
            for h in range(AHEAD):
                for b in range(f + 1):
                    plan("z", u, h, b, cost=1.0)
            for b in range(f + 1):
                plan("later", u, 0, b, cost=2.0)
            for h in range(H):
                if h + 1 < H:
                    for b in range(f + 1):
                        plan("later", u, h + 1, b, cost=2.0)
                plan("sbo", u, h, cost=1.5 + f)
                if h + AHEAD < H:
                    for b in range(f + 1):
                        plan("z", u, h + AHEAD, b, cost=1.0)
            plan_memory_attention(u, lambda i: None)
        for w in range(NOUT):
            load("out", u, w)
            plan("out", u, w, cost=10.5)
        plan_norm(0, u, then=(u, 1))
        LAST.append(len(PLAN))
        for w in range(NQRY):
            load("qry", u, w)
            plan("qry", u, w, cost=14.0)
            if NORM_BESIDE_QUERIES[u]:
                for c in CHUNKS_AFTER_QUERY[w]:
                    plan("norm_g", 1, u - 1, c)
                    plan("norm_b", 1, u - 1, c)
        if not NORM_BESIDE_QUERIES[u]:
            LAST[u] = len(PLAN)
        for t in range(TU):
            plan("score", u, t, 0)
            plan("score", u, t, 1)
        if u + 1 < len(UNITS):
            if UNITS[u + 1][1] == 0:
                plan_memory(UNITS[u + 1][0])
            if NORM_AFTER_ROUTING[u]:
                plan_norm(1, u - 1, then=(u + 1, 0))
            else:
                plan_turn(u + 1)
    plan_norm(1, len(UNITS) - 2)
    for t in range(TU):
        plan_norm(1, len(UNITS) - 1, tile=(t,))

    ON_DVE = [8, 8, 8, 0]
    SLOT_COUNT = TU * SLOTS
    DIAG_SLOTS = [n for n in range(len(UNITS) * SLOT_COUNT) if n % GROUP >= ON_DVE[n // SLOT_COUNT]]
    LAG = 1
    STEPS = 2 * (SLOT_COUNT + GROUP + LAG + 1)
    STEPS_AT = {}
    ROUTING_TIME = (0, 23, 0, 23)
    for u in range(1, len(UNITS)):
        whole, so_far = sum(COSTS[FIRST[u]:LAST[u]]) - ROUTING_TIME[u], -ROUTING_TIME[u]
        for n in range(FIRST[u], LAST[u]):
            STEPS_AT[n] = (u - 1, int(STEPS * max(0.0, so_far / whole)))
            so_far += COSTS[n]
        STEPS_AT[LAST[u]] = (u - 1, STEPS)

    NORM_AT = [2 * (12 + 6 * c) for c in range(4)]
    TILE_NORM_AT = [2 * (GROUP + SLOTS + LAG + 1 + i) for i in (2, 4, 8, 12, 16)]

    class Experts:

        def __init__(self, step):
            self.step, self.at = step, {}

        def until(self, u, k):
            for i in range(self.at.get(u, 0), k):
                self.step(u, i)
            self.at[u] = max(k, self.at.get(u, 0))

        def before(self, *name):
            if PLAN[name] in STEPS_AT:
                self.until(*STEPS_AT[PLAN[name]])

        def rest(self, u):
            self.until(u, STEPS)

    def full(eng, *name, experts=None):
        if experts:
            experts.before(*name)
        eng.wait_ge(group_done, PLAN[name] + 1)

    def was_read(eng, *name, experts=None):
        if experts:
            experts.before(*name)
        n = PLAN[name]
        eng.wait_ge(bank_read[n % BANKS], n // BANKS + 1)

    with ExitStack() as ctx:
        def sb(name, shape, dt=F32):
            return ctx.enter_context(nc.sbuf_tensor(name, shape, dt))

        def sem(name):
            return ctx.enter_context(nc.semaphore(name))

        acc = ctx.enter_context(nc.psum_tensor("acc", [P, 4, 512], F32))
        banks = ctx.enter_context(nc.psum_tensor("banks", [P, BANKS, 512], F32))

        X = sb("X", [P, NT, D])
        XT = sb("XT", [P, KT * T])
        W = sb("W", [P, 2, KT * WCOLS])
        UR = sb("UR", [P, RING, D])
        VR = sb("VR", [P, RING, D])
        NV = sb("NV", [64, 256])
        MIX = sb("MIX", [P, KO * T])
        KM = sb("KM", [P, MH, NMEM])
        VM = sb("VM", [P, NMEM // P, MH * P])
        R = sb("R", [P, 11264])
        xT = XT[:, :].rearrange("p (k t) -> p k t", k=KT)
        mixT = MIX[:, :].rearrange("p (k t) -> p k t", k=KO)
        qryT = MIX[:, 0:2 * PH * T].rearrange("p (k t) -> p k t", k=2 * PH)
        qT = R[:, 0:2048].rearrange("p (h t) -> p h t", t=T)
        qmT = R[:, 2048:3072].rearrange("p (h t) -> p h t", t=T)
        vT = R[:, 3072:5120].rearrange("p (h t) -> p h t", t=T)
        zT = R[:, 5120:7168].rearrange("p (h t) -> p h t", t=T)
        convin = R[:, 7168:7168 + 1040].rearrange("p (r b t) -> p r b t", r=2, b=2)
        convout = R[:, 8208:8208 + 1024].rearrange("p (r b t) -> p r b t", r=2, b=2)
        sbkT = R[:, 3072:7168].rearrange("p (h t) -> p h t", t=S)
        sbv = R[:, 7168:11264].rearrange("p (t f) -> p t f", t=NT)

        def half_bank(region, i):
            return region[:, 512 * i:512 * i + 512]

        kbT, Kp, Vp, Lm = (half_bank(XT, i) for i in range(4))
        seg_g, decay = (half_bank(MIX, i) for i in (4, 5))
        Pm, MT = seg_g, decay
        levels = (Lm, kbT)
        TT = R[:, 7168:8192].rearrange("p (h w t c) -> p h w t c", h=2, w=2, t=TU)
        qgT = [half_bank(XT, i) for i in (4, 5)]
        Kd = [half_bank(XT, i) for i in (6, 7)]
        aqkT = [R[:, 8192 + 512 * i:8704 + 512 * i] for i in (0, 1)]
        bgT = R[0:16, 9216:9216 + T]
        vnew = R[:, 9472:9728].rearrange("p (h v) -> p h v", h=2)
        wT = R[:, 9728:10240]
        u_sb, o_sq = (W[:, 0, KO * WCOLS + 512 * i:KO * WCOLS + 512 * i + 512] for i in (0, 1))
        state = R[:, 10240:11264].rearrange("p (h v) -> p h v", h=H)
        sq = [half_bank(MIX, i) for i in range(4)]
        rs = [half_bank(MIX, 4 + i) for i in range(2)]
        hist = sb("hist", [P, 16, 3])
        convw = sb("convw", [P, 16, 4])
        wba = sb("wba", [P, KT, 16])
        onorm = sb("onorm", [P, 1])
        dtb = sb("dtb", [P, H])
        nexp = sb("nexp", [P, H])
        gx = sb("gx", [P, TU, 16])
        ge = sb("ge", [P, TU, 16])
        ga = sb("ga", [P, TU, H])
        gl = sb("gl", [P, TU, H])
        g = sb("g", [P, TU, H])
        eg = sb("eg", [P, TU, 32])
        bg = sb("bg", [P, TU, 16])
        bexpg = sb("bexpg", [P, TU, H])
        ident = sb("ident", [P, P])
        ones = sb("ones", [P, P])
        tri_le = sb("tri_le", [P, P])
        tri_gt = sb("tri_gt", [P, P])
        full_ge = sb("full_ge", [P, P])
        lvl = sb("lvl", [P, 6, P])
        before = lvl[:, 0, :]
        bound = lvl[:, 1, :]
        iota16 = sb("iota16", [P, 16])
        eps = sb("eps", [P, 2])
        stats = [sb("stats0", [P, TU, NOUT, 6]), sb("stats1", [P, TU, 4, 6])]
        mv = sb("mv", [P, TU, 2])
        rstd = sb("rstd", [P, TU, 2])
        keysT = sb("keysT", [P, 2 * DEPTH, NK])
        nmax = sb("nmax", [P, 2, TU])
        msum = sb("msum", [P, 2, TU])
        sb_space = [XT[:, 1024 * i:1024 * i + 1024] for i in range(4)] + [W[:, i, KO * WCOLS:KT * WCOLS] for i in range(2)]
        sb_z = [a.rearrange("p (s t) -> p s t", t=T) for a in sb_space[0::2]]
        sb_sp = [a.rearrange("p (s t) -> p s t", t=T) for a in sb_space[1::2]]
        mem_p = [half_bank(XT, i).rearrange("p (t m) -> p t m", t=TU) for i in (0, 1)]
        mem_pT = [half_bank(XT, i).rearrange("p (m t) -> p m t", m=2) for i in (2, 3)]
        s_sb = [R[:, 1024 * t:1024 * t + 1024].rearrange("p (g n) -> p g n", g=8) for t in range(TU)]
        s_wk = R[:, 2048:3072].rearrange("p (g n) -> p g n", g=8)
        hot = [R[:, 2048 + 512 * i:2560 + 512 * i].rearrange("p (h k i) -> p h k i", h=PH, k=TOPK) for i in range(2)]
        sums = MIX[:, 2048:3072]
        cand = sums.rearrange("p (h i j) -> p h i j", h=PH, i=16)
        tv = MIX[:, 0:128].rearrange("p (g k) -> p g k", g=2 * PH)
        ti = MIX[:, 128:256].bitcast(U32).rearrange("p (g k) -> p g k", g=2 * PH)
        tif = MIX[:, 256:384].rearrange("p (g k) -> p g k", g=2 * PH)
        cv = MIX[:, 384:416].rearrange("p (h k) -> p h k", h=PH)
        ci = MIX[:, 416:448].bitcast(U32).rearrange("p (h k) -> p h k", h=PH)
        cp = MIX[:, 448:512].bitcast(U32).rearrange("p (s k) -> p s k", s=2)
        cpf = MIX[:, 512:576].rearrange("p (s k) -> p s k", s=2)
        i12 = MIX[:, 576:640].rearrange("p (s k) -> p s k", s=2)
        cd = [MIX[:, 640 + 32 * t:672 + 32 * t].rearrange("p (h k) -> p h k", h=PH) for t in range(TU)]
        csum = MIX[:, 704:712].rearrange("p (s h) -> p s h", s=2)
        gate = sb("gate", [P, 2, TU, SLOTS])
        idx = sb("idx", [P, 2, TU, SLOTS], U32)
        hdot = sb("hdot", [P, 2, GROUP])
        gel = sb("gel", [P, 2, GROUP])
        coef = sb("coef", [P, 2, GROUP])
        diag = sb("diag", [P, DIAGS, P])

        group_done = sem("group_done")
        bank_read = [sem(f"bank_read{b}") for b in range(BANKS)]
        w_landed = [sem(f"w_landed{b}") for b in range(2)]
        x_landed = sem("x_landed")
        small_landed = sem("small_landed")
        ident_made = sem("ident_made")
        consts_made = sem("consts_made")
        pool_step = sem("pool_step")
        sbmask_made = sem("sbmask_made")
        dve_step = sem("dve_step")
        act_step = sem("act_step")
        conv_made = sem("conv_made")
        qkv_made = sem("qkv_made")
        gate_in = sem("gate_in")
        gate_exp = sem("gate_exp")
        g_made = sem("g_made")
        rows_made = sem("rows_made")
        squared = sem("squared")
        inverse_norm = sem("inverse_norm")
        qk_normed = sem("qk_normed")
        seg_made = sem("seg_made")
        kv_scaled = sem("kv_scaled")
        level_made = sem("level_made")
        inverse_made = sem("inverse_made")
        o_gated = sem("o_gated")
        softplus_ln = sem("softplus_ln")
        softplus_made = sem("softplus_made")
        att_in = sem("att_in")
        att_exp = sem("att_exp")
        mmax_made = sem("mmax_made")
        mexp_made = sem("mexp_made")
        mprob_made = sem("mprob_made")
        stats_made = sem("stats_made")
        rstd_made = sem("rstd_made")
        cdiff_made = sem("cdiff_made")
        cexp_made = sem("cexp_made")
        routed = sem("routed")
        u_landed = [sem(f"u_landed{r}") for r in range(RING)]
        v_landed = [sem(f"v_landed{r}") for r in range(RING)]
        dot_made = sem("dot_made")
        gelu_made = sem("gelu_made")
        coef_made = sem("coef_made")
        diag_made = sem("diag_made")
        v_freed = [sem(f"v_freed{r}") for r in range(RING)]
        v_scaled = sem("v_scaled")
        acc_read = sem("acc_read")
        stored = sem("stored")

        xr = x.rearrange("a (t p) d -> p (a t) d", p=P)
        outr = out.rearrange("a (t p) d -> p (a t) d", p=P)
        u_rows = peer_u.rearrange("l e d -> (l e) d")
        v_rows = peer_v.rearrange("l e d -> (l e) d")

        norms = []
        for u in range(len(UNITS)):
            norms += [(0, u)] + ([(1, u - 1)] if u else [])
        norms += [(1, len(UNITS) - 1, t) for t in range(TU)]

        def norm_index(*name):
            return norms.index(name)

        def bank(*name):
            return banks[:, PLAN[name] % BANKS, :]

        def sub(ap, n=SUB):
            return ap.rearrange("p (s c) -> p s c", s=n)

        block = ctx.enter_context(nc.Block())

        @block.sync
        def _(sp):
            def weights(*name):
                m = LOADS[name]
                if m >= 2:
                    full(sp, *USER[m - 2])
                dst = W[:, m % 2, :]
                what, a = name[0], name[1]
                if what == "mem":
                    src = mem.rearrange("a (t p) d -> p (a t) d", p=P)
                    dst = dst.rearrange("p (t d) -> p t d", t=NMEM // P)
                else:
                    if what == "kv":
                        src = mem_w_kv[a, :, WCOLS * name[2]:WCOLS * (name[2] + 1)]
                    elif what == "proj":
                        c = WCOLS * name[2]
                        if UNITS[a][0] == 0:
                            c += 16 if name[2] >= 12 else 0
                            src = gdn_w_in[0, :, c:c + WCOLS]
                        else:
                            src = sb_w_in[0, :, c:c + WCOLS]
                    elif what == "out":
                        src = w_out[UNITS[a][0], :, WCOLS * name[2]:WCOLS * (name[2] + 1)]
                        dst = W[:, m % 2, 0:KO * WCOLS]
                    else:
                        src = peer_w_q[UNITS[a][0], :, WCOLS * name[2]:WCOLS * (name[2] + 1)]
                    src = src.rearrange("(k p) c -> p k c", p=P)
                    dst = dst.rearrange("p (k c) -> p k c", c=WCOLS)
                sp.dma_start(dst, src).then_inc(w_landed[m % 2], 16)

            def parameters():
                with nc.allow_non_contiguous_dma(reason="small parameters, once"):
                    for i, v in enumerate((ln_mix_g, ln_mix_b, ln_ffn_g, ln_ffn_b)):
                        sp.dma_start(NV[16 * i:16 * i + 16, :], v.rearrange("l (a c) -> (l a) c", c=256)).then_inc(small_landed, 16)
                    sp.dma_start(UR[:, 0, 0:2 * DEPTH * P].rearrange("p (a c) -> p a c", c=P),
                                 peer_keys.rearrange("l h n c -> n (l h) c")).then_inc(small_landed, 16)
                    for i in range(4):
                        sp.dma_start(convw[:, :, i], gdn_conv[0, i, :].rearrange("(b p) -> p b", p=P)).then_inc(small_landed, 16)
                    sp.dma_start(wba[:, :, :], gdn_w_in[0, :, QM0 - 16:QM0].rearrange("(k p) c -> p k c", p=P)).then_inc(small_landed, 16)
                    sp.dma_start(onorm[:, :], gdn_onorm.rearrange("a p -> p a")).then_inc(small_landed, 16)
                    sp.dma_start(dtb[:, :], gdn_dt_bias.to_broadcast([P, H])).then_inc(small_landed, 16)
                    sp.dma_start(nexp[:, :], gdn_a_log.to_broadcast([P, H])).then_inc(small_landed, 16)

            for name in LOADS:
                weights(*name)
                if LOADS[name] == 1:
                    parameters()
                    sp.dma_start(X[:, :, :], xr).then_inc(x_landed, 16)
            was_read(sp, "norm_b", 1, len(UNITS) - 2, 3)
            sp.dma_start(outr[:, 0:NT - TU, :], X[:, 0:NT - TU, :]).then_inc(stored, 16)
            for t in range(TU):
                was_read(sp, "norm_b", 1, len(UNITS) - 1, 3, t)
                sp.dma_start(outr[:, NT - TU + t, :], X[:, NT - TU + t, :]).then_inc(stored, 16)
            sp.wait_ge(stored, 16 * (1 + TU))

        @block.gpsimd
        def _(pool):
            steps = [0]

            def link(ins):
                steps[0] += 1
                ins.then_inc(pool_step, 1)
                pool.wait_ge(pool_step, steps[0])

            link(pool.memset(ident[:, :], 0.0))
            pool.affine_select(out=ident[:, :], in_=ident[:, :], compare_op=ALU.not_equal, fill=1.0, base=0, pattern=[[-1, P]],
                               channel_multiplier=1).then_inc(ident_made, 1)
            for m in (tri_le, tri_gt, full_ge, lvl):
                link(pool.memset(m[:], 0.0 if m is lvl else 1.0))
            link(pool.memset(ones[:, :], 1.0))
            link(pool.memset(eps[:, 0:1], LN_EPS))
            link(pool.memset(eps[:, 1:2], RMS_EPS))

            def keep(ap, pattern, base, mult, op=ALU.is_ge, fill=0.0):
                link(pool.affine_select(out=ap, in_=ap, compare_op=op, fill=fill, base=base, pattern=pattern,
                                        channel_multiplier=mult))

            keep(tri_le[:, :], [[1, P]], 0, -1)
            keep(tri_le[:, CHUNK:P], [[0, CHUNK]], -CHUNK, 1)
            keep(tri_gt[:, :], [[-1, P]], 0, 1, ALU.is_gt)
            keep(tri_gt[:, 0:CHUNK], [[0, CHUNK]], CHUNK - 1, -1)
            keep(full_ge[:, :], [[-1, P]], 0, 1)
            for i, w in enumerate((1,) + LEVELS):
                v = lvl[:, i, :].rearrange("p (b h w) -> p b h w", h=2, w=w)[:, :, 1, :]
                link(pool.memset(v, 1.0))
                keep(v, [[-2 * w, P // (2 * w)], [0, w]], 0, 1)
                keep(v, [[2 * w, P // (2 * w)], [0, w]], w - 1, -1)
            link(pool.iota(iota16[:, :], [[1, 16]], base=0, channel_multiplier=0, allow_small_or_imprecise_dtypes=True))
            pool.memset(state[:, :, :], 0.0).then_inc(consts_made, 1)

            def gather(ring, rows, landed, u, k):
                n = u * SLOT_COUNT + k
                if n >= RING:
                    if ring is UR:
                        pool.wait_ge(dot_made, n - RING + 1)
                    else:
                        pool.wait_ge(v_freed[n % RING], n // RING)
                t, s = k // SLOTS, k % SLOTS
                pool.indirect_dma_start(ring[:, n % RING, :], None, rows,
                                        bass.IndirectOffsetOnAxis(idx[:, u % 2, t, s:s + 1], 0)
                                        ).then_inc(landed[n % RING], 16)

            for u in range(len(UNITS)):
                for k in range(SLOT_COUNT + GROUP):
                    if k < SLOT_COUNT:
                        if k % SLOTS == 0:
                            pool.wait_ge(routed, TU * u + k // SLOTS + 1)
                            if k == 0 and u == HALVES - 1:
                                link(pool.memset(before, 1.0))
                                link(pool.memset(bound, FLT_MAX))
                                link(pool.affine_select(out=before, in_=before, compare_op=ALU.is_gt, fill=0.0, base=0,
                                                        pattern=[[1, P]], channel_multiplier=-1))
                                pool.affine_select(out=bound, in_=bound, compare_op=ALU.is_gt, fill=-FLT_MAX, base=0,
                                                   pattern=[[1, P]], channel_multiplier=-1).then_inc(sbmask_made, 1)
                        if u == 0 and k == 0:
                            was_read(pool, "keys", 0)
                        gather(UR, u_rows, u_landed, u, k)
                    if k >= GROUP:
                        gather(VR, v_rows, v_landed, u, k - GROUP)

        @block.tensor
        def _(pe):
            order = [0]

            def group(*name):
                n = PLAN[name]
                assert n == order[0], (name, n, order[0])
                order[0] += 1
                experts.before(*name)
                if n >= BANKS:
                    pe.wait_ge(bank_read[n % BANKS], n // BANKS)
                return banks[:, n % BANKS, :]

            def done(ins):
                ins.then_inc(group_done, 1)

            def weights(*name):
                m = LOADS[name]
                pe.wait_ge(w_landed[m % 2], 16 * (m // 2 + 1))
                return W[:, m % 2, :].rearrange("p (k c) -> p k c", c=WCOLS)

            def by_feature(ps, w, src, kt):
                for b in range(2):
                    for k in range(kt):
                        last = pe.matmul(sub(ps, 2)[:, b, :], w[:, k, b * P:b * P + P], src[:, k, :],
                                         start=(k == 0), stop=(k == kt - 1))
                done(last)

            def by_token(ps, w, src, kt):
                for t in range(TU):
                    for k in range(kt):
                        last = pe.matmul(sub(ps, 2)[:, t, :], src[:, k, t * P:t * P + P], w[:, k, :],
                                         start=(k == 0), stop=(k == kt - 1))
                done(last)

            def norm(kind, u, then):
                for c in range(4 + 1):
                    if c < 4:
                        norm_vectors(kind, u, c)
                    if c >= 1:
                        was_read(pe, "norm_b", kind, u, c - 1)
                        x_transposes(*then, 2 * c - 2)
                        x_transposes(*then, 2 * c - 1)
                x_turned(*then)

            def x_transposes(u, which, j):
                ps = sub(group("xT", u, which, j))
                for i in range(SUB):
                    k = SUB * (j // 2) + i
                    last = pe.transpose(ps[:, i, :], X[:, TU * UNITS[u][1] + j % 2, k * P:k * P + P], ident[:, :])
                done(last)

            def x_turned(u, which):
                for j in range(4, 8):
                    was_read(pe, "xT", u, which, j)

            def project(u):
                l = UNITS[u][0]
                if l % 2 == 0:
                    ps = group("ba", u)
                    for t in range(TU):
                        for k in range(KT):
                            last = pe.matmul(ps[:, 16 * t:16 * t + 16], xT[:, k, t * P:t * P + P], wba[:, k, :],
                                             start=(k == 0), stop=(k == KT - 1))
                    done(last)
                for w in range(NPROJ):
                    ps = group("proj", u, w)
                    tokens = l % 2 == 1 and 8 <= w < 12
                    (by_token if tokens else by_feature)(ps, weights("proj", u, w), xT, KT)
                    if l % 2 == 0:
                        beside_projection(u, w)

            def memory_kv(l):
                m = LOADS[("mem", l)]
                pe.wait_ge(w_landed[m % 2], 16 * (m // 2 + 1))
                rows = W[:, m % 2, :].rearrange("p (t d) -> p t d", t=2)
                for j in range(8):
                    ps = sub(group("memT", l, j))
                    for i in range(SUB):
                        last = pe.transpose(ps[:, i, :], rows[:, j // 4, ((j % 4) * SUB + i) * P:((j % 4) * SUB + i + 1) * P],
                                            ident[:, :])
                    done(last)
                for j in range(4, 8):
                    was_read(pe, "memT", l, j)
                for w in range(NKV):
                    ps = group("kv", l, w)
                    (by_feature if w < NKV // 2 else by_token)(ps, weights("kv", l, w), xT, KT)

            def beside_projection(u, w):
                f = UNITS[u][1]
                if 4 <= w < 8:
                    pe.wait_ge(squared, 4 * f + w - 3)
                    done(pe.matmul(group("l2", u, w - 4), ones[:, :], sq[w - 4], start=True, stop=True))
                if w == 8:
                    pe.wait_ge(g_made, u + 1)
                    ps = group("gcum", u)
                    for t in range(TU):
                        chunks = [tri_le[:, c:c + 1].to_broadcast([P, P]) for c in (CHUNK - 1, P - 1)]
                        for i, a in enumerate([tri_le[:, :], tri_gt[:, :]] + chunks):
                            last = pe.matmul(ps[:, 32 * t + 8 * i:32 * t + 8 * i + 8], a, g[:, t, :], start=True, stop=True)
                    done(last)
                if w == 10:
                    pe.wait_ge(rows_made, u + 1)
                    ps = group("rows", u)
                    for t in range(TU):
                        last = pe.transpose(ps[0:16, t * P:t * P + P], bg[:, t, :], ident[:, :])
                    done(last)

            def deltanet(u):
                for j in range(HQ):
                    delta_heads(u, j)

            def delta_heads(u, j):
                f = UNITS[u][1]
                gj = HQ * f + j
                if j == 0:
                    pe.wait_ge(qk_normed, 4 * f + 4)
                    pe.wait_ge(qkv_made, 8 * f + 8)
                    was_read(pe, "rows", u)
                ps = sub(group("ktok", u, j))
                for t in range(TU):
                    last = pe.transpose(ps[:, t, :], qT[:, HQ + j, t * P:t * P + P], ident[:, :])
                done(last)
                ps = sub(group("vtok", u, j))
                for i in range(SUB):
                    last = pe.transpose(ps[:, i, :], vT[:, 2 * j + i // 2, (i % 2) * P:(i % 2) * P + P], ident[:, :])
                done(last)
                scan(u, j - 1, 0)
                for s, base in (("bcb", 0), ("bcg", H)):
                    ps = sub(group(s, u, j), 2)
                    for h in range(2):
                        r = base + 2 * j + h
                        last = pe.matmul(ps[:, h, :], ident[0:16, r:r + 1].to_broadcast([16, P]), bgT, start=True, stop=True)
                    done(last)
                scan(u, j - 1, 1)
                pe.wait_ge(seg_made, gj + 1)
                ps = sub(group("seg", u, j))
                for i in range(SUB):
                    last = pe.matmul(ps[:, i, :], sub(seg_g)[:, i, :], tri_le[:, :], start=True, stop=True)
                done(last)
                scan(u, j - 1, 2)
                ps = sub(group("kq", u, j))
                for t in range(TU):
                    last = pe.matmul(ps[:, t, :], qT[:, HQ + j, t * P:t * P + P], qT[:, j, t * P:t * P + P],
                                     start=True, stop=True)
                done(last)
                ps = sub(group("kk", u, j))
                was_read(pe, "bcb", u, j)
                for i in range(SUB):
                    t = i % 2
                    last = pe.matmul(ps[:, i, :], qT[:, HQ + j, t * P:t * P + P], sub(kbT)[:, i, :], start=True, stop=True)
                done(last)
                scan(u, j - 1, 3)
                ps = sub(group("T0", u, j))
                pe.wait_ge(inverse_made, gj + 1)
                for i in range(SUB):
                    last = pe.transpose(ps[:, i, :], TT[:, i // 2, 1, i % 2, :], ident[:, :])
                done(last)
                scan(u, j - 1, 4)
                for n in range(len(LEVELS)):
                    L = levels[(n + 1) % 2]
                    for h in range(2):
                        ps = sub(group("P", u, j, n, h))
                        if h == 0:
                            pe.wait_ge(level_made, len(LEVELS) * gj + n + 1)
                        if n:
                            was_read(pe, "TPU", u, j, n - 1, h)
                        elif h == 0:
                            was_read(pe, "T0", u, j)
                        for t in range(TU):
                            last = pe.matmul(ps[:, t, :], sub(L)[:, 2 * h + t, :], TT[:, h, 0, t, :], start=True, stop=True)
                        done(last)
                    scan(u, j - 1, 5 + n)
                    for h in range(2):
                        ps = sub(group("TPU", u, j, n, h))
                        was_read(pe, "P", u, j, n, h)
                        for t in range(TU):
                            pe.matmul(ps[:, t, :], TT[:, h, 1, t, :], sub(Pm)[:, 2 * h + t, :], start=True, stop=True)
                        for t in range(TU):
                            last = pe.matmul(ps[:, TU + t, :], sub(Pm)[:, 2 * h + t, :], TT[:, h, 1, t, :], start=True, stop=True)
                        done(last)
                ps = sub(group("w", u, j))
                for h in range(2):
                    was_read(pe, "TPU", u, j, len(LEVELS) - 1, h)
                pe.wait_ge(kv_scaled, gj + 1)
                was_read(pe, "vtok", u, j)
                for i in range(SUB):
                    last = pe.matmul(ps[:, i, :], sub(Kp)[:, i, :], TT[:, i // 2, 1, i % 2, :], start=True, stop=True)
                done(last)
                ps = sub(group("u", u, j))
                for i in range(SUB):
                    last = pe.matmul(ps[:, i, :], TT[:, i // 2, 1, i % 2, :], sub(Vp)[:, i, :], start=True, stop=True)
                done(last)

            def scan(u, j, i):
                if j < 0 or i > 4 * TU:
                    return
                if i == 4 * TU:
                    ps = group("oss", u, j)
                    was_read(pe, "o", u, j, 2 * TU - 1)
                    done(pe.matmul(ps, ones[:, :], o_sq, start=True, stop=True))
                    return
                c = i // 2
                t, lo = c // 2, CHUNK * (c % 2)
                cols = slice(t * P + lo, t * P + lo + CHUNK)
                if i % 2 == 0:
                    ps = sub(group("ws", u, j, c))
                    if c:
                        was_read(pe, "ds", u, j, c - 1)
                    else:
                        for name in ("w", "ktok", "bcg", "kq"):
                            was_read(pe, name, u, j)
                    for h in range(2):
                        last = pe.matmul(ps[lo:lo + CHUNK, h, :], sub(wT)[:, 2 * h + t, lo:lo + CHUNK],
                                         state[:, 2 * j + h, :], start=True, stop=True)
                    done(last)
                    return
                ps = group("o", u, j, c)
                was_read(pe, "ws", u, j, c)
                for h in range(2):
                    o = ps[:, CHUNK * h:CHUNK * h + CHUNK]
                    pe.matmul(o, state[:, 2 * j + h, :], sub(qgT[j % 2], 2)[:, h, cols], start=True, stop=False)
                    last = pe.matmul(o, vnew[lo:lo + CHUNK, h, :], sub(aqkT[j % 2])[lo:lo + CHUNK, 2 * h + t, lo:lo + CHUNK],
                                     start=False, stop=True)
                done(last)
                ps = sub(group("ds", u, j, c))
                for h in range(2):
                    last = pe.matmul(ps[:, h, :], sub(Kd[j % 2])[lo:lo + CHUNK, 2 * h + t, :], vnew[lo:lo + CHUNK, h, :],
                                     start=True, stop=True)
                done(last)

            def stick_breaking(u):
                f = UNITS[u][1]
                nb = f + 1

                def scores(h):
                    for b in range(nb):
                        ps = sub(group("z", u, h, b), 2)
                        if h == 0 and b == 0:
                            for w in range(10, 14):
                                was_read(pe, "proj", u, w)
                        for i in range(2):
                            s = (2 * b + i) * P
                            last = pe.matmul(ps[:, i, :], sbkT[:, h, s:s + P], qT[:, h, :], start=True, stop=True)
                        done(last)

                def later(h):
                    pe.wait_ge(softplus_made, H * f + h + 1)
                    for b in range(nb):
                        ps = sub(group("later", u, h, b), 2)
                        for i in range(2):
                            for s in range(2 * b + i, 2 * nb):
                                a = full_ge if s == 2 * b + i else ones
                                lo = P if s == 2 * nb - 1 and s > 2 * b + i else 0
                                last = pe.matmul(ps[:, i, lo:T], a[:, :], sb_sp[h % AHEAD][:, s, lo:T],
                                                 start=(s == 2 * b + i), stop=(s == 2 * nb - 1))
                        done(last)

                for h in range(AHEAD):
                    scores(h)
                later(0)
                for h in range(H):
                    if h + 1 < H:
                        later(h + 1)
                    pe.wait_ge(att_exp, H * f + h + 1)
                    ps = group("sbo", u, h)
                    for s in range(2 * nb):
                        lo = P if s == 2 * nb - 1 else 0
                        last = pe.matmul(ps[:, lo:T], sbv[:, s, h * P:h * P + P], sb_z[h % AHEAD][:, s, lo:T],
                                         start=(s == 0), stop=(s == 2 * nb - 1))
                    done(last)
                    if h + AHEAD < H:
                        scores(h + AHEAD)

            def memory_attention(u):
                def beside(i):
                    if UNITS[u][0] % 2 == 0:
                        scan(u, HQ - 1, i)

                def scores(m):
                    ps = sub(group("ms", u, m), 2)
                    for t in range(TU):
                        last = pe.matmul(ps[:, t, :], qmT[:, m, t * P:t * P + P], KM[:, m, :], start=True, stop=True)
                    done(last)

                def turn(m):
                    ps = sub(group("mpT", u, m))
                    pe.wait_ge(mprob_made, MH * u + m + 1)
                    for mm in range(2):
                        for t in range(TU):
                            last = pe.transpose(ps[:, 2 * mm + t, :], mem_p[m % 2][:, t, mm * P:mm * P + P], ident[:, :])
                    done(last)

                scores(0)
                scores(1)
                beside(0)
                turn(0)
                beside(1)
                for m in range(MH):
                    if m + 2 < MH:
                        scores(m + 2)
                    if m + 1 < MH:
                        turn(m + 1)
                    beside(2 * m + 2)
                    ps = group("mo", u, m)
                    was_read(pe, "mpT", u, m)
                    for mm in range(2):
                        last = pe.matmul(ps[:, 0:T], VM[:, mm, m * P:m * P + P], mem_pT[m % 2][:, mm, :], start=(mm == 0), stop=(mm == 1))
                    done(last)
                    if m + 1 < MH:
                        beside(2 * m + 3)

            def out_projection(u):
                for w in range(NOUT):
                    ps = group("out", u, w)
                    if w == 0:
                        was_read(pe, "mo", u, MH - 1)
                        f = UNITS[u][1]
                        if UNITS[u][0] % 2 == 0:
                            pe.wait_ge(o_gated, HQ * (f + 1))
                        else:
                            was_read(pe, "sbo", u, H - 1)
                    by_token(ps, weights("out", u, w), mixT, KO)

            def norm_vectors(kind, u, c, *tile):
                for v, name in enumerate(("norm_g", "norm_b")):
                    ps = group(name, kind, u, c, *tile)
                    for i in range(2):
                        r = 8 * (4 * kind + 2 * v + UNITS[u][0]) + 2 * c + i
                        last = pe.matmul(ps[:, 256 * i:256 * i + 256], ident[0:64, r:r + 1].to_broadcast([64, P]),
                                         NV[:, :], start=True, stop=True)
                    done(last)

            def queries(u):
                for w in range(NQRY):
                    by_feature(group("qry", u, w), weights("qry", u, w), xT, KT)
                    if NORM_BESIDE_QUERIES[u]:
                        for c in CHUNKS_AFTER_QUERY[w]:
                            norm_vectors(1, u - 1, c)
                for t in range(TU):
                    for i in range(2):
                        ps = sub(group("score", u, t, i))
                        if t == 0 and i == 0:
                            for w in range(NQRY):
                                was_read(pe, "qry", u, w)
                        for k in range(SUB):
                            b = SUB * i + k
                            last = pe.matmul(ps[:, k, :], qryT[:, b, t * P:t * P + P], keysT[:, 2 * UNITS[u][0] + b % 2, :],
                                             start=True, stop=True)
                        done(last)

            def expert_slot(u, k):
                n, i, D_ = u * SLOT_COUNT + k, k % GROUP, ON_DVE[u]
                if i < D_ - 1:
                    return
                if i == D_ - 1:
                    pe.wait_ge(v_freed[(n - 1) % RING], (n - 1) // RING + 1)
                    a = ident[:, :]
                else:
                    d = DIAG_SLOTS.index(n)
                    pe.wait_ge(diag_made, d + 1)
                    pe.wait_ge(v_landed[n % RING], 16 * (n // RING + 1))
                    a = diag[:, d % DIAGS, :]
                first = k % SLOTS == max(D_ - 1, 0)
                if first and n >= SLOTS:
                    pe.wait_ge(acc_read, n // SLOTS)
                for c in range(4):
                    last = pe.matmul(acc[:, c, :], a, VR[:, n % RING, 512 * c:512 * c + 512],
                                     start=first, stop=(k % SLOTS == SLOTS - 1))
                last.then_inc(v_freed[n % RING], 1)

            def expert_step(u, i):
                k, second = divmod(i, 2)
                if not second and 0 <= k - GROUP - LAG < SLOT_COUNT:
                    expert_slot(u, k - GROUP - LAG)

            experts = Experts(expert_step)
            pe.wait_ge(ident_made, 1)
            memory_kv(0)
            pe.wait_ge(consts_made, 1)
            pe.wait_ge(small_landed, 16 * 13)
            ps = sub(group("keys", 0))
            for i in range(2 * DEPTH):
                last = pe.transpose(ps[:, i, :], UR[:, 0, i * P:i * P + P], ident[:, :])
            done(last)

            def turn(u):
                for j in range(8):
                    x_transposes(u, 0, j)
                x_turned(u, 0)

            pe.wait_ge(x_landed, 16)
            turn(0)
            for u, (l, f) in enumerate(UNITS):
                project(u)
                (deltanet if l % 2 == 0 else stick_breaking)(u)
                memory_attention(u)
                out_projection(u)
                norm(0, u, then=(u, 1))
                queries(u)
                if u + 1 < len(UNITS):
                    if UNITS[u + 1][1] == 0:
                        memory_kv(UNITS[u + 1][0])
                    if NORM_AFTER_ROUTING[u]:
                        norm(1, u - 1, then=(u + 1, 0))
                    else:
                        turn(u + 1)
            for c in range(4):
                experts.until(len(UNITS) - 1, NORM_AT[c])
                norm_vectors(1, len(UNITS) - 2, c)
            for c in range(4):
                experts.until(len(UNITS) - 1, TILE_NORM_AT[c + 1])
                norm_vectors(1, len(UNITS) - 1, c, 0)
            experts.rest(len(UNITS) - 1)
            for c in range(4):
                norm_vectors(1, len(UNITS) - 1, c, 1)

        @block.scalar
        def _(act):
            counts = {}

            def experts_full(eng, *name):
                full(eng, *name, experts=experts)

            def experts_read(eng, *name):
                was_read(eng, *name, experts=experts)

            def link(ins, s=None):
                s = act_step if s is None else s
                counts[s.name] = counts.get(s.name, 0) + 1
                ins.then_inc(s, 1)
                act.wait_ge(s, counts[s.name])

            def read(ins, *name):
                ins.then_inc(bank_read[PLAN[name] % BANKS], 1)

            def copy_out(dst, *name, cols=512, func=ACT.Copy, scale=1.0, shape=None, rows=P):
                experts_full(act, *name)
                src = bank(*name)[0:rows, 0:cols]
                if shape:
                    src = sub(src, shape)
                read(act.activation(dst, src, func, scale=scale), *name)

            def x_copies(u, which):
                for j in range(8):
                    k, t = SUB * (j // 2), j % 2
                    copy_out(xT[:, k:k + SUB, t * P:t * P + P], "xT", u, which, j, shape=SUB)

            def memory_kv(l, beside=None):
                for j in range(8):
                    k, t = SUB * (j % 4), j // 4
                    copy_out(xT[:, k:k + SUB, t * P:t * P + P], "memT", l, j, shape=SUB)
                for w in range(NKV):
                    if beside is not None and w in (1, 2):
                        routing_exp(beside, w - 1)
                    if w < NKV // 2:
                        copy_out(KM[:, 2 * w:2 * w + 2, :], "kv", l, w, shape=2)
                    else:
                        c = WCOLS * (w - NKV // 2)
                        copy_out(VM[:, :, c:c + WCOLS], "kv", l, w, shape=2)

            def project(u):
                l, f = UNITS[u]
                if u:
                    act.wait_ge(routed, TU * u)
                if l % 2 == 1:
                    for w in range(NPROJ):
                        if w < 4:
                            copy_out(qT[:, 2 * w:2 * w + 2, :], "proj", u, w, scale=SCALE, shape=2)
                        elif w < 8:
                            copy_out(sbkT[:, 2 * w - 8:2 * w - 6, f * T:f * T + T], "proj", u, w, shape=2)
                        elif w < 12:
                            c = WCOLS * (w - 8)
                            copy_out(sbv[:, TU * f:TU * f + TU, c:c + WCOLS], "proj", u, w, shape=2)
                        else:
                            copy_out(qmT[:, 2 * w - 24:2 * w - 22, :], "proj", u, w, shape=2)
                    return

                def silu(w):
                    act.wait_ge(conv_made, 8 * f + w + 1)
                    dst = qT[:, 2 * w:2 * w + 2, :] if w < 4 else vT[:, 2 * w - 8:2 * w - 6, :]
                    act.activation(dst, convout[:, w % 2, :, :], ACT.Silu).then_inc(qkv_made, 1)

                for w in range(NPROJ):
                    if 5 <= w < 9:
                        inverse(u, w - 5)
                    if w == 9:
                        experts_full(act, "gcum", u)
                        read(act.activation(eg[:, :, :], sub(bank("gcum", u)[:, 0:64], 2), ACT.Exp), "gcum", u)
                    if w == 11:
                        copy_out(bgT, "rows", u, cols=T, rows=16)
                    if w < 8:
                        if w >= 2:
                            act.wait_ge(conv_made, 8 * f + w - 1)
                        copy_out(convin[:, w % 2, :, 3:3 + T], "proj", u, w, shape=2)
                        if w == 1:
                            gates(u)
                    elif w < 12:
                        copy_out(zT[:, 2 * w - 16:2 * w - 14, :], "proj", u, w, func=ACT.Silu, shape=2)
                    else:
                        copy_out(qmT[:, 2 * w - 24:2 * w - 22, :], "proj", u, w, shape=2)
                    if 1 <= w < 9:
                        silu(w - 1)
                        if w < 5:
                            act.wait_ge(qkv_made, 8 * f + w)
                            act.activation(sq[w - 1], R[:, 512 * w - 512:512 * w], ACT.Square).then_inc(squared, 1)

            def gates(u):
                experts.before("ba", u)
                act.wait_ge(gate_in, u + 1)
                link(act.activation(ge[:, :, :], gx[:, :, :], ACT.Exp))
                act.activation(gl[:, :, :], ge[:, :, 0:H], ACT.Ln, bias=1.0).then_inc(gate_exp, 1)

            def deltanet(u):
                for j in range(HQ):
                    delta_heads(u, j)

            def inverse(u, i):
                f = UNITS[u][1]
                experts_full(act, "l2", u, i)
                if i >= 2:
                    act.wait_ge(qk_normed, 4 * f + i - 1)
                ins = act.activation(rs[i % 2], bank("l2", u, i), ACT.Ln, bias=eps[:, 1:2])
                read(ins, "l2", u, i)
                experts_read(act, "l2", u, i)
                act.activation(rs[i % 2], rs[i % 2], ACT.Exp, scale=-0.5).then_inc(inverse_norm, 1)

            def delta_heads(u, j):
                f = UNITS[u][1]
                if j == 0:
                    act.wait_ge(qk_normed, 4 * f + 4)
                for i in range(SUB):
                    h, t = 2 * j + i // 2, i % 2
                    ins = act.activation(sub(seg_g)[:, i, :], tri_gt[:, :], ACT.Copy, scale=g[:, t, h:h + 1])
                ins.then_inc(seg_made, 1)
                experts_full(act, "vtok", u, j)
                for i in range(SUB):
                    h, t = 2 * j + i // 2, i % 2
                    ins = act.activation(sub(Vp)[:, i, :], sub(bank("vtok", u, j))[:, i, :], ACT.Copy, scale=bg[:, t, h:h + 1])
                read(ins, "vtok", u, j)
                scan(u, j - 1, 1)
                experts_full(act, "seg", u, j)
                read(act.activation(decay, bank("seg", u, j), ACT.Exp), "seg", u, j)
                scan(u, j - 1, 3)
                experts_full(act, "T0", u, j)
                read(act.activation(TT[:, :, 0, :, :], bank("T0", u, j).rearrange("p (h t c) -> p h t c", h=2, t=TU), ACT.Copy),
                     "T0", u, j)
                for n in range(len(LEVELS)):
                    for h in range(2):
                        copy_out(Pm[:, 2 * P * h:2 * P * h + 2 * P], "P", u, j, n, h, cols=2 * P)
                    scan(u, j - 1, 5 + n)
                copy_out(wT, "w", u, j)
                copy_out(u_sb, "u", u, j)

            def scan(u, j, i):
                f = UNITS[u][1]
                if j < 0 or i > 4 * TU:
                    return
                if i == 4 * TU:
                    experts_full(act, "oss", u, j)
                    read(act.activation(o_sq, bank("oss", u, j), ACT.Ln, scale=1.0 / P, bias=eps[:, 1:2]), "oss", u, j)
                    experts_read(act, "oss", u, j)
                    act.activation(o_sq, o_sq, ACT.Exp, scale=-0.5).then_inc(inverse_norm, 1)
                elif i % 2 == 1:
                    c = i // 2
                    experts_full(act, "o", u, j, c)
                    if c == 0 and j:
                        act.wait_ge(o_gated, HQ * f + j)
                    ps = sub(bank("o", u, j, c)[:, 0:2 * CHUNK], 2)
                    cols = slice(CHUNK * c, CHUNK * c + CHUNK)
                    act.activation(sub(o_sq, 2)[:, :, cols], ps, ACT.Square)
                    read(act.activation(mixT[:, 2 * j:2 * j + 2, cols], ps, ACT.Copy), "o", u, j, c)

            def stick_breaking(u):
                f = UNITS[u][1]
                nb = f + 1

                def scores(h):
                    for b in range(nb):
                        experts_full(act, "z", u, h, b)
                        ins = act.activation(sb_sp[h % AHEAD][:, 2 * b:2 * b + 2, :], sub(bank("z", u, h, b), 2), ACT.Abs)
                        if b == nb - 1:
                            link(ins)
                        copy_out(sb_z[h % AHEAD][:, 2 * b:2 * b + 2, :], "z", u, h, b, shape=2)
                    e = sb_sp[h % AHEAD][:, 0:2 * nb, :]
                    link(act.activation(e, e, ACT.Exp, scale=-1.0))
                    act.activation(e, e, ACT.Ln, bias=1.0).then_inc(softplus_ln, 1)

                def attention(h):
                    experts.before("later", u, h, nb - 1)
                    act.wait_ge(att_in, H * f + h + 1)
                    a = sb_z[h % AHEAD][:, 0:2 * nb, :]
                    act.activation(a, a, ACT.Exp).then_inc(att_exp, 1)

                for h in range(AHEAD):
                    scores(h)
                attention(0)
                for h in range(H):
                    if h + 1 < H:
                        attention(h + 1)
                    copy_out(mixT[:, h, :], "sbo", u, h, cols=T)
                    if h + AHEAD < H:
                        scores(h + AHEAD)

            def memory_attention(u):
                def exponentials(m):
                    experts_full(act, "ms", u, m)
                    act.wait_ge(mmax_made, MH * u + m + 1)
                    ps = sub(bank("ms", u, m), 2)
                    for t in range(TU):
                        ins = act.activation(mem_p[m % 2][:, t, :], ps[:, t, :], ACT.Exp, scale=SCALE, bias=nmax[:, m % 2, t:t + 1],
                                             accum_out=msum[:, m % 2, t:t + 1])
                        if t == 0:
                            link(ins)
                    read(ins, "ms", u, m)

                def turned(m):
                    copy_out(mem_pT[m % 2][:, :, :], "mpT", u, m, shape=2)

                def beside(i):
                    if UNITS[u][0] % 2 == 0:
                        scan(u, HQ - 1, i)

                exponentials(0)
                exponentials(1)
                beside(0)
                turned(0)
                beside(1)
                for m in range(MH):
                    if m + 2 < MH:
                        exponentials(m + 2)
                    if m + 1 < MH:
                        turned(m + 1)
                    beside(2 * m + 2)
                    copy_out(mixT[:, H + m, :], "mo", u, m, cols=T)
                    if m + 1 < MH:
                        beside(2 * m + 3)

            def norm(kind, u, *tile):
                if kind == 0:
                    experts.before("out", u, NOUT - 1)
                act.wait_ge(stats_made, norm_index(kind, u, *tile) + 1)
                link(act.activation(rstd[:, :, 0], mv[:, :, 1], ACT.Ln, bias=eps[:, 0:1]))
                act.activation(rstd[:, :, 1], rstd[:, :, 0], ACT.Exp, scale=-0.5).then_inc(rstd_made, 1)

            def queries(u):
                for w in range(NQRY):
                    copy_out(qryT[:, 2 * w:2 * w + 2, :], "qry", u, w, shape=2)
                for t in range(TU):
                    for i in range(2):
                        copy_out(s_sb[t][:, SUB * i:SUB * i + SUB, :], "score", u, t, i, shape=SUB)

            def routing_exp(u, t):
                act.wait_ge(cdiff_made, TU * u + t + 1)
                act.activation(cd[t], cd[t], ACT.Exp).then_inc(cexp_made, 1)

            def expert_gelu(u, kk):
                n = u * TU * SLOTS // GROUP + kk
                act.wait_ge(dot_made, GROUP * (n + 1))
                if n >= 2:
                    act.wait_ge(coef_made, n - 1)
                act.activation(gel[:, n % 2, :], hdot[:, n % 2, :], ACT.Gelu).then_inc(gelu_made, 1)

            def expert_diag(u, k):
                n = u * SLOT_COUNT + k
                if k % GROUP < ON_DVE[u]:
                    return
                d = DIAG_SLOTS.index(n)
                if k % GROUP == ON_DVE[u]:
                    act.wait_ge(coef_made, n // GROUP + 1)
                if d >= DIAGS:
                    m = DIAG_SLOTS[d - DIAGS]
                    act.wait_ge(v_freed[m % RING], m // RING + 1)
                act.activation(diag[:, d % DIAGS, :], ident[:, :], ACT.Copy,
                               scale=coef[:, (n // GROUP) % 2, k % GROUP:k % GROUP + 1]).then_inc(diag_made, 1)

            def expert_step(u, i):
                k, second = divmod(i, 2)
                if not second:
                    return
                if 0 <= k - GROUP < SLOT_COUNT:
                    expert_diag(u, k - GROUP)
                if k % GROUP == GROUP - 1 and k < SLOT_COUNT:
                    expert_gelu(u, k // GROUP)

            experts = Experts(expert_step)
            memory_kv(0)
            act.wait_ge(consts_made, 1)
            act.wait_ge(small_landed, 16 * 13)
            copy_out(keysT[:, :, :], "keys", 0, shape=4)
            link(act.activation(nexp[:, :], nexp[:, :], ACT.Exp))

            x_copies(0, 0)
            for u, (l, f) in enumerate(UNITS):
                project(u)
                (deltanet if l % 2 == 0 else stick_breaking)(u)
                memory_attention(u)
                norm(0, u)
                x_copies(u, 1)
                if NORM_BESIDE_QUERIES[u]:
                    experts.before("qry", u, 0)
                    norm(1, u - 1)
                queries(u)
                with_memory = u + 1 < len(UNITS) and UNITS[u + 1][1] == 0
                if with_memory:
                    memory_kv(UNITS[u + 1][0], beside=u)
                if NORM_AFTER_ROUTING[u]:
                    norm(1, u - 1)
                if u + 1 < len(UNITS):
                    x_copies(u + 1, 0)
                if not with_memory:
                    routing_exp(u, 0)
                    routing_exp(u, 1)
            norm(1, len(UNITS) - 2)
            experts.until(len(UNITS) - 1, TILE_NORM_AT[0])
            norm(1, len(UNITS) - 1, 0)
            experts.rest(len(UNITS) - 1)
            norm(1, len(UNITS) - 1, 1)

        @block.vector
        def _(dve):
            counts = {}

            def experts_full(eng, *name):
                full(eng, *name, experts=experts)

            def experts_read(eng, *name):
                was_read(eng, *name, experts=experts)

            def link(ins, s=None):
                s = dve_step if s is None else s
                counts[s.name] = counts.get(s.name, 0) + 1
                ins.then_inc(s, 1)
                dve.wait_ge(s, counts[s.name])

            def read(ins, *name):
                ins.then_inc(bank_read[PLAN[name] % BANKS], 1)
                experts_read(dve, *name)

            def project(u):
                l, f = UNITS[u]
                if l % 2 == 1:
                    return
                gates(u)
                for w in range(8):
                    if w == 2:
                        decays(u)
                    if 5 <= w:
                        normalise(u, w - 5)
                    r = w % 2
                    if w >= 2:
                        dve.wait_ge(qkv_made, 8 * f + w - 1)
                    if f == 0:
                        link(dve.memset(convin[:, r, :, 0:3], 0.0))
                    else:
                        link(dve.tensor_copy(convin[:, r, :, 0:3], hist[:, 2 * w:2 * w + 2, :]))
                    experts_read(dve, "proj", u, w)
                    link(dve.tensor_copy(hist[:, 2 * w:2 * w + 2, :], convin[:, r, :, T:T + 3]))
                    for i in range(4):
                        for b in range(2):
                            c, o = convw[:, 2 * w + b, i:i + 1], convout[:, r, b, :]
                            src = convin[:, r, b, i:i + T]
                            if i == 0:
                                ins = dve.tensor_scalar(o, src, c, None, ALU.mult)
                            else:
                                ins = dve.scalar_tensor_tensor(out=o, in0=src, scalar=c, in1=o, op0=ALU.mult, op1=ALU.add)
                            if i == 3 and b == 1:
                                link(ins, conv_made)
                            elif b == 1:
                                link(ins)
                normalise(u, 3)
                experts_read(dve, "gcum", u)
                link(dve.tensor_tensor(bexpg[:, :, :], bg[:, :, 0:H], eg[:, :, 0:H], ALU.mult))
                link(dve.tensor_copy(bg[:, :, H:2 * H], eg[:, :, 0:H]), rows_made)

            def gates(u):
                experts_full(dve, "ba", u)
                ps = sub(bank("ba", u)[:, 0:32], 2)
                link(dve.tensor_tensor(ga[:, :, :], ps[:, :, H:2 * H], dtb[:, None, :].to_broadcast([P, TU, H]), ALU.add))
                read(dve.tensor_scalar(gx[:, :, H:2 * H], ps[:, :, 0:H], -1.0, 80.0, ALU.mult, ALU.min), "ba", u)
                link(dve.scalar_tensor_tensor(out=gx[:, :, 0:H], in0=ga[:, :, :], scalar=-1.0, in1=ga[:, :, :],
                                              op0=ALU.mult, op1=ALU.min), gate_in)

            def decays(u):
                dve.wait_ge(gate_exp, u + 1)
                link(dve.scalar_tensor_tensor(out=gl[:, :, :], in0=ga[:, :, :], scalar=0.0, in1=gl[:, :, :],
                                              op0=ALU.max, op1=ALU.add))
                link(dve.tensor_scalar(bg[:, :, 0:H], ge[:, :, H:2 * H], 1.0, None, ALU.add))
                link(dve.reciprocal(bg[:, :, 0:H], bg[:, :, 0:H]))
                link(dve.scalar_tensor_tensor(out=g[:, :, :], in0=gl[:, :, :], scalar=-1.0,
                                              in1=nexp[:, None, :].to_broadcast([P, TU, H]), op0=ALU.mult, op1=ALU.mult), g_made)

            def normalise(u, i):
                f = UNITS[u][1]
                experts.before("l2", u, i)
                dve.wait_ge(inverse_norm, (4 + HQ) * f + i + 1)
                a = R[:, 512 * i:512 * i + 512]
                link(dve.scalar_tensor_tensor(out=a, in0=a, scalar=SCALE if i < 2 else 1.0, in1=rs[i % 2],
                                              op0=ALU.mult, op1=ALU.mult), qk_normed)

            def deltanet(u):
                for j in range(HQ):
                    delta_heads(u, j)

            def delta_heads(u, j):
                experts_full(dve, "ktok", u, j)
                ps = sub(bank("ktok", u, j))
                for i in range(SUB):
                    h, t = 2 * j + i // 2, i % 2
                    ins = dve.tensor_scalar(sub(Kp)[:, i, :], ps[:, t, :], bexpg[:, t, h:h + 1], None, ALU.mult)
                ins.then_inc(kv_scaled, 1)
                for i in range(SUB):
                    h, t = 2 * j + i // 2, i % 2
                    ins = dve.tensor_scalar(sub(Kd[j % 2])[:, i, :], ps[:, t, :], eg[:, t, H + h:H + h + 1], None, ALU.mult)
                read(ins, "ktok", u, j)
                scan(u, j - 1, 0)
                experts_full(dve, "bcb", u, j)
                k2 = qT[:, HQ + j:HQ + j + 1, :].to_broadcast([P, 2, T])
                q2 = qT[:, j:j + 1, :].to_broadcast([P, 2, T])
                read(dve.tensor_tensor(sub(kbT, 2), k2, sub(bank("bcb", u, j), 2), ALU.mult), "bcb", u, j)
                experts_full(dve, "bcg", u, j)
                read(dve.tensor_tensor(sub(qgT[j % 2], 2), q2, sub(bank("bcg", u, j), 2), ALU.mult), "bcg", u, j)
                scan(u, j - 1, 1)
                experts_read(dve, "seg", u, j)
                four = [P, SUB, P]
                link(dve.tensor_tensor(sub(decay), sub(decay), tri_le[:, None, :].to_broadcast(four), ALU.mult))
                scan(u, j - 1, 2)
                experts_full(dve, "kq", u, j)
                for h in range(2):
                    ins = dve.tensor_tensor(sub(aqkT[j % 2])[:, 2 * h:2 * h + 2, :], sub(bank("kq", u, j))[:, 0:2, :],
                                            sub(decay)[:, 2 * h:2 * h + 2, :], ALU.mult)
                read(ins, "kq", u, j)
                experts_full(dve, "kk", u, j)
                read(dve.tensor_tensor(MT, bank("kk", u, j), decay, ALU.mult), "kk", u, j)
                link(dve.tensor_tensor(sub(Lm), sub(MT), lvl[:, 0:1, :].to_broadcast(four), ALU.mult))
                quarters = [P, 2, TU, P]
                link(dve.tensor_tensor(TT[:, :, 1, :, :], ident[:, None, None, :].to_broadcast(quarters),
                                       Lm.rearrange("p (h t c) -> p h t c", h=2, t=TU), ALU.subtract), inverse_made)

                def level(n):
                    if n < len(LEVELS):
                        link(dve.tensor_tensor(sub(levels[(n + 1) % 2]), sub(MT), lvl[:, n + 1:n + 2, :].to_broadcast(four), ALU.mult), level_made)

                level(0)
                level(1)
                scan(u, j - 1, 3)
                scan(u, j - 1, 4)
                for n in range(len(LEVELS)):
                    scan(u, j - 1, 5 + n)
                    for h in range(2):
                        experts_full(dve, "TPU", u, j, n, h)
                        a = R[:, 7168 + 512 * h:7680 + 512 * h]
                        read(dve.tensor_tensor(a, a, bank("TPU", u, j, n, h), ALU.subtract), "TPU", u, j, n, h)
                    level(n + 2)

            def scan(u, j, i):
                if j < 0 or i > 4 * TU:
                    return
                f = UNITS[u][1]
                if i == 4 * TU:
                    experts.before("oss", u, j)
                    dve.wait_ge(inverse_norm, (4 + HQ) * f + 4 + j + 1)
                    o = MIX[:, 2 * j * T:(2 * j + 2) * T]
                    link(dve.scalar_tensor_tensor(out=o, in0=o, scalar=onorm[:, 0:1], in1=o_sq, op0=ALU.mult, op1=ALU.mult))
                    link(dve.tensor_tensor(o, o, R[:, 5120 + 2 * j * T:5120 + (2 * j + 2) * T], ALU.mult), o_gated)
                    return
                c = i // 2
                t, lo = c // 2, CHUNK * (c % 2)
                if i % 2 == 0:
                    if c == 0:
                        experts_read(dve, "u", u, j)
                    experts_full(dve, "ws", u, j, c)
                    us = u_sb.rearrange("p (h t v) -> p h t v", h=2, t=TU)[lo:lo + CHUNK, :, t, :]
                    read(dve.tensor_tensor(vnew[lo:lo + CHUNK, :, :], us, sub(bank("ws", u, j, c))[lo:lo + CHUNK, 0:2, :], ALU.subtract),
                         "ws", u, j, c)
                    return
                experts_full(dve, "ds", u, j, c)
                ps = sub(bank("ds", u, j, c))
                for h in range(2):
                    s = state[:, 2 * j + h, :]
                    x0 = 16 + H * (c % 2) + 2 * j + h
                    ins = dve.scalar_tensor_tensor(out=s, in0=s, scalar=eg[:, t, x0:x0 + 1], in1=ps[:, h, :],
                                                   op0=ALU.mult, op1=ALU.add)
                read(ins, "ds", u, j, c)

            def stick_breaking(u):
                f = UNITS[u][1]
                nb = f + 1
                dve.wait_ge(sbmask_made, 1)

                def diagonal(a):
                    return a[:, 2 * nb - 2:2 * nb, :].rearrange("p s (t c) -> p (s t) c", t=TU)[:, ::TU + 1, :]

                def softplus(h):
                    z, e = (a[h % AHEAD][:, 0:2 * nb, :] for a in (sb_z, sb_sp))
                    for b in range(nb):
                        experts_read(dve, "z", u, h, b)
                    dve.wait_ge(softplus_ln, H * f + h + 1)
                    link(dve.scalar_tensor_tensor(out=e, in0=z, scalar=0.0, in1=e, op0=ALU.max, op1=ALU.add))
                    m = diagonal(sb_sp[h % AHEAD])
                    link(dve.tensor_tensor(m, m, before[:, None, :].to_broadcast([P, 2, P]), ALU.mult), softplus_made)

                def subtract_later(h):
                    for b in range(nb):
                        experts_full(dve, "later", u, h, b)
                        a = sb_z[h % AHEAD][:, 2 * b:2 * b + 2, :]
                        read(dve.tensor_tensor(a, a, sub(bank("later", u, h, b), 2), ALU.subtract), "later", u, h, b)
                    m = diagonal(sb_z[h % AHEAD])
                    link(dve.tensor_tensor(m, m, bound[:, None, :].to_broadcast([P, 2, P]), ALU.min), att_in)

                for h in range(AHEAD):
                    softplus(h)
                subtract_later(0)
                for h in range(H):
                    if h + 1 < H:
                        subtract_later(h + 1)
                    if h + AHEAD < H:
                        softplus(h + AHEAD)

            def memory_attention(u):
                def maxima(m):
                    experts_full(dve, "ms", u, m)
                    link(dve.tensor_reduce(nmax[:, m % 2, :], sub(bank("ms", u, m), 2), AX_X, ALU.max))
                    link(dve.tensor_scalar(nmax[:, m % 2, :], nmax[:, m % 2, :], -SCALE, None, ALU.mult), mmax_made)

                def probabilities(m):
                    experts_read(dve, "ms", u, m)
                    link(dve.reciprocal(msum[:, m % 2, :], msum[:, m % 2, :]))
                    for t in range(TU):
                        ins = dve.tensor_scalar(mem_p[m % 2][:, t, :], mem_p[m % 2][:, t, :], msum[:, m % 2, t:t + 1], None, ALU.mult)
                    link(ins, mprob_made)

                def beside(i):
                    if UNITS[u][0] % 2 == 0:
                        scan(u, HQ - 1, i)

                maxima(0)
                maxima(1)
                beside(0)
                probabilities(0)
                beside(1)
                for m in range(MH):
                    if m + 2 < MH:
                        maxima(m + 2)
                    if m + 1 < MH:
                        probabilities(m + 1)
                    beside(2 * m + 2)
                    if m + 1 < MH:
                        beside(2 * m + 3)

            def out_projection(u):
                t0 = TU * UNITS[u][1]
                for w in range(NOUT):
                    experts_full(dve, "out", u, w)
                    a = X[:, t0:t0 + TU, WCOLS * w:WCOLS * (w + 1)]
                    read(dve.scalar_tensor_tensor(out=a, in0=a, scalar=ALPHA, in1=sub(bank("out", u, w), 2),
                                                  op0=ALU.mult, op1=ALU.add), "out", u, w)
                    for t in range(TU):
                        ins = dve.bn_stats(stats[0][:, t, w, :], X[:, t0 + t, WCOLS * w:WCOLS * (w + 1)])
                link(ins)

            def norm_start(kind, u, *tile):
                for t in tile or range(TU):
                    ins = dve.bn_aggr(mv[:, t, :], stats[kind][:, t, :, :])
                link(ins, stats_made)
                dve.wait_ge(rstd_made, norm_index(kind, u, *tile) + 1)

            def norm_chunk(kind, u, c, *tile):
                t0 = TU * UNITS[u][1]
                for name in ("norm_g", "norm_b"):
                    experts_full(dve, name, kind, u, c, *tile)
                    for t in tile or range(TU):
                        a = X[:, t0 + t, 512 * c:512 * c + 512]
                        if name == "norm_g":
                            ins = dve.scalar_tensor_tensor(out=a, in0=a, scalar=mv[:, t, 0:1], in1=bank(name, kind, u, c, *tile),
                                                           op0=ALU.subtract, op1=ALU.mult)
                        else:
                            ins = dve.scalar_tensor_tensor(out=a, in0=a, scalar=rstd[:, t, 1:2], in1=bank(name, kind, u, c, *tile),
                                                           op0=ALU.mult, op1=ALU.add)
                    read(ins, name, kind, u, c, *tile)

            def norm(kind, u):
                norm_start(kind, u)
                for c in range(4):
                    norm_chunk(kind, u, c)

            def queries(u):
                l = UNITS[u][0]
                experts.before("score", u, 0, 0)
                full(dve, "score", u, TU - 1, 1)
                for t in range(TU):
                    for i in range(2):
                        experts_read(dve, "score", u, t, i)
                    G8 = range(2 * PH)
                    for b in G8:
                        ins = dve.max(tv[:, b, 0:8], s_sb[t][:, b, :])
                    link(ins)
                    for b in G8:
                        dve.max_index(ti[:, b, 0:8], tv[:, b, 0:8], s_sb[t][:, b, :])
                        ins = dve.match_replace(s_wk[:, b, :], tv[:, b, 0:8], s_sb[t][:, b, :], -3.0e38)
                    link(ins)
                    for b in G8:
                        ins = dve.max(tv[:, b, 8:16], s_wk[:, b, :])
                    link(ins)
                    for b in G8:
                        ins = dve.max_index(ti[:, b, 8:16], tv[:, b, 8:16], s_wk[:, b, :])
                    link(ins)
                    link(dve.tensor_copy(tif[:, :, :], ti[:, :, :]))
                    tvh = tv[:, :, :].rearrange("p (h s) k -> p h s k", s=2)
                    tih = tif[:, :, :].rearrange("p (h s) k -> p h s k", s=2)
                    c4 = [P, PH, HALF_TOPK, HALF_TOPK]
                    link(dve.tensor_tensor(cand, tvh[:, :, 0, :, None].to_broadcast(c4), tvh[:, :, 1, None, :].to_broadcast(c4), ALU.add))
                    flat = sums.rearrange("p (h c) -> p h c", h=PH)
                    for h in range(PH):
                        ins = dve.max(cv[:, h, :], flat[:, h, :])
                    link(ins)
                    for h in range(PH):
                        ins = dve.max_index(ci[:, h, :], cv[:, h, :], flat[:, h, :])
                    link(ins)
                    link(dve.tensor_tensor(cd[t], cv[:, :, :], cv[:, :, 0:1].to_broadcast([P, PH, TOPK]), ALU.subtract), cdiff_made)
                    cif = ci[:, :, :].rearrange("p h k -> p (h k)")
                    dve.tensor_scalar(cp[:, 0, :], cif, 4, None, ALU.logical_shift_right)
                    link(dve.tensor_scalar(cp[:, 1, :], cif, 15, None, ALU.bitwise_and))
                    link(dve.tensor_copy(cpf[:, :, :], cp[:, :, :]))
                    h3 = [P, SLOTS, HALF_TOPK]
                    for s in range(2):
                        o = hot[s].rearrange("p h k i -> p (h k) i")
                        ins = dve.tensor_tensor(o, cpf[:, s, :, None].to_broadcast(h3), iota16[:, None, :].to_broadcast(h3), ALU.is_equal)
                    link(ins)
                    for s in range(2):
                        ins = dve.tensor_tensor(hot[s], hot[s], tih[:, :, s, None, :].to_broadcast([P, PH, TOPK, HALF_TOPK]), ALU.mult)
                    link(ins)
                    for s in range(2):
                        ins = dve.tensor_reduce(i12[:, s, :], hot[s].rearrange("p h k i -> p (h k) i"), AX_X, ALU.add)
                    link(ins)
                    link(dve.scalar_tensor_tensor(out=i12[:, 0, :], in0=i12[:, 0, :], scalar=float(NK), in1=i12[:, 1, :],
                                                  op0=ALU.mult, op1=ALU.add))
                    link(dve.tensor_scalar(idx[:, u % 2, t, :], i12[:, 0, :], float(l * NE), None, ALU.add))
                    dve.wait_ge(cexp_made, TU * u + t + 1)
                    link(dve.tensor_reduce(csum[:, 0, :], cd[t], AX_X, ALU.add))
                    link(dve.reciprocal(csum[:, 1, :], csum[:, 0, :]))
                    link(dve.tensor_tensor(gate[:, u % 2, t, :].rearrange("p (h k) -> p h k", h=PH), cd[t],
                                           csum[:, 1, :, None].to_broadcast([P, PH, TOPK]), ALU.mult), routed)

            def expert_dot(u, k):
                n = u * TU * SLOTS + k
                dve.wait_ge(u_landed[n % RING], 16 * (n // RING + 1))
                if k % GROUP == 0 and n // GROUP >= 2:
                    dve.wait_ge(gelu_made, n // GROUP - 1)
                a = UR[:, n % RING, :]
                gi = (n // GROUP) % 2
                dve.tensor_tensor_reduce(a, a, X[:, TU * UNITS[u][1] + k // SLOTS, :], 1.0, 0.0, ALU.mult, ALU.add,
                                         hdot[:, gi, k % GROUP:k % GROUP + 1]).then_inc(dot_made, 1)

            def expert_coef(u, kk):
                n = u * TU * SLOTS // GROUP + kk
                dve.wait_ge(gelu_made, n + 1)
                diags = sum(m < GROUP * (n - 1) for m in DIAG_SLOTS)
                if diags:
                    dve.wait_ge(diag_made, diags)
                t, s = kk * GROUP // SLOTS, kk * GROUP % SLOTS
                link(dve.tensor_tensor(coef[:, n % 2, :], gel[:, n % 2, :], gate[:, u % 2, t, s:s + GROUP], ALU.mult), coef_made)

            def expert_value(u, k):
                n, i = u * SLOT_COUNT + k, k % GROUP
                if i >= ON_DVE[u]:
                    return
                dve.wait_ge(v_landed[n % RING], 16 * (n // RING + 1))
                a, c = VR[:, n % RING, :], coef[:, (n // GROUP) % 2, i:i + 1]
                if i == 0:
                    link(dve.tensor_scalar(a, a, c, None, ALU.mult), v_scaled)
                else:
                    m = n - 1
                    dve.scalar_tensor_tensor(out=a, in0=a, scalar=c, in1=VR[:, m % RING, :], op0=ALU.mult, op1=ALU.add
                                             ).then_inc(v_freed[m % RING], 1)
                    dve.wait_ge(v_freed[m % RING], m // RING + 1)

            def expert_sum(u, t):
                n = TU * u + t
                m = SLOTS * (n + 1) - 1
                dve.wait_ge(v_freed[m % RING], m // RING + 1)
                dve.wait_ge(dot_made, SLOTS * (n + 1))
                a = X[:, TU * UNITS[u][1] + t, :]
                dve.scalar_tensor_tensor(out=a, in0=a, scalar=ALPHA, in1=acc[:, :, :].rearrange("p c n -> p (c n)"),
                                         op0=ALU.mult, op1=ALU.add).then_inc(acc_read, 1)
                dve.wait_ge(acc_read, n + 1)
                for c in range(4):
                    ins = dve.bn_stats(stats[1][:, t, c, :], a[:, 512 * c:512 * c + 512])
                link(ins)

            dve.wait_ge(consts_made, 1)
            dve.wait_ge(small_landed, 16 * 13)
            dve.wait_ge(x_landed, 16)

            def expert_step(u, i):
                k, second = divmod(i, 2)
                if second:
                    if 0 <= k - GROUP < SLOT_COUNT:
                        expert_value(u, k - GROUP)
                    return
                if k % GROUP == 0 and 0 < k <= SLOT_COUNT:
                    expert_coef(u, k // GROUP - 1)
                if k < SLOT_COUNT:
                    expert_dot(u, k)
                summed = k - GROUP - LAG
                if summed > 0 and summed % SLOTS == 0:
                    expert_sum(u, summed // SLOTS - 1)

            experts = Experts(expert_step)
            for u, (l, f) in enumerate(UNITS):
                project(u)
                (deltanet if l % 2 == 0 else stick_breaking)(u)
                memory_attention(u)
                out_projection(u)
                norm(0, u)
                if NORM_BESIDE_QUERIES[u]:
                    experts.before("qry", u, 0)
                    norm(1, u - 1)
                queries(u)
                if NORM_AFTER_ROUTING[u]:
                    norm(1, u - 1)
            last_unit = len(UNITS) - 1
            norm_start(1, last_unit - 1)
            for c in range(4):
                experts.until(last_unit, NORM_AT[c])
                norm_chunk(1, last_unit - 1, c)
            experts.until(last_unit, TILE_NORM_AT[0])
            norm_start(1, last_unit, 0)
            for c in range(4):
                experts.until(last_unit, TILE_NORM_AT[c + 1])
                norm_chunk(1, last_unit, c, 0)
            experts.rest(last_unit)
            norm_start(1, last_unit, 1)
            for c in range(4):
                norm_chunk(1, last_unit, c, 1)


_INS = ['x', 'mem', 'gdn_w_in', 'gdn_conv', 'gdn_a_log', 'gdn_dt_bias', 'gdn_onorm', 'sb_w_in', 'mem_w_kv', 'w_out',
        'ln_mix_g', 'ln_mix_b', 'peer_w_q', 'peer_keys', 'peer_u', 'peer_v', 'ln_ffn_g', 'ln_ffn_b']


def kernel(**inputs):
    import numpy as _np
    import concourse.bacc as _bacc
    from concourse import mybir as _mybir
    from concourse.bass_utils import run_bass_kernel_spmd as _run

    nc = _bacc.Bacc("TRN2", target_bir_lowering=False, num_devices=1)
    arrays, args = {}, []
    for name in _INS:
        a = _np.ascontiguousarray(inputs[name])
        arrays[f"in_{name}"] = a
        args.append(nc.dram_tensor(f"in_{name}", a.shape, _mybir.dt.from_np(a.dtype), kind="ExternalInput").ap())
    shape = inputs['x'].shape
    args.append(nc.dram_tensor("out_0", shape, _mybir.dt.float32, kind="ExternalOutput").ap())
    build(nc, *args)
    r = _run(nc, [arrays], core_ids=[0])
    return r.results[0]["out_0"]
```
